# Optimizing a Trainium2 kernel written in Bass

```python
import jax
import jax.numpy as jnp
from jax import lax
import numpy as np

D_MODEL = 1024
BATCH = 1
SEQ = 512
DEPTH = 2
DEC_BATCH = 8
DEC_SEQ = 1
PAST_LEN = 2048
PAGE_SIZE = 128

N_MIXERS = 2
N_NSA_LAYERS = (DEPTH + 1) // 2
N_GLA_LAYERS = DEPTH // 2

NSA_HEADS = 16
NSA_HEAD_DIM = D_MODEL // NSA_HEADS
NSA_KV_HEADS = 4
NSA_GROUP = NSA_HEADS // NSA_KV_HEADS
NSA_Q_COLS = NSA_HEADS * NSA_HEAD_DIM
NSA_KV_COLS = 2 * NSA_KV_HEADS * NSA_HEAD_DIM
NSA_GATE_OFF = NSA_Q_COLS + 3 * NSA_KV_COLS
NSA_PROJ = NSA_GATE_OFF + 3 * NSA_HEADS
CMP_BLK = 64
SEL_BLK = 64
N_SEL = 16
WINDOW = 512
WIN_Q_BLK = 128
SEL_Q_BLK = 32
ATTN_SCALE = NSA_HEAD_DIM ** -0.5
ROPE_THETA = 10000.0
NEG_INF = -1e30
SEL_FORCE = 1e4

GLA_HEADS = 4
GLA_DK = D_MODEL // 2
GLA_DV = D_MODEL
GLA_DK_HEAD = GLA_DK // GLA_HEADS
GLA_DV_HEAD = GLA_DV // GLA_HEADS
GLA_RANK = 16
GLA_TAU = 16.0
GLA_CHUNK = 32
GLA_SCALE = GLA_DK_HEAD ** -0.5
GLA_PROJ = 2 * GLA_DK + 2 * GLA_DV + GLA_RANK

D_FF = -(-8 * D_MODEL // (3 * 256)) * 256
DN_ALPHA = (2.0 * DEPTH) ** 0.25
DN_BETA = (8.0 * DEPTH) ** -0.25
LN_EPS = 1e-5

kernel_name = 'nsa_gla_hybrid_decode_step'

def layer_norm(x, g, b):
    xf = x.astype(jnp.float32)
    mu = jnp.mean(xf, axis=-1, keepdims=True)
    var = jnp.mean(jnp.square(xf - mu), axis=-1, keepdims=True)
    return ((xf - mu) * lax.rsqrt(var + LN_EPS) * g + b).astype(x.dtype)

def rope(x, pos):
    half = x.shape[-1] // 2
    inv = ROPE_THETA ** (-jnp.arange(half, dtype=jnp.float32) / half)
    ang = pos.astype(jnp.float32)[:, None] * inv[None, :]
    cos = jnp.cos(ang)[:, None, :]
    sin = jnp.sin(ang)[:, None, :]
    xf = x.astype(jnp.float32)
    x1, x2 = xf[..., :half], xf[..., half:]
    return jnp.concatenate([x1 * cos - x2 * sin, x2 * cos + x1 * sin], axis=-1).astype(x.dtype)

def masked_softmax(s, mask):
    s = jnp.where(mask, s.astype(jnp.float32), NEG_INF)
    p = jnp.where(mask, jnp.exp(s - jnp.max(s, axis=-1, keepdims=True)), 0.0)
    return p / jnp.maximum(jnp.sum(p, axis=-1, keepdims=True), 1e-30)

def swiglu(x, w_gu, w_down):
    gu = x @ w_gu
    return (jax.nn.silu(gu[..., :D_FF]) * gu[..., D_FF:]) @ w_down

def nsa_project(x, pos, w_in, b_gate):
    B, T, _ = x.shape
    G, R, D = NSA_KV_HEADS, NSA_GROUP, NSA_HEAD_DIM
    proj = x @ w_in
    q = proj[..., :NSA_Q_COLS].reshape(B, T, NSA_HEADS, D)

    def branch(i):
        lo = NSA_Q_COLS + i * NSA_KV_COLS
        return proj[..., lo:lo + NSA_KV_COLS].reshape(B, T, 2, G, D)

    cmp_kv = branch(0)
    slc_kv = branch(1)
    win_kv = branch(2)
    slc_kv = jnp.stack([rope(slc_kv[:, :, 0], pos), slc_kv[:, :, 1]], axis=2)
    win_kv = jnp.stack([rope(win_kv[:, :, 0], pos), win_kv[:, :, 1]], axis=2)
    gates = jax.nn.sigmoid((proj[..., NSA_GATE_OFF:] + b_gate).astype(jnp.float32)).reshape(B, T, 3, G, R)
    q_rot = rope(q, pos).reshape(B, T, G, R, D)
    return q.reshape(B, T, G, R, D), q_rot, cmp_kv, slc_kv, win_kv, gates

def compress_blocks(rows, pe, w1, w2):
    B, L = rows.shape[:2]
    nb = L // CMP_BLK
    blk = rows[:, :nb * CMP_BLK].reshape(B, nb, CMP_BLK, 2, NSA_KV_HEADS, NSA_HEAD_DIM)
    h = jax.nn.silu(jnp.einsum('bnlcgd,lcde->bncge', blk + pe[:, :, None, :], w1))
    return jnp.einsum('bncge,cef->bncgf', h, w2)

def cmp_attention(q, q_pos, ckv):
    nb = ckv.shape[1]
    s = jnp.einsum('btgrd,bngd->btgrn', q, ckv[:, :, 0]) * ATTN_SCALE
    blk_end = (jnp.arange(nb, dtype=jnp.int32) + 1) * CMP_BLK - 1
    mask = (blk_end[None, :] <= q_pos[:, None])[None, :, None, None, :]
    p = masked_softmax(s, mask)
    o = jnp.einsum('btgrn,bngd->btgrd', p.astype(ckv.dtype), ckv[:, :, 1])
    return o, jnp.sum(p, axis=3)

def select_blocks(imp, q_pos, nb_sel):
    nbc = imp.shape[-1]
    imp = jnp.pad(imp, ((0, 0), (0, 0), (0, 0), (0, nb_sel - nbc)))
    blk = jnp.arange(nb_sel, dtype=jnp.int32)[None, :]
    cur = (q_pos // SEL_BLK)[:, None]
    forced = (blk == 0) | (blk == cur) | (blk == cur - 1)
    valid = blk <= cur
    score = jnp.where(forced[None, :, None, :], SEL_FORCE,
                      jnp.where(valid[None, :, None, :], imp, -1.0))
    _, idx = lax.top_k(score, min(N_SEL, nb_sel))
    return idx, idx <= (q_pos // SEL_BLK)[None, :, None, None]

def sel_attention(q, q_pos, key_pos, sel_valid, kg, vg):
    B, T, G, R, D = q.shape
    kk = kg.reshape(B, T, G, -1, D)
    vv = vg.reshape(B, T, G, -1, D)
    s = jnp.einsum('btgrd,btgkd->btgrk', q, kk) * ATTN_SCALE
    mask = sel_valid[..., None] & (key_pos <= q_pos[None, :, None, None, None])
    p = masked_softmax(s, mask.reshape(B, T, G, 1, -1))
    return jnp.einsum('btgrk,btgkd->btgrd', p.astype(vv.dtype), vv)

def win_attention(q, q_pos, k, v, k_pos):
    s = jnp.einsum('btgrd,bkgd->btgrk', q, k) * ATTN_SCALE
    diff = q_pos[:, None] - k_pos[None, :]
    mask = ((diff >= 0) & (diff <= WINDOW) & (k_pos[None, :] >= 0))[None, :, None, None, :]
    p = masked_softmax(s, mask)
    return jnp.einsum('btgrk,bkgd->btgrd', p.astype(v.dtype), v)

def nsa_combine(o_cmp, o_slc, o_win, gates, w_out, dtype):
    B, T = o_cmp.shape[:2]
    o = (gates[:, :, 0, :, :, None] * o_cmp + gates[:, :, 1, :, :, None] * o_slc
         + gates[:, :, 2, :, :, None] * o_win)
    return o.reshape(B, T, NSA_Q_COLS).astype(dtype) @ w_out

def nsa_prompt(x, pos, w_in, b_gate, pe, w1, w2, w_out):
    q, q_rot, cmp_kv, slc_kv, win_kv, gates = nsa_project(x, pos, w_in, b_gate)
    B, T = x.shape[:2]
    G, R, D = NSA_KV_HEADS, NSA_GROUP, NSA_HEAD_DIM
    ckv = compress_blocks(cmp_kv, pe, w1, w2)
    o_cmp, imp = cmp_attention(q, pos, ckv)
    idx, valid = select_blocks(imp, pos, T // SEL_BLK)
    nq = T // SEL_Q_BLK
    b_e = jnp.arange(B)[:, None, None, None, None]
    g_e = jnp.arange(G)[None, None, :, None, None]

    def chunks(a):
        return a.reshape((B, nq, SEL_Q_BLK) + a.shape[2:]).swapaxes(0, 1)

    def sel_block(args):
        qb, pb, ib, vb = args
        key_pos = ib[..., None] * SEL_BLK + jnp.arange(SEL_BLK, dtype=jnp.int32)
        kg = slc_kv[b_e, key_pos, 0, g_e]
        vg = slc_kv[b_e, key_pos, 1, g_e]
        return sel_attention(qb, pb, key_pos, vb, kg, vg)

    o_slc = lax.map(sel_block, (chunks(q_rot), pos.reshape(nq, SEL_Q_BLK), chunks(idx), chunks(valid)))
    o_slc = o_slc.swapaxes(0, 1).reshape(B, T, G, R, D)
    win_pad = jnp.pad(win_kv, ((0, 0), (WINDOW, 0), (0, 0), (0, 0), (0, 0)))

    def win_block(j):
        start = j * WIN_Q_BLK
        qb = lax.dynamic_slice_in_dim(q_rot, start, WIN_Q_BLK, axis=1)
        kvb = lax.dynamic_slice_in_dim(win_pad, start, WINDOW + WIN_Q_BLK, axis=1)
        qp = start + jnp.arange(WIN_Q_BLK, dtype=jnp.int32)
        kp = start - WINDOW + jnp.arange(WINDOW + WIN_Q_BLK, dtype=jnp.int32)
        return win_attention(qb, qp, kvb[:, :, 0], kvb[:, :, 1], kp)

    o_win = lax.map(win_block, jnp.arange(T // WIN_Q_BLK, dtype=jnp.int32))
    o_win = o_win.swapaxes(0, 1).reshape(B, T, G, R, D)
    y = nsa_combine(o_cmp, o_slc, o_win, gates, w_out, x.dtype)
    return y, cmp_kv, slc_kv, win_kv[:, -min(WINDOW, T):]

def nsa_sample(x, pos, li, cache_cmp_kv, cache_slc_kv, cache_win_kv, page_table,
               w_in, b_gate, pe, w1, w2, w_out):
    q, q_rot, cmp_kv, slc_kv, win_kv, gates = nsa_project(x, pos, w_in, b_gate)
    B, T = x.shape[:2]
    G, D = NSA_KV_HEADS, NSA_HEAD_DIM
    past_len = page_table.shape[1] * PAGE_SIZE
    cmp_past = cache_cmp_kv[li, page_table].reshape(B, past_len, 2, G, D)
    ckv = jnp.concatenate([compress_blocks(cmp_past, pe, w1, w2),
                           compress_blocks(cmp_kv, pe, w1, w2)], axis=1)
    o_cmp, imp = cmp_attention(q, pos, ckv)
    idx, valid = select_blocks(imp, pos, -(-(past_len + T) // SEL_BLK))
    key_pos = idx[..., None] * SEL_BLK + jnp.arange(SEL_BLK, dtype=jnp.int32)
    b_e = jnp.arange(B)[:, None, None, None, None]
    g_e = jnp.arange(G)[None, None, :, None, None]
    kp = jnp.minimum(key_pos, past_len - 1)
    phys = page_table[b_e, kp // PAGE_SIZE]
    off = kp % PAGE_SIZE
    kn = jnp.clip(key_pos - past_len, 0, T - 1)
    from_past = (key_pos < past_len)[..., None]
    kg = jnp.where(from_past, cache_slc_kv[li, phys, off, 0, g_e], slc_kv[b_e, kn, 0, g_e])
    vg = jnp.where(from_past, cache_slc_kv[li, phys, off, 1, g_e], slc_kv[b_e, kn, 1, g_e])
    o_slc = sel_attention(q_rot, pos, key_pos, valid, kg, vg)
    wb = cache_win_kv.shape[2]
    buf = jnp.concatenate([cache_win_kv[li], win_kv], axis=1)
    k_pos = past_len - wb + jnp.arange(wb + T, dtype=jnp.int32)
    o_win = win_attention(q_rot, pos, buf[:, :, 0], buf[:, :, 1], k_pos)
    y = nsa_combine(o_cmp, o_slc, o_win, gates, w_out, x.dtype)
    return y, cmp_kv, slc_kv, buf[:, T:]

def gla_chunked(q, k, v, log_a, s0):
    B, T, H, DK = q.shape
    DV = v.shape[-1]
    C = GLA_CHUNK
    pad = (-T) % C

    def prep(a):
        a = jnp.pad(a.astype(jnp.float32), ((0, 0), (0, pad), (0, 0), (0, 0)))
        nc = a.shape[1] // C
        return a.reshape(B, nc, C, H, a.shape[-1]).transpose(1, 0, 3, 2, 4)

    qc, kc, vc, lac = prep(q), prep(k), prep(v), prep(log_a)
    lb = jnp.cumsum(lac, axis=3)
    lb_last = lb[:, :, :, -1:, :]
    q_i = qc * jnp.exp(lb) * GLA_SCALE
    k_i = kc * jnp.exp(-lb)
    k_s = kc * jnp.exp(lb_last - lb)
    a_last = jnp.exp(lb_last[:, :, :, 0, :])
    causal = jnp.tril(jnp.ones((C, C), dtype=bool))

    def step(S, inp):
        qi, ki, ks, vv, al = inp
        att = jnp.where(causal, jnp.einsum('bhtk,bhsk->bhts', qi, ki), 0.0)
        o = jnp.einsum('bhts,bhsv->bhtv', att, vv) + jnp.einsum('bhtk,bhkv->bhtv', qi, S)
        S = al[..., None] * S + jnp.einsum('bhsk,bhsv->bhkv', ks, vv)
        return S, o

    S, o = lax.scan(step, s0.astype(jnp.float32), (q_i, k_i, k_s, vc, a_last))
    o = o.transpose(1, 0, 3, 2, 4).reshape(B, -1, H, DV)[:, :T]
    return o, S

def gla_mixer(x, s0, w_in, w_gate2, b_gate2, norm_g, w_out):
    B, T, _ = x.shape
    H = GLA_HEADS
    proj = x @ w_in
    o1, o2, o3, o4 = GLA_DK, 2 * GLA_DK, 2 * GLA_DK + GLA_DV, 2 * GLA_DK + 2 * GLA_DV
    q = proj[..., :o1].reshape(B, T, H, GLA_DK_HEAD)
    k = proj[..., o1:o2].reshape(B, T, H, GLA_DK_HEAD)
    v = proj[..., o2:o3].reshape(B, T, H, GLA_DV_HEAD)
    r = proj[..., o3:o4]
    low = proj[..., o4:]
    log_a = jax.nn.log_sigmoid((low @ w_gate2 + b_gate2).astype(jnp.float32)) / GLA_TAU
    o, s_new = gla_chunked(q, k, v, log_a.reshape(B, T, H, GLA_DK_HEAD), s0)
    o = o * lax.rsqrt(jnp.mean(jnp.square(o), axis=-1, keepdims=True) + LN_EPS)
    o = o.reshape(B, T, GLA_DV) * norm_g * jax.nn.silu(r.astype(jnp.float32))
    return o.astype(x.dtype) @ w_out, s_new

def setup_inputs(seed: int = 0) -> dict:
    key = jax.random.key(seed)
    ks = jax.random.split(key, 24)
    f32 = jnp.float32
    n_pages = PAST_LEN // PAGE_SIZE
    n_used = DEC_BATCH * n_pages
    n_pool = (5 * n_used + 3) // 4
    win_buf = min(WINDOW, PAST_LEN)

    def nrm(k, shape, scale):
        return jax.random.normal(k, shape, f32) * scale

    page_table = jax.random.permutation(ks[0], n_pool)[:n_used].reshape(DEC_BATCH, n_pages).astype(jnp.int32)
    kv_shape = (N_NSA_LAYERS, n_pool, PAGE_SIZE, 2, NSA_KV_HEADS, NSA_HEAD_DIM)
    return {
        'x_prompt': nrm(ks[1], (BATCH, SEQ, D_MODEL), 1.0),
        'x_sample': nrm(ks[2], (DEC_BATCH, DEC_SEQ, D_MODEL), 1.0),
        'cache_cmp_kv': nrm(ks[3], kv_shape, 1.0),
        'cache_slc_kv': nrm(ks[4], kv_shape, 1.0),
        'cache_win_kv': nrm(ks[5], (N_NSA_LAYERS, DEC_BATCH, win_buf, 2, NSA_KV_HEADS, NSA_HEAD_DIM), 1.0),
        'state_gla': nrm(ks[6], (N_GLA_LAYERS, DEC_BATCH, GLA_HEADS, GLA_DK_HEAD, GLA_DV_HEAD), 1.0),
        'page_table': page_table,
        'nsa_w_in': nrm(ks[7], (N_NSA_LAYERS, D_MODEL, NSA_PROJ), D_MODEL ** -0.5),
        'nsa_b_gate': nrm(ks[8], (N_NSA_LAYERS, 3 * NSA_HEADS), 0.1),
        'nsa_pe_cmp': nrm(ks[9], (N_NSA_LAYERS, CMP_BLK, 2, NSA_HEAD_DIM), 0.5),
        'nsa_w_cmp1': nrm(ks[10], (N_NSA_LAYERS, CMP_BLK, 2, NSA_HEAD_DIM, NSA_HEAD_DIM), (CMP_BLK * NSA_HEAD_DIM) ** -0.5),
        'nsa_w_cmp2': nrm(ks[11], (N_NSA_LAYERS, 2, NSA_HEAD_DIM, NSA_HEAD_DIM), NSA_HEAD_DIM ** -0.5),
        'nsa_w_out': nrm(ks[12], (N_NSA_LAYERS, NSA_Q_COLS, D_MODEL), DN_BETA * NSA_Q_COLS ** -0.5),
        'gla_w_in': nrm(ks[13], (N_GLA_LAYERS, D_MODEL, GLA_PROJ), D_MODEL ** -0.5),
        'gla_w_gate2': nrm(ks[14], (N_GLA_LAYERS, GLA_RANK, GLA_DK), GLA_RANK ** -0.5),
        'gla_b_gate2': nrm(ks[15], (N_GLA_LAYERS, GLA_DK), 0.1),
        'gla_norm_g': 1.0 + nrm(ks[16], (N_GLA_LAYERS, GLA_DV), 0.1),
        'gla_w_out': nrm(ks[17], (N_GLA_LAYERS, GLA_DV, D_MODEL), DN_BETA * GLA_DV ** -0.5),
        'ffn_w_gu': nrm(ks[18], (DEPTH, D_MODEL, 2 * D_FF), D_MODEL ** -0.5),
        'ffn_w_down': nrm(ks[19], (DEPTH, D_FF, D_MODEL), DN_BETA * D_FF ** -0.5),
        'ln_g': 1.0 + nrm(ks[20], (DEPTH, 2, D_MODEL), 0.1),
        'ln_b': nrm(ks[21], (DEPTH, 2, D_MODEL), 0.1),
    }

def reference(x_prompt, x_sample, cache_cmp_kv, cache_slc_kv, cache_win_kv, state_gla, page_table,
              nsa_w_in, nsa_b_gate, nsa_pe_cmp, nsa_w_cmp1, nsa_w_cmp2, nsa_w_out,
              gla_w_in, gla_w_gate2, gla_b_gate2, gla_norm_g, gla_w_out,
              ffn_w_gu, ffn_w_down, ln_g, ln_b):
    past_len = page_table.shape[1] * PAGE_SIZE
    pos_p = jnp.arange(x_prompt.shape[1], dtype=jnp.int32)
    pos_s = past_len + jnp.arange(x_sample.shape[1], dtype=jnp.int32)
    cmp_p, slc_p, win_p, gla_p = [], [], [], []
    cmp_s, slc_s, win_s, gla_s = [], [], [], []
    yp, ys = x_prompt, x_sample
    for i in range(DEPTH):
        li = i // N_MIXERS
        if i % N_MIXERS == 0:
            nsa_w = (nsa_w_in[li], nsa_b_gate[li], nsa_pe_cmp[li], nsa_w_cmp1[li], nsa_w_cmp2[li], nsa_w_out[li])
            mp, ckp, skp, wkp = nsa_prompt(yp, pos_p, *nsa_w)
            ms, cks, sks, wks = nsa_sample(ys, pos_s, li, cache_cmp_kv, cache_slc_kv, cache_win_kv,
                                           page_table, *nsa_w)
            cmp_p.append(ckp); slc_p.append(skp); win_p.append(wkp)
            cmp_s.append(cks); slc_s.append(sks); win_s.append(wks)
        else:
            gla_w = (gla_w_in[li], gla_w_gate2[li], gla_b_gate2[li], gla_norm_g[li], gla_w_out[li])
            s0 = jnp.zeros((yp.shape[0], GLA_HEADS, GLA_DK_HEAD, GLA_DV_HEAD), jnp.float32)
            mp, sp = gla_mixer(yp, s0, *gla_w)
            ms, ss = gla_mixer(ys, state_gla[li], *gla_w)
            gla_p.append(sp); gla_s.append(ss)
        yp = layer_norm(DN_ALPHA * yp + mp, ln_g[i, 0], ln_b[i, 0])
        ys = layer_norm(DN_ALPHA * ys + ms, ln_g[i, 0], ln_b[i, 0])
        yp = layer_norm(DN_ALPHA * yp + swiglu(yp, ffn_w_gu[i], ffn_w_down[i]), ln_g[i, 1], ln_b[i, 1])
        ys = layer_norm(DN_ALPHA * ys + swiglu(ys, ffn_w_gu[i], ffn_w_down[i]), ln_g[i, 1], ln_b[i, 1])
    return (yp, ys, jnp.stack(cmp_p), jnp.stack(slc_p), jnp.stack(win_p), jnp.stack(gla_p),
            jnp.stack(cmp_s), jnp.stack(slc_s), jnp.stack(win_s), jnp.stack(gla_s))


_drawn_inputs = setup_inputs


def setup_inputs(seed=0):
    import zlib

    import numpy as np

    out = dict(_drawn_inputs(seed))
    spreads = {}
    factors = {'cache_slc_kv': 5.411, 'nsa_b_gate': 7.736, 'gla_norm_g': 2.699}
    for name, (base, spread) in spreads.items():
        noise = np.random.default_rng([zlib.crc32(name.encode()), seed]).standard_normal(out[name].shape)
        drawn = base * np.exp(spread * noise) if base else spread * noise
        out[name] = jnp.asarray(drawn.astype(out[name].dtype))
    for name, factor in factors.items():
        out[name] = (out[name] * factor).astype(out[name].dtype)
    return out
```

```python
from contextlib import ExitStack

import numpy as np

import concourse.bass as bass
from concourse import mybir

ALU = mybir.AluOpType
ACT = mybir.ActivationFunctionType
AX = mybir.AxisListType
F32 = mybir.dt.float32
I32 = mybir.dt.int32
U32 = mybir.dt.uint32

P = 128
D_MODEL = 1024
KT = D_MODEL // P
SEQ = 512
TILES = SEQ // P
NB = 8
NTOK = SEQ + NB
HALF = NTOK // 2
ROWS = [P] * TILES + [NB]
PAST = 2048
PAGE = 128
PAGES = PAST // PAGE
N_POOL = 160
HEADS = 16
G = 4
R = 4
D = 64
BLK = 64
WIN = 512
NBLK = PAST // BLK + 1
N_SEL = 16
SCALE = D ** -0.5
NEG = -1e30
FORCE = 1e4
NSA_PROJ = 2608
DFF = 2816
FT = DFF // P
ALPHA = 4.0 ** 0.25
EPS = 1e-5
GH = 4
CH = 32
GLA_TAU = 16.0
VEC_B, VEC_N, VEC_Z = 32, 64, 72
VECS = VEC_Z + 4
GSCALE = 128 ** -0.5


class Chain:

    def __init__(self, eng, sem):
        self.eng, self.sem, self.n = eng, sem, 0

    def step(self, ins):
        self.n += 1
        ins.then_inc(self.sem, 1)
        self.eng.wait_ge(self.sem, self.n)


class Semaphores:

    def __init__(self, nc):
        self.nc, self.all = nc, []

    def new(self, name):
        self.all.append(self.nc.alloc_semaphore(name))
        return self.all[-1]

    def recycle(self):
        self.nc.clear_and_free_semaphores(self.all)
        self.nc.all_engine_barrier()
        self.all = []


def phase_project(nc, io, ps, S, cst):
    CW = 512
    CHUNKS = [512] * 5 + [NSA_PROJ - 5 * 512]
    NT = len(ROWS)
    UNITS = [(c, t) for c in range(len(CHUNKS)) for t in range(NT)]
    ROPE_UNITS = [i for i, (c, t) in enumerate(UNITS) if c not in (2, 5)]

    TR = [("q", t, hf) for t in range(TILES) for hf in range(2)] + \
         [("r", t, hf) for t in range(TILES) for hf in range(2)] + \
         [("k", t, br) for t in range(TILES) for br in range(2)]

    with ExitStack() as ctx:
        def sb(name, shape, dt=F32):
            return ctx.enter_context(nc.sbuf_tensor(name, shape, dt))

        def sem(name):
            return cst["sems"].new(name)

        xn = sb("xn", [P, NT, D_MODEL])
        xT = sb("xT0", [P, KT, NTOK])
        w = sb("w_in", [P, 2, KT, CW])
        qn = sb("qn", [P, NT, D_MODEL])
        qrn = sb("qrn", [P, NT, D_MODEL])
        t1 = sb("rope_t1", [P, CW])
        t2 = sb("rope_t2", [P, CW])
        rope = sb("rope_tab", [P, NT, 2, D])
        bg = sb("b_gate", [P, 48])
        gpre = sb("gpre", [P, NT, 48])

        kdup = xn[:, 0:TILES, :].rearrange("p t (a g u d) -> p t a g u d", a=2, g=G, u=2)
        qdup = w[0:NB, 0, 0:4, :].rearrange("b k n -> b (k n)").rearrange("b (h u d) -> b h u d", h=HEADS, u=2)
        qgrp = w[0:NB, 0, 4:6, :].rearrange("b k n -> b (k n)").rearrange("b (j r g d) -> b j r g d", j=2, r=R, g=2)
        kdup_done = sem("kdup_done")
        x_in, w_in = sem("x_in"), [sem("w_in0"), sem("w_in1")]
        tab_in = sem("tab_in")
        xtr_done, xT_ready = sem("xtr_done"), sem("xT_ready")
        proj_done, raw_done, rope_done = sem("proj_done"), sem("raw_done"), sem("rope_done")
        tr_done, trA, trV = sem("tr_done"), sem("tr_evac_act"), sem("tr_evac_dve")
        gate_pre, gate_done = sem("gate_pre"), sem("gate_done")
        vch, vmul, vmul2 = sem("p0_vchain"), sem("p0_vmul"), sem("p0_vmul2")
        smp_tr, smp_ev = sem("smp_tr"), sem("smp_ev")
        kv_out = sem("kv_out")

        W = io["nsa_w_in"][0].rearrange("(k p) n -> p k n", p=P)
        col = [c * CW for c in range(len(CHUNKS))]
        block = ctx.enter_context(nc.Block())

        @block.sync
        def _(sp):
            for t in range(TILES):
                sp.dma_start(xn[:, t, :], io["x_prompt"][0, t * P:(t + 1) * P, :]).then_inc(x_in, 16)
            sp.dma_start(xn[0:NB, TILES, :], io["x_sample"][:, 0, :]).then_inc(x_in, 16)
            for c, n in enumerate(CHUNKS):
                if c >= 2:
                    sp.wait_ge(proj_done, NT * (c - 1))
                sp.dma_start(w[:, c % 2, :, 0:n], W[:, :, col[c]:col[c] + n]).then_inc(w_in[c % 2], 16)
            sp.wait_ge(rope_done, len(ROPE_UNITS))
            sp.wait_ge(raw_done, len(UNITS))
            for src, name in ((S["cmpn"], "cmp"), (S["slcn"], "slc"), (S["winn"], "win")):
                o = io["new_%s_p" % name][0, 0].rearrange("(t p) a g d -> p t (a g d)", p=P)
                sp.dma_start(o, src[:, 0:TILES, :]).then_inc(kv_out, 16)
            for src, name in ((S["cmpn"], "cmp"), (S["slcn"], "slc")):
                o = io["new_%s_s" % name][0].rearrange("b t a g d -> b (t a g d)")
                sp.dma_start(o, src[0:NB, TILES, :]).then_inc(kv_out, 16)
            ow = io["new_win_s"][0].rearrange("b t a g d -> b t (a g d)")
            sp.dma_start(ow[:, WIN - 1, :], S["winn"][0:NB, TILES, :]).then_inc(kv_out, 16)
            cw = io["cache_win"][0].rearrange("b t a g d -> b (t a g d)")
            ROW = 2 * G * D
            sp.dma_start(ow.rearrange("b t n -> b (t n)")[:, 0:(WIN - 1) * ROW],
                         cw[:, ROW:WIN * ROW]).then_inc(kv_out, 16)
            sp.wait_ge(kv_out, 16 * 7)

        @block.gpsimd
        def _(pool):
            pool.dma_start(rope[:], io["rope_tab"]).then_inc(tab_in, 16)
            pool.dma_start(bg[:], io["nsa_b_gate"][0:1, :].to_broadcast([P, 48])).then_inc(tab_in, 16)
            pool.wait_ge(rope_done, len(ROPE_UNITS))
            pool.wait_ge(raw_done, len(UNITS))
            pool.wait_ge(proj_done, len(UNITS))
            for t in range(TILES):
                for br in range(2):
                    k = (S["slcn"], S["winn"])[br][:, t, 0:G * D].rearrange("p (g d) -> p g d", g=G)
                    for u in range(2):
                        ins = nc.gpsimd.tensor_copy(kdup[:, t, br, :, u, :], k)
                ins.then_inc(kdup_done, 1)
            for u in range(2):
                nc.gpsimd.tensor_copy(qdup[:, :, u, :], qn[0:NB, TILES, :].rearrange("b (h d) -> b h d", h=HEADS))
            for j in range(2):
                for gi in range(2):
                    g = 2 * j + gi
                    ins = nc.gpsimd.tensor_copy(qgrp[:, j, :, gi, :],
                                                qrn[0:NB, TILES, g * R * D:(g + 1) * R * D]
                                                .rearrange("b (r d) -> b r d", r=R))
            ins.then_inc(kdup_done, 1)

        @block.tensor
        def _(pe):
            pe.wait_ge(cst["in"], cst["n"])
            pe.wait_ge(x_in, 16 * NT)
            n = 0
            for t in range(NT):
                for hf in range(2):
                    if n >= 2:
                        pe.wait_ge(xT_ready, n - 1)
                    for k in range(4):
                        ins = nc.tensor.transpose(ps[:, n % 2, k * P:k * P + ROWS[t]],
                                                  xn[0:ROWS[t], t, (hf * 4 + k) * P:(hf * 4 + k + 1) * P],
                                                  cst["ident"][0:ROWS[t], 0:ROWS[t]])
                    ins.then_inc(xtr_done, 1)
                    n += 1
            pe.wait_ge(xT_ready, n)
            for u, (c, t) in enumerate(UNITS):
                if t == 0:
                    pe.wait_ge(w_in[c % 2], 16 * (c // 2 + 1))
                if u >= 4:
                    pe.wait_ge(raw_done, u - 3)
                m = CHUNKS[c]
                for k in range(KT):
                    ins = nc.tensor.matmul(ps[0:ROWS[t], 2 + u % 4, 0:m], xT[:, k, t * P:t * P + ROWS[t]],
                                           w[:, c % 2, k, 0:m], start=(k == 0), stop=(k == KT - 1))
                ins.then_inc(proj_done, 1)
            pe.wait_ge(rope_done, len(ROPE_UNITS))
            pe.wait_ge(raw_done, len(UNITS))
            for n, (kind, t, a) in enumerate(TR):
                if n >= 2:
                    pe.wait_ge(trA if n % 2 == 0 else trV, n // 2)
                if kind == "k" and a == 0:
                    pe.wait_ge(kdup_done, t + 1)
                for k in range(4):
                    if kind == "k":
                        src = kdup[:, t, a, k].rearrange("p u d -> p (u d)")
                    else:
                        src = (qn if kind == "q" else qrn)[:, t, (a * 4 + k) * P:(a * 4 + k + 1) * P]
                    ins = nc.tensor.transpose(ps[:, n % 2, k * P:(k + 1) * P], src, cst["ident"][:])
                ins.then_inc(tr_done, 1)
            id8 = cst["ident"][0:NB, 0:NB]
            pe.wait_ge(kdup_done, TILES + 1)
            for h in range(HEADS):
                nc.tensor.transpose(ps[:, 6, h * NB:(h + 1) * NB], qdup[:, h].rearrange("b u d -> b (u d)"), id8)
            for j in range(2):
                for r in range(R):
                    nc.tensor.transpose(ps[:, 7, (j * R + r) * NB:(j * R + r + 1) * NB],
                                        qgrp[:, j, r].rearrange("b g d -> b (g d)"), id8)
            for br in range(2):
                for j in range(2):
                    src = (S["slcn"], S["winn"])[br]
                    c = 64 + (br * 2 + j) * NB
                    ins = nc.tensor.transpose(ps[:, 7, c:c + NB], src[0:NB, TILES, j * P:(j + 1) * P], id8)
            ins.then_inc(smp_tr, 1)

        def tr_dst(n):
            kind, t, a = TR[n]
            if kind == "k":
                return S["kT"][:, a, :, t * P:(t + 1) * P]
            return (S["qT"] if kind == "q" else S["qrT"])[:, a * 4:a * 4 + 4, t * P:(t + 1) * P]

        @block.scalar
        def _(act):
            for u, (c, t) in enumerate(UNITS):
                m = ROWS[t]
                b = ps[0:m, 2 + u % 4, :]
                act.wait_ge(proj_done, u + 1)
                if c < 2:
                    ins = nc.scalar.copy(qn[0:m, t, c * CW:(c + 1) * CW], b)
                elif c == 2:
                    ins = nc.scalar.copy(S["cmpn"][0:m, t, :], b)
                elif c < 5:
                    ins = nc.scalar.copy((S["slcn"], S["winn"])[c - 3][0:m, t, :], b)
                else:
                    ins = nc.scalar.copy(gpre[0:m, t, :], b[:, 0:48])
                ins.then_inc(raw_done, 1)
            for t in range(NT):
                m = ROWS[t]
                act.wait_ge(gate_pre, t + 1)
                nc.scalar.activation(S["gates"][0:m, t, :], gpre[0:m, t, :], ACT.Sigmoid).then_inc(gate_done, 1)
            for n in range(0, len(TR), 2):
                act.wait_ge(tr_done, n + 1)
                nc.scalar.copy(tr_dst(n), ps[:, 0, :].rearrange("p (k t) -> p k t", k=4)).then_inc(trA, 1)

        @block.vector
        def _(dve):
            ch = Chain(dve, vch)
            for n in range(2 * NT):
                t, hf = n // 2, n % 2
                dve.wait_ge(xtr_done, n + 1)
                src = ps[:, n % 2, :].rearrange("p (k t) -> p k t", k=4)[:, :, 0:ROWS[t]]
                nc.vector.tensor_copy(xT[:, hf * 4:hf * 4 + 4, t * P:t * P + ROWS[t]], src).then_inc(xT_ready, 1)
            dve.wait_ge(tab_in, 32)
            roped = 0
            for u in ROPE_UNITS + [i for i, (c, t) in enumerate(UNITS) if c == 5]:
                c, t = UNITS[u]
                m = ROWS[t]
                dve.wait_ge(raw_done, u + 1)
                if c == 5:
                    nc.vector.tensor_tensor(gpre[0:m, t, :], gpre[0:m, t, :], bg[0:m, :],
                                            ALU.add).then_inc(gate_pre, 1)
                    continue
                nh = 8 if c < 2 else 4
                if c < 2:
                    v, out = (q[0:m, t, c * CW:(c + 1) * CW] for q in (qn, qrn))
                else:
                    v = out = (S["slcn"], S["winn"])[c - 3][0:m, t, 0:256]
                v = v.rearrange("p (h d) -> p h d", d=D)
                a = t1[0:m, 0:nh * D].rearrange("p (h d) -> p h d", d=D)
                b = t2[0:m, 0:nh * D].rearrange("p (h d) -> p h d", d=D)
                cos = rope[0:m, t, 0, :].unsqueeze(1).to_broadcast([m, nh, D])
                sin = rope[0:m, t, 1, :].unsqueeze(1).to_broadcast([m, nh, D])
                if roped:
                    dve.wait_ge(rope_done, roped)
                roped += 1
                nc.vector.tensor_tensor(a, v, cos, ALU.mult).then_inc(vmul, 1)
                nc.vector.tensor_tensor(b[:, :, 0:32], v[:, :, 32:64], sin[:, :, 0:32], ALU.mult).then_inc(vmul2, 1)
                dve.wait_ge(vmul2, roped)
                ch.step(nc.vector.tensor_tensor(b[:, :, 32:64], v[:, :, 0:32], sin[:, :, 32:64], ALU.mult))
                dve.wait_ge(vmul, roped)
                nc.vector.tensor_tensor(out.rearrange("p (h d) -> p h d", d=D), a, b, ALU.add).then_inc(rope_done, 1)
            for n in range(1, len(TR), 2):
                dve.wait_ge(tr_done, n + 1)
                nc.vector.tensor_copy(tr_dst(n), ps[:, 1, :].rearrange("p (k t) -> p k t", k=4)).then_inc(trV, 1)
            dve.wait_ge(smp_tr, 1)
            nc.vector.memset(S["qz"][:], 0.0).then_inc(smp_ev, 1)
            nc.vector.tensor_copy(S["qs"][:].rearrange("p b h -> p h b"),
                                  ps[:, 6, 0:P].rearrange("p (h b) -> p h b", h=HEADS))
            nc.vector.tensor_copy(S["knew"][:].rearrange("p a j b -> p (a j b)"), ps[:, 7, 64:96])
            dve.wait_ge(smp_ev, 1)
            for j in range(2):
                for gi in range(2):
                    h0 = 8 * j + 4 * gi
                    dst = S["qz"][64 * gi:64 * gi + 64, j, :, h0:h0 + 4].rearrange("p b r -> p r b")
                    nc.vector.tensor_copy(dst, ps[64 * gi:64 * gi + 64, 7, j * 32:(j + 1) * 32]
                                          .rearrange("p (r b) -> p r b", r=R))


def phase_compress(nc, io, ps, S, cst):
    QP = 32
    PARTS = NB * PAGES // QP
    EXTRA = TILES
    SLOTS = QP + EXTRA + 1
    COLS = QP * G
    XC = EXTRA * G
    NALL = NB * PAGES * G + XC
    UN = [(c, u) for c in range(2) for u in range(PARTS)]

    def cols(u):
        return COLS + (XC + 1 if u == 0 else 0)

    with ExitStack() as ctx:
        def sb(name, shape, dt=F32):
            return ctx.enter_context(nc.sbuf_tensor(name, shape, dt))

        def sem(name):
            return cst["sems"].new(name)

        rows = sb("rows", [P, 2, SLOTS, G, D])
        w1 = sb("w1", [P, D, P])
        w2 = sb("w2", [P, 2, P])
        hid = sb("hid", [P, 2, NALL])
        pe_bias = sb("pe_bias", [P, 2])
        pt = sb("pt", [1, NB * PAGES], I32)
        sig = sb("c_sig", [P, 2, cols(0)])
        pre = sb("c_pre", [P, 2, cols(0)])

        pt_in = sem("pt_in")
        rows_in = [sem("rows_in0"), sem("rows_in1")]
        ex_in = sem("pe_in")
        w1_in, w1v_in, w1_zero, w2_in = sem("w1_in"), sem("w1v_in"), sem("w1_zero"), sem("w2_in")
        ex_ready, conv_done, pre_done, sig_done, hid_done = (sem(n) for n in
                                                             ("ex_ready", "conv_done", "pre_done", "sig_done", "hid_done"))
        bias_done, out_done, ck_done = sem("bias_done"), sem("cmp_out_done"), sem("ck_done")
        block = ctx.enter_context(nc.Block())
        cache = io["cache_cmp"][0].rearrange("n t a g d -> n t a (g d)")

        def rows_parts(n):
            return 16 * QP * (n // 2 + 1)

        @block.sync
        def _(sp):
            sp.dma_start(pt[:], io["page_table"].rearrange("b p -> (b p)").unsqueeze(0)).then_inc(pt_in, 16)
            sp.wait_ge(pt_in, 16)
            for n, (c, u) in enumerate(UN):
                if n >= 2:
                    sp.wait_ge(conv_done, n - 1)
                with sp.Fori(0, QP) as i:
                    page = sp.value_load(pt[0:1, bass.ds(u * QP + i, 1)], min_val=0, max_val=N_POOL - 1)
                    dst = rows[:, n % 2, :, :, :].rearrange("p s g d -> p s (g d)")[:, bass.ds(i, 1), :]
                    sp.dma_start(dst, cache[bass.ds(page, 1), :, c, :].rearrange("n t x -> t n x"))\
                        .then_inc(rows_in[n % 2], 16)

        @block.gpsimd
        def _(pool):
            nc.gpsimd.memset(w1[:], 0.0).then_inc(w1_zero, 1)
            nc.gpsimd.memset(w2[:], 0.0).then_inc(w1_zero, 1)
            for c in range(2):
                n = c * PARTS
                if c:
                    pool.wait_ge(conv_done, n - 1)
                sl = rows[:, n % 2]
                for t in range(TILES):
                    nc.gpsimd.tensor_copy(sl[:, QP + t].rearrange("p g d -> p (g d)"),
                                          S["cmpn"][:, t, c * 256:(c + 1) * 256]).then_inc(ex_ready, 1)
                for hf in range(2):
                    pool.dma_start(sl[64 * hf:64 * hf + 64, QP + EXTRA, 0, :],
                                   io["nsa_pe_cmp"][0, :, c, :]).then_inc(ex_in, 16)
            pool.wait_ge(conv_done, PARTS)
            for hf in range(2):
                o = 64 * hf
                pool.dma_start(w1[o:o + 64, :, o:o + 64], io["nsa_w_cmp1"][0, :, 1]).then_inc(w1v_in, 16)

        @block.scalar
        def _(act):
            act.wait_ge(w1_zero, 2)
            for hf in range(2):
                o = 64 * hf
                act.dma_start(w1[o:o + 64, :, o:o + 64], io["nsa_w_cmp1"][0, :, 0]).then_inc(w1_in, 16)
                for c in range(2):
                    act.dma_start(w2[o:o + 64, c, o:o + 64], io["nsa_w_cmp2"][0, c]).then_inc(w2_in, 16)
            for n in range(len(UN)):
                act.wait_ge(pre_done, n + 1)
                k = cols(UN[n][1])
                if n >= 2:
                    act.wait_ge(hid_done, n - 1)
                nc.scalar.activation(sig[:, n % 2, 0:k], pre[:, n % 2, 0:k], ACT.Sigmoid).then_inc(sig_done, 1)

        @block.vector
        def _(dve):
            for n, (c, u) in enumerate(UN):
                k = cols(u)
                dve.wait_ge(conv_done, n + 1)
                if u == 0:
                    nc.vector.tensor_copy(pe_bias[:, c:c + 1], ps[:, n % 2, k - 1:k]).then_inc(bias_done, 1)
                    dve.wait_ge(bias_done, c + 1)
                if n >= 2:
                    dve.wait_ge(hid_done, n - 1)
                nc.vector.tensor_scalar(pre[:, n % 2, 0:k], ps[:, n % 2, 0:k], pe_bias[:, c:c + 1], None,
                                        ALU.add).then_inc(pre_done, 1)
                dve.wait_ge(sig_done, n + 1)
                dve.wait_ge(pre_done, n + 1)
                if u == 0:
                    nc.vector.tensor_tensor(hid[:, c, NALL - XC:NALL], pre[:, n % 2, COLS:COLS + XC],
                                            sig[:, n % 2, COLS:COLS + XC], ALU.mult).then_inc(out_done, 1)
                nc.vector.tensor_tensor(hid[:, c, u * COLS:(u + 1) * COLS], pre[:, n % 2, 0:COLS],
                                        sig[:, n % 2, 0:COLS], ALU.mult).then_inc(hid_done, 1)
            for c in range(2):
                dve.wait_ge(ck_done, c + 1)
                nc.vector.tensor_copy(S["ckT"][:, c, 0:NALL - XC], ps[:, 2 + c, 0:NALL - XC])
                nc.vector.tensor_copy(S["ckT"][:, c, NALL - XC:NALL], ps[:, 4 + c, 0:XC])

        @block.tensor
        def _(pe):
            for n, (c, u) in enumerate(UN):
                k = cols(u)
                if u == 0:
                    pe.wait_ge(w1v_in if c else w1_in, 32)
                    pe.wait_ge(ex_ready, TILES * (c + 1))
                    pe.wait_ge(ex_in, 32 * (c + 1))
                pe.wait_ge(rows_in[n % 2], rows_parts(n))
                if n >= 2:
                    pe.wait_ge(pre_done, n - 1)
                flat = rows[:, n % 2].rearrange("p s g d -> p d (s g)")
                for d in range(D):
                    ins = nc.tensor.matmul(ps[:, n % 2, 0:k], w1[:, d, :], flat[:, d, 0:k],
                                           start=(d == 0), stop=(d == D - 1))
                ins.then_inc(conv_done, 1)
            pe.wait_ge(w2_in, 64)
            pe.wait_ge(hid_done, len(UN))
            pe.wait_ge(out_done, 2)
            for c in range(2):
                nc.tensor.matmul(ps[:, 2 + c, 0:NALL - XC], w2[:, c, :], hid[:, c, 0:NALL - XC], start=True, stop=True)
                nc.tensor.matmul(ps[:, 4 + c, 0:XC], w2[:, c, :], hid[:, c, NALL - XC:NALL], start=True,
                                 stop=True).then_inc(ck_done, 1)


def phase_cmp_attention(nc, io, ps, S, cst):
    NP4 = TILES * HEADS
    NPB = SEQ // BLK
    COLS = NB * PAGES * G
    with ExitStack() as ctx:
        def sb(name, shape, dt=F32):
            return ctx.enter_context(nc.sbuf_tensor(name, shape, dt))

        def sem(name):
            return cst["sems"].new(name)

        kp = sb("kp", [P, G, NPB])
        vp = sb("vp", [TILES * G, P])
        vb = sb("vb", [P, HEADS, D])
        sp_ = sb("sp_", [P, NP4, NPB])
        mx = sb("mx_p", [P, NP4])
        sm = sb("sm_p", [P, NP4])
        pT = sb("pT_p", [P, TILES, P])
        pm = sb("pm_add", [P, TILES, NPB])
        pm01 = sb("pm_01", [P, TILES, NPB])
        ss = sb("ss", [P, 2, COLS])
        ms = sb("mask_s", [P, COLS])
        mxs, nmx, sms = sb("mxs", [P, 1]), sb("nmx", [P, 1]), sb("sms", [P, 1])
        psT = sb("psT", [P, 8, P])
        vn = sb("vn", [P, 4, P])
        os_ = sb("os_", [P, D])
        gsum = sb("gsum", [P, NB * G])
        expand = sb("expand", [NB * G, NB, HEADS])
        imp = sb("imp", [NB * G, NBLK])
        tri = sb("tri", [NB * G, NBLK, NBLK])
        gt = sb("gt", [NB * G, NBLK, NBLK])
        eq = sb("eq", [NB * G, NBLK, NBLK])
        rank = sb("rank", [NB * G, NBLK])
        sel = sb("sel", [NB * G, NBLK])

        tab, vch, vb_zero = sem("p2_tab"), sem("p2_vchain"), sem("vb_zero")
        kp_ready, s_done, e_ready, e_done, p_ready, pT_done, pT_ready, o_done, o_out = (
            sem(n) for n in ("kp_ready", "s_prompt", "shifted_prompt", "exp_prompt", "p_prompt", "pT_prompt",
                             "pT_in_sbuf", "o_prompt", "o_in_sbuf"))
        vp_done, vp_ready, vb_in = sem("vp_done"), sem("vp_ready"), sem("vb_in")
        s2_done, s2_ready, e2_done, p2_ready, imp_done, sel_ready, selx_done = (
            sem(n) for n in ("s_sample", "max_sample", "exp_sample", "p_sample", "imp_done", "sel_ready", "selx_done"))
        pT2_done, pT2_ready, o2_done, o2_ready, osn_in = (
            sem(n) for n in ("pT_sample", "pT_sample_sbuf", "o_sample", "o_sample_sbuf", "osn_cmp_in"))
        block = ctx.enter_context(nc.Block())

        @block.sync
        def _(sp):
            for dst, name in ((pm, "pm_add"), (pm01, "pm_01"), (ms, "mask_s"), (gsum, "gsum"), (expand, "expand"),
                              (tri, "tri")):
                sp.dma_start(dst[:], io[name + "_tab"]).then_inc(tab, 16)
            sp.wait_ge(vp_ready, 1)
            sp.wait_ge(vb_zero, 1)
            for h in range(HEADS):
                for t in range(TILES):
                    r = t * G + h // R
                    sp.dma_start(vb[h * NPB + 2 * t:h * NPB + 2 * t + 2, h, :],
                                 vp[r:r + 1, :].rearrange("r (u f) -> r u f", u=2)).then_inc(vb_in, 16)
            sp.wait_ge(o2_ready, 1)
            sp.dma_start(S["osn"][:, 0, :].rearrange("b (h d) -> b h d", d=D), os_[:]).then_inc(osn_in, 16)
            sp.wait_ge(osn_in, 16)

        @block.gpsimd
        def _(pool):
            nc.gpsimd.memset(vb[:], 0.0).then_inc(vb_zero, 1)

        @block.tensor
        def _(pe):
            for hf in range(2):
                a = slice(64 * hf, 64 * hf + 64)
                ins = nc.tensor.matmul(ps[:, 1 + hf, :], S["qs"][a].rearrange("p b h -> p (b h)"),
                                       S["ckT"][a, 0, 0:COLS], start=True, stop=True)
            ins.then_inc(s2_done, 1)
            nc.tensor.transpose(ps[0:TILES * G, 7, 0:P], S["ckT"][:, 1, COLS:COLS + TILES * G],
                                cst["ident"][:]).then_inc(vp_done, 1)
            pe.wait_ge(kp_ready, 1)
            for t in range(TILES):
                for h in range(HEADS):
                    a = slice(64 * (h % 2), 64 * (h % 2) + 64)
                    c = (t * HEADS + h) * NPB
                    ins = nc.tensor.matmul(ps[:, 3 * (h % 2), c:c + NPB], S["qT"][a, h // 2, t * P:(t + 1) * P],
                                           kp[a, h // R, :], start=True, stop=True)
            ins.then_inc(s_done, 1)
            pe.wait_ge(p2_ready, 1)
            pe.wait_ge(tab, 16 * 6)
            for hf in range(2):
                ins = nc.tensor.matmul(ps[0:NB * G, 1 + hf, :], gsum[:], ss[:, hf, :], start=True, stop=True)
            ins.then_inc(imp_done, 1)
            for hf in range(2):
                for c in range(4):
                    ins = nc.tensor.transpose(ps[:, 5 + hf, c * P:(c + 1) * P], ss[:, hf, c * P:(c + 1) * P],
                                              cst["ident"][:])
            pe.wait_ge(vp_ready, 1)
            for c in range(4):
                ins = nc.tensor.transpose(ps[:, 7, c * P:(c + 1) * P], S["ckT"][:, 1, c * P:(c + 1) * P],
                                          cst["ident"][:])
            ins.then_inc(pT2_done, 1)
            pe.wait_ge(pT2_ready, 1)
            for n in range(8):
                hf, c = n // 4, n % 4
                ins = nc.tensor.matmul(ps[:, 4, 0:D], psT[:, n, :], vn[:, c, 64 * hf:64 * hf + 64],
                                       start=(n == 0), stop=(n == 7))
            ins.then_inc(o2_done, 1)
            pe.wait_ge(p_ready, 1)
            for t in range(TILES):
                ins = nc.tensor.transpose(ps[:, 5, t * P:(t + 1) * P],
                                          sp_[:, t * HEADS:(t + 1) * HEADS, :].rearrange("p h n -> p (h n)"),
                                          cst["ident"][:])
            ins.then_inc(pT_done, 1)
            pe.wait_ge(sel_ready, 1)
            for b in range(NB):
                ins = nc.tensor.matmul(ps[0:HEADS, 2, b * NBLK:(b + 1) * NBLK], expand[:, b, :], sel[:],
                                       start=True, stop=True)
            ins.then_inc(selx_done, 1)
            pe.wait_ge(pT_ready, 1)
            pe.wait_ge(vb_in, 16 * HEADS * TILES)
            for n in range(2 * TILES):
                t, hf = n // 2, n % 2
                bank = 6 + n % 2
                if n >= 2:
                    pe.wait_ge(o_out, n - 1)
                nc.tensor.matmul(ps[:, bank, :], pT[:, t, :],
                                 vb[:, 8 * hf:8 * hf + 8, :].rearrange("p h d -> p (h d)"),
                                 start=True, stop=True).then_inc(o_done, 1)

        @block.scalar
        def _(act):
            act.wait_ge(s2_ready, 1)
            nc.scalar.activation(ss[:], ss[:], ACT.Exp, bias=nmx[:], scale=SCALE, accum_out=sms[:]).then_inc(e2_done, 1)
            act.wait_ge(e_ready, 1)
            nc.scalar.activation(sp_[:], sp_[:], ACT.Exp, scale=SCALE).then_inc(e_done, 1)
            act.wait_ge(pT2_done, 1)
            nc.scalar.copy(psT[:, 0:4, :], ps[:, 5, :].rearrange("p (c q) -> p c q", c=4))
            nc.scalar.copy(psT[:, 4:8, :], ps[:, 6, :].rearrange("p (c q) -> p c q", c=4))
            nc.scalar.copy(vn[:], ps[:, 7, :].rearrange("p (c q) -> p c q", c=4)).then_inc(pT2_ready, 1)
            act.wait_ge(o2_done, 1)
            nc.scalar.copy(os_[:], ps[:, 4, 0:D]).then_inc(o2_ready, 1)
            act.wait_ge(pT_done, 1)
            nc.scalar.copy(pT[:], ps[:, 5, :].rearrange("p (t q) -> p t q", t=TILES)).then_inc(pT_ready, 1)
            for n in range(2 * TILES):
                act.wait_ge(o_done, n + 1)
                nc.scalar.copy(S["oacc"][:, n // 2, 512 * (n % 2):512 * (n % 2) + 512], ps[:, 6 + n % 2, :])\
                    .then_inc(o_out, 1)

        @block.vector
        def _(dve):
            ch = Chain(dve, vch)
            for dup in range(2):
                for hf in range(2):
                    src = S["ckT"][64 * hf:64 * hf + 64, 0, COLS:].rearrange("p (t g) -> p g t", g=G)
                    dst = kp[64 * dup:64 * dup + 64].rearrange("p g (t u) -> p g t u", u=2)[:, :, :, hf]
                    ins = nc.vector.tensor_copy(dst, src)
                    if dup == 0 or hf == 0:
                        ch.step(ins)
            ins.then_inc(kp_ready, 1)
            dve.wait_ge(vp_done, 1)
            nc.vector.tensor_copy(vp[:], ps[0:TILES * G, 7, 0:P]).then_inc(vp_ready, 1)
            dve.wait_ge(tab, 16 * 6)
            dve.wait_ge(s2_done, 1)
            for hf in range(2):
                ch.step(nc.vector.tensor_tensor(ss[:, hf, :], ps[:, 1 + hf, :], ms[:], ALU.add))
            ch.step(nc.vector.tensor_reduce(mxs[:], ss[:].rearrange("p a c -> p (a c)"), AX.X, ALU.max))
            nc.vector.tensor_scalar(nmx[:], mxs[:], -SCALE, None, ALU.mult).then_inc(s2_ready, 1)
            dve.wait_ge(e2_done, 1)
            ch.step(nc.vector.reciprocal(sms[:], sms[:]))
            nc.vector.tensor_scalar(ss[:], ss[:], sms[:], None, ALU.mult).then_inc(p2_ready, 1)
            dve.wait_ge(s_done, 1)
            s4 = sp_[:].rearrange("p (t h) n -> p t h n", t=TILES)
            for t in range(TILES):
                for par in range(2):
                    src = ps[:, 3 * par, t * P:(t + 1) * P].rearrange("p (h u n) -> p h u n", u=2, n=NPB)[:, :, par]
                    ch.step(nc.vector.tensor_tensor(s4[:, t].rearrange("p (h u) n -> p h u n", u=2)[:, :, par], src,
                                                    pm[:, t, :].unsqueeze(1).to_broadcast([P, HEADS // 2, NPB]),
                                                    ALU.add))
            ch.step(nc.vector.tensor_reduce(mx[:], sp_[:], AX.X, ALU.max))
            nc.vector.tensor_tensor(sp_[:], sp_[:], mx[:].unsqueeze(2).to_broadcast([P, NP4, NPB]),
                                    ALU.subtract).then_inc(e_ready, 1)
            dve.wait_ge(e_done, 1)
            for t in range(TILES):
                ch.step(nc.vector.tensor_tensor(s4[:, t], s4[:, t],
                                                pm01[:, t, :].unsqueeze(1).to_broadcast([P, HEADS, NPB]), ALU.mult))
            ch.step(nc.vector.tensor_reduce(sm[:], sp_[:], AX.X, ALU.add))
            ch.step(nc.vector.tensor_scalar(sm[:], sm[:], 1e-30, None, ALU.max))
            ch.step(nc.vector.reciprocal(sm[:], sm[:]))
            ch.step(nc.vector.tensor_tensor(sm[:].rearrange("p (t h) -> p t h", t=TILES),
                                            sm[:].rearrange("p (t h) -> p t h", t=TILES),
                                            S["gates"][:, 0:TILES, 0:HEADS], ALU.mult))
            nc.vector.tensor_tensor(sp_[:], sp_[:], sm[:].unsqueeze(2).to_broadcast([P, NP4, NPB]),
                                    ALU.mult).then_inc(p_ready, 1)
            dve.wait_ge(imp_done, 1)
            iv = imp[:, 0:NBLK - 1].rearrange("q (p u) -> q p u", u=2)
            for hf in range(2):
                ch.step(nc.vector.tensor_reduce(iv[:, :, hf], ps[0:NB * G, 1 + hf, :]
                                                .rearrange("q (b p g) -> q p b g", b=NB, g=G), AX.XY, ALU.add))
            ch.step(nc.vector.memset(imp[:, NBLK - 2:NBLK], FORCE))
            ch.step(nc.vector.memset(imp[:, 0:1], FORCE))
            a = imp[:].unsqueeze(1).to_broadcast([NB * G, NBLK, NBLK])
            b = imp[:].unsqueeze(2).to_broadcast([NB * G, NBLK, NBLK])
            ch.step(nc.vector.tensor_tensor(gt[:], a, b, ALU.is_gt))
            ch.step(nc.vector.tensor_tensor(eq[:], a, b, ALU.is_equal))
            ch.step(nc.vector.tensor_tensor(eq[:], eq[:], tri[:], ALU.mult))
            ch.step(nc.vector.tensor_tensor(gt[:], gt[:], eq[:], ALU.add))
            ch.step(nc.vector.tensor_reduce(rank[:], gt[:], AX.X, ALU.add))
            nc.vector.tensor_scalar(sel[:], rank[:], N_SEL - 0.5, None, ALU.is_lt).then_inc(sel_ready, 1)
            dve.wait_ge(selx_done, 1)
            nc.vector.tensor_scalar(S["selneg"][:].rearrange("h b n -> h (b n)"), ps[0:HEADS, 2, 0:NB * NBLK],
                                    -1.0, -NEG, ALU.add, ALU.mult)


def phase_sample_attention(nc, io, ps, S, cst):
    WP = WIN // PAGE
    NPG = PAGES + WP
    GRP = NPG // 4
    NS, NW = PAST + 1, WIN + 1
    KEYS = NS + NW
    with ExitStack() as ctx:
        def sb(name, shape, dt=F32):
            return ctx.enter_context(nc.sbuf_tensor(name, shape, dt))

        def sem(name):
            return cst["sems"].new(name)

        kv = sb("kv", [P, 2, NPG, 2 * G * D])
        dead = S["cmpn"][:].rearrange("p t n -> p (t n)")
        kTs = dead[:, 0:2048].rearrange("p (s j n) -> p s j n", s=2, j=2)
        pt = sb("pt3", [1, NB * PAGES], I32)
        sc = S["actA"][0:HEADS].rearrange("h k n -> h (k n)")[:, 0:KEYS]
        pTs = dead[:, 2048:2048 + (NPG + 2) * HEADS].rearrange("p (n h) -> p n h", h=HEADS)
        vnew = sb("vnew", [1, 2, 2, G * D])
        gm = sb("gmask", [HEADS, G])
        mx, nmx, sm = sb("mx3", [HEADS, 2]), sb("nmx3", [HEADS, 2]), sb("sm3", [HEADS, NB, 2])
        og = sb("og", [HEADS, 2, G, D])
        ob = S["ckT"][0:HEADS].rearrange("h a n -> h (a n)")[:, 0:2 * NB * D].rearrange("h (a b d) -> h a b d", a=2,
                                                                                       b=NB)

        pt_in, vn_in, gm_in = sem("pt3_in"), [sem("vnew_in0"), sem("vnew_in1")], sem("gmask_in")
        kv_in, wkv_in = [sem("kv_in0"), sem("kv_in1")], [sem("wkv_in0"), sem("wkv_in1")]
        ktr_done, kT_a, kT_v = sem("ktr_done"), sem("kT_evac_act"), sem("kT_evac_dve")
        sc_done, sc_out, new_done = sem("sc_done"), sem("sc_out"), sem("sc_new_done")
        mx_ready, exp_done, pT_done, pT_out, pv_done, og_done = (
            sem(n) for n in ("mx_ready3", "exp_done3", "pT_done3", "pT_out3", "pv_done3", "og_done3"))
        vch, ob_ready, osn_in = sem("p3_vchain"), sem("ob_ready"), sem("osn_in")
        block = ctx.enter_context(nc.Block())
        cache = io["cache_slc"][0].rearrange("n t a g d -> n t (a g d)")
        wcache = io["cache_win"][0].rearrange("b (w p) a g d -> b p w (a g d)", p=P)

        def key0(i):
            return i * PAGE if i < PAGES else NS + (i - PAGES) * PAGE

        @block.sync
        def _(sp):
            sp.dma_start(pt[:], io["page_table"].rearrange("b p -> (b p)").unsqueeze(0)).then_inc(pt_in, 16)
            sp.dma_start(gm[:], io["gmask_tab"]).then_inc(gm_in, 16)
            sp.wait_ge(pt_in, 16)
            for b in range(NB):
                if b >= 2:
                    sp.wait_ge(pv_done, b - 1)
                for br, src in enumerate((S["slcn"], S["winn"])):
                    sp.dma_start(vnew[:, b % 2, br, :], src[b:b + 1, TILES, G * D:]).then_inc(vn_in[b % 2], 16)
                sp.dma_start(kv[:, b % 2, PAGES:NPG, :], wcache[b]).then_inc(wkv_in[b % 2], 16)
                with sp.Fori(0, PAGES) as i:
                    page = sp.value_load(pt[0:1, bass.ds(b * PAGES + i, 1)], min_val=0, max_val=N_POOL - 1)
                    sp.dma_start(kv[:, b % 2, bass.ds(i, 1), :], cache[bass.ds(page, 1)].rearrange("n t x -> t n x"))\
                        .then_inc(kv_in[b % 2], 16)
            sp.wait_ge(ob_ready, 2 * NB)
            for br in range(2):
                for b in range(NB):
                    sp.dma_start(S["osn"][b:b + 1, 1 + br, :].rearrange("b (h d) -> b h d", d=D),
                                 ob[:, br, b, :]).then_inc(osn_in, 16)
            sp.wait_ge(osn_in, 16 * 2 * NB)

        def scores(pe, n):
            b, g = n // GRP, n % GRP
            pe.wait_ge(kT_a, n + 1)
            pe.wait_ge(kT_v, n + 1)
            if n >= 2:
                pe.wait_ge(sc_out, n - 1)
            for j in range(2):
                ins = nc.tensor.matmul(ps[0:HEADS, 4 + n % 2, :], S["qz"][:, j, b, :], kTs[:, n % 2, j, :],
                                       start=(j == 0), stop=(j == 1))
            ins.then_inc(sc_done, 1)
            if g == GRP - 1:
                if b >= 1:
                    pe.wait_ge(og_done, 2 * b)
                for br in range(2):
                    for j in range(2):
                        ins = nc.tensor.matmul(ps[0:HEADS, 7, br:br + 1], S["qz"][:, j, b, :],
                                               S["knew"][:, br, j, b:b + 1], start=(j == 0), stop=(j == 1))
                ins.then_inc(new_done, 1)

        def finish(pe, b):
            pe.wait_ge(exp_done, 2 * (b + 1))
            if b >= 1:
                pe.wait_ge(pT_out, b)
            idh = cst["ident"][0:HEADS, 0:HEADS]
            for i in range(NPG):
                nc.tensor.transpose(ps[:, 6, i * HEADS:(i + 1) * HEADS], sc[:, key0(i):key0(i) + PAGE], idh)
            for br in range(2):
                last = (NS if br == 0 else KEYS) - 1
                c = (NPG + br) * HEADS
                ins = nc.tensor.transpose(ps[0:1, 6, c:c + HEADS], sc[:, last:last + 1], idh)
            ins.then_inc(pT_done, 1)
            pe.wait_ge(pT_out, b + 1)
            pe.wait_ge(mx_ready, 2 * (b + 1))
            pe.wait_ge(vn_in[b % 2], 32 * (b // 2 + 1))
            for br in range(2):
                pages = range(PAGES) if br == 0 else range(PAGES, NPG)
                for i in pages:
                    nc.tensor.matmul(ps[0:HEADS, 7, br * 256:br * 256 + 256], pTs[:, i, :],
                                     kv[:, b % 2, i, 256:512], start=(i == pages[0]), stop=False)
                ins = nc.tensor.matmul(ps[0:HEADS, 7, br * 256:br * 256 + 256], pTs[0:1, NPG + br, :],
                                       vnew[0:1, b % 2, br, :], start=False, stop=True)
            ins.then_inc(pv_done, 1)

        @block.tensor
        def _(pe):
            for b in range(NB):
                for g in range(GRP):
                    n = b * GRP + g
                    if g == 0:
                        pe.wait_ge(kv_in[b % 2], 16 * PAGES * (b // 2 + 1))
                        pe.wait_ge(wkv_in[b % 2], 16 * (b // 2 + 1))
                    if n >= 2:
                        pe.wait_ge(kT_a, n - 1)
                        pe.wait_ge(kT_v, n - 1)
                    for j in range(2):
                        for i in range(4):
                            ins = nc.tensor.transpose(ps[:, 2 * (n % 2) + j, i * P:(i + 1) * P],
                                                      kv[:, b % 2, 4 * g + i, j * P:(j + 1) * P], cst["ident"][:])
                    ins.then_inc(ktr_done, 1)
                    if n >= 1:
                        scores(pe, n - 1)
                    if g == 1 and b >= 1:
                        finish(pe, b - 1)
            scores(pe, NB * GRP - 1)
            finish(pe, NB - 1)

        @block.scalar
        def _(act):
            for n in range(NB * GRP + 1):
                if n < NB * GRP:
                    act.wait_ge(ktr_done, n + 1)
                    if n >= 2:
                        act.wait_ge(sc_done, n - 1)
                    nc.scalar.copy(kTs[:, n % 2, 0, :], ps[:, 2 * (n % 2), :]).then_inc(kT_a, 1)
                if n >= GRP and n % GRP == 0:
                    b = n // GRP - 1
                    for br, a, z in ((0, 0, NS), (1, NS, KEYS)):
                        act.wait_ge(mx_ready, 2 * b + br + 1)
                        nc.scalar.activation(sc[:, a:z], sc[:, a:z], ACT.Exp, bias=nmx[:, br:br + 1], scale=SCALE,
                                             accum_out=sm[:, b, br:br + 1]).then_inc(exp_done, 1)

        @block.vector
        def _(dve):
            ch = Chain(dve, vch)

            def evac(n):
                dve.wait_ge(ktr_done, n + 1)
                if n >= 2:
                    dve.wait_ge(sc_done, n - 1)
                nc.vector.tensor_copy(kTs[:, n % 2, 1, :], ps[:, 2 * (n % 2) + 1, :]).then_inc(kT_v, 1)

            def take(n):
                b, g = n // GRP, n % GRP
                dve.wait_ge(sc_done, n + 1)
                if g == 0 and b >= 1:
                    dve.wait_ge(pT_done, b)
                src = ps[0:HEADS, 4 + n % 2, :]
                if g < GRP - 1:
                    m = S["selneg"][:, b, 8 * g:8 * g + 8].unsqueeze(2).to_broadcast([HEADS, 8, BLK])
                    nc.vector.tensor_tensor(sc[:, g * 512:(g + 1) * 512].rearrange("h (n l) -> h n l", l=BLK),
                                            src.rearrange("h (n l) -> h n l", l=BLK), m, ALU.add).then_inc(sc_out, 1)
                else:
                    nc.vector.tensor_copy(sc[:, NS:NS + WIN], src).then_inc(sc_out, 1)
                    dve.wait_ge(new_done, b + 1)
                    ch.step(nc.vector.tensor_copy(sc[:, NS - 1:NS], ps[0:HEADS, 7, 0:1]))
                    ch.step(nc.vector.tensor_copy(sc[:, KEYS - 1:KEYS], ps[0:HEADS, 7, 1:2]))
                    dve.wait_ge(sc_out, n + 1)
                    for br, a, z in ((0, 0, NS), (1, NS, KEYS)):
                        ch.step(nc.vector.tensor_reduce(mx[:, br:br + 1], sc[:, a:z], AX.X, ALU.max))
                        if b >= 1:
                            dve.wait_ge(exp_done, 2 * b)
                        nc.vector.tensor_scalar(nmx[:, br:br + 1], mx[:, br:br + 1], -SCALE, None,
                                                ALU.mult).then_inc(mx_ready, 1)

            def take_pT(b):
                dve.wait_ge(pT_done, b + 1)
                if b >= 1:
                    dve.wait_ge(pv_done, b)
                nc.vector.tensor_copy(pTs[:, 0:NPG, :].rearrange("p n h -> p (n h)"), ps[:, 6, 0:NPG * HEADS])
                nc.vector.tensor_copy(pTs[0:1, NPG:NPG + 2, :].rearrange("p n h -> p (n h)"),
                                      ps[0:1, 6, NPG * HEADS:(NPG + 2) * HEADS]).then_inc(pT_out, 1)

            def take_o(b):
                dve.wait_ge(pv_done, b + 1)
                ch.step(nc.vector.reciprocal(sm[:, b, :], sm[:, b, :]))
                for br in range(2):
                    nc.vector.tensor_tensor(og[:, br], ps[0:HEADS, 7, br * 256:br * 256 + 256]
                                            .rearrange("h (g d) -> h g d", g=G),
                                            gm[:].unsqueeze(2).to_broadcast([HEADS, G, D]), ALU.mult)\
                        .then_inc(og_done, 1)
                    dve.wait_ge(og_done, 2 * b + br + 1)
                    ch.step(nc.vector.tensor_reduce(ob[:, br, b, :], og[:, br].rearrange("h g d -> h d g"), AX.X,
                                                    ALU.add))
                    nc.vector.tensor_scalar(ob[:, br, b, :], ob[:, br, b, :], sm[:, b, br:br + 1], None,
                                            ALU.mult).then_inc(ob_ready, 1)

            dve.wait_ge(gm_in, 16)
            for n in range(NB * GRP + 1):
                if n < NB * GRP:
                    evac(n)
                if n % GRP == 1 and n > GRP:
                    take_pT(n // GRP - 1)
                if n >= 1:
                    take(n - 1)
                if n % GRP == 3 and n > GRP:
                    take_o(n // GRP - 1)
            take_pT(NB - 1)
            take_o(NB - 1)


def phase_prompt_attention(nc, io, ps, S, cst):
    assert SEQ // BLK <= N_SEL and SEQ <= WIN
    UN = [(br, t, p) for br in range(2) for t in range(TILES) for p in range(HEADS // 2)]
    U = len(UN)
    with ExitStack() as ctx:
        def sb(name, shape, dt=F32):
            return ctx.enter_context(nc.sbuf_tensor(name, shape, dt))

        def sem(name):
            return cst["sems"].new(name)

        e = sb("e4", [P, 2, 2, 512])
        pT = sb("pT4", [P, 2, 2, 512])
        causal = sb("causal", [P, P])
        mx, nmx, sm, rg = (sb(n, [P, 2, 2]) for n in ("mx4", "nmx4", "sm4", "rg4"))
        tab = sem("causal_in")
        qk_done, masked, maxed, nmx_ready, exp_done, tp_done, pT_a, pT_v, pv_done, recip, rg_ready, o_done = (
            sem(n) for n in ("qk_done4", "masked4", "maxed4", "nmx_ready4", "exp_done4", "tp_done4", "pT_act4",
                             "pT_dve4", "pv_done4", "recip4", "rg_ready4", "o_done4"))
        block = ctx.enter_context(nc.Block())

        @block.sync
        def _(sp):
            sp.dma_start(causal[:], io["causal_tab"]).then_inc(tab, 16)

        @block.tensor
        def _(pe):
            def qk(n):
                br, t, p = UN[n]
                w = (t + 1) * P
                if n >= 2:
                    pe.wait_ge(exp_done, 2 * (n - 1))
                for s in range(2):
                    a = slice(64 * s, 64 * s + 64)
                    nc.tensor.matmul(ps[:, 2 * (n % 2) + s, 0:w], S["qrT"][a, p, t * P:(t + 1) * P],
                                     S["kT"][a, br, p // 2, 0:w], start=True, stop=True).then_inc(qk_done, 1)

            def turn(n):
                t = UN[n][1]
                pe.wait_ge(exp_done, 2 * (n + 1))
                if n >= 1:
                    pe.wait_ge(pT_a, n)
                    pe.wait_ge(pT_v, n)
                for s in range(2):
                    for k in range(t + 1):
                        ins = nc.tensor.transpose(ps[:, 4 + s, k * P:(k + 1) * P], e[:, n % 2, s, k * P:(k + 1) * P],
                                                  cst["ident"][:])
                ins.then_inc(tp_done, 1)

            def pv(n):
                br, t, p = UN[n]
                pe.wait_ge(pT_a, n + 1)
                pe.wait_ge(pT_v, n + 1)
                if n >= 2:
                    pe.wait_ge(o_done, 2 * (n - 1))
                v = (S["slcn"], S["winn"])[br]
                c = G * D + (p // 2) * D
                for s in range(2):
                    for k in range(t + 1):
                        ins = nc.tensor.matmul(ps[:, 6 + n % 2, s * D:(s + 1) * D], pT[:, n % 2, s, k * P:(k + 1) * P],
                                               v[:, k, c:c + D], start=(k == 0), stop=(k == t))
                ins.then_inc(pv_done, 1)

            for n in range(U + 2):
                if n < U:
                    qk(n)
                if n >= 2:
                    pv(n - 2)
                if 1 <= n <= U:
                    turn(n - 1)

        @block.scalar
        def _(act):
            for n in range(U + 1):
                if n < U:
                    w = (UN[n][1] + 1) * P
                    act.wait_ge(nmx_ready, n + 1)
                    if n >= 2:
                        act.wait_ge(tp_done, n - 1)
                        act.wait_ge(rg_ready, n - 1)
                    for s in range(2):
                        nc.scalar.activation(e[:, n % 2, s, 0:w], ps[:, 2 * (n % 2) + s, 0:w], ACT.Exp,
                                             bias=nmx[:, n % 2, s:s + 1], scale=SCALE,
                                             accum_out=sm[:, n % 2, s:s + 1]).then_inc(exp_done, 1)
                if n >= 1:
                    w = (UN[n - 1][1] + 1) * P
                    act.wait_ge(tp_done, n)
                    if n >= 3:
                        act.wait_ge(pv_done, n - 2)
                    nc.scalar.copy(pT[:, (n - 1) % 2, 0, 0:w], ps[:, 4, 0:w]).then_inc(pT_a, 1)

        @block.vector
        def _(dve):
            def stats(n):
                t = UN[n][1]
                w = (t + 1) * P
                dve.wait_ge(qk_done, 2 * (n + 1))
                sc = ps[:, 2 * (n % 2):2 * (n % 2) + 2, 0:w]
                m = causal[:].unsqueeze(1).to_broadcast([P, 2, P])
                nc.vector.tensor_tensor(sc[:, :, t * P:w], sc[:, :, t * P:w], m, ALU.add).then_inc(masked, 1)
                dve.wait_ge(masked, n + 1)
                nc.vector.tensor_reduce(mx[:, n % 2], sc, AX.X, ALU.max).then_inc(maxed, 1)
                dve.wait_ge(maxed, n + 1)
                if n >= 2:
                    dve.wait_ge(exp_done, 2 * (n - 1))
                nc.vector.tensor_scalar(nmx[:, n % 2], mx[:, n % 2], -SCALE, None, ALU.mult).then_inc(nmx_ready, 1)

            def copy(n):
                w = (UN[n][1] + 1) * P
                dve.wait_ge(tp_done, n + 1)
                if n >= 2:
                    dve.wait_ge(pv_done, n - 1)
                nc.vector.tensor_copy(pT[:, n % 2, 1, 0:w], ps[:, 5, 0:w]).then_inc(pT_v, 1)

            def gate(n):
                br, t, p = UN[n]
                dve.wait_ge(exp_done, 2 * (n + 1))
                if n >= 2:
                    dve.wait_ge(o_done, 2 * (n - 1))
                nc.vector.reciprocal(rg[:, n % 2], sm[:, n % 2]).then_inc(recip, 1)
                dve.wait_ge(recip, n + 1)
                c = (1 + br) * HEADS + 2 * p
                nc.vector.tensor_tensor(rg[:, n % 2], rg[:, n % 2], S["gates"][:, t, c:c + 2],
                                        ALU.mult).then_inc(rg_ready, 1)

            def add(n):
                br, t, p = UN[n]
                dve.wait_ge(pv_done, n + 1)
                dve.wait_ge(rg_ready, n + 1)
                for s in range(2):
                    o = S["oacc"][:, t, (2 * p + s) * D:(2 * p + s + 1) * D]
                    nc.vector.scalar_tensor_tensor(out=o, in0=ps[:, 6 + n % 2, s * D:(s + 1) * D],
                                                   scalar=rg[:, n % 2, s:s + 1], in1=o, op0=ALU.mult,
                                                   op1=ALU.add).then_inc(o_done, 1)

            dve.wait_ge(tab, 16)
            for n in range(U + 3):
                if n < U:
                    stats(n)
                if n >= 3:
                    if n == 3 + U // 2:
                        dve.wait_ge(o_done, U)
                    add(n - 3)
                if 1 <= n <= U:
                    gate(n - 1)
                if 1 <= n <= U:
                    copy(n - 1)


def phase_attention_out(nc, io, ps, S, cst):
    NT = len(ROWS)
    with ExitStack() as ctx:
        def sem(name):
            return cst["sems"].new(name)

        og = ctx.enter_context(nc.sbuf_tensor("os_gated", [NB, 3, D_MODEL], F32))
        os_ = ctx.enter_context(nc.sbuf_tensor("os_sum", [NB, D_MODEL], F32))
        vch, os_ready, tr_done, tr_out = sem("p5_vchain"), sem("os_ready"), sem("otr_done"), sem("otr_out")
        block = ctx.enter_context(nc.Block())

        @block.tensor
        def _(pe):
            pe.wait_ge(os_ready, 1)
            for n in range(2 * NT):
                t, hf = n // 2, n % 2
                if n >= 4:
                    pe.wait_ge(tr_out, n - 3)
                for k in range(4 * hf, 4 * hf + 4):
                    src = S["oacc"][:, t] if t < TILES else os_[:]
                    ins = nc.tensor.transpose(ps[:, n % 4, (k % 4) * P:(k % 4) * P + ROWS[t]],
                                              src[:, k * P:(k + 1) * P], cst["ident"][0:ROWS[t], 0:ROWS[t]])
                ins.then_inc(tr_done, 1)

        @block.vector
        def _(dve):
            ch = Chain(dve, vch)
            for br in range(3):
                g = S["gates"][0:NB, TILES, br * HEADS:(br + 1) * HEADS].unsqueeze(2).to_broadcast([NB, HEADS, D])
                ch.step(nc.vector.tensor_tensor(og[:, br].rearrange("b (h d) -> b h d", d=D),
                                                S["osn"][:, br].rearrange("b (h d) -> b h d", d=D), g, ALU.mult))
            ch.step(nc.vector.tensor_tensor(os_[:], og[:, 0], og[:, 1], ALU.add))
            nc.vector.tensor_tensor(os_[:], os_[:], og[:, 2], ALU.add).then_inc(os_ready, 1)
            for n in range(2 * NT):
                t, hf = n // 2, n % 2
                dve.wait_ge(tr_done, n + 1)
                nc.vector.tensor_copy(S["actA"][:, 4 * hf:4 * hf + 4, t * P:t * P + ROWS[t]],
                                      ps[:, n % 4].rearrange("p (k t) -> p k t", k=4)[:, :, 0:ROWS[t]])\
                    .then_inc(tr_out, 1)


def phase_residual_in(nc, io, ps, xT, cst):
    NT = len(ROWS)
    with ExitStack() as ctx:
        def sem(name):
            return cst["sems"].new(name)

        xn = ctx.enter_context(nc.sbuf_tensor("xn5", [P, NT, D_MODEL], F32))
        x_in, tr_done, tr_out = sem("x_in5"), sem("xtr_done5"), sem("xtr_out5")
        block = ctx.enter_context(nc.Block())

        @block.sync
        def _(sp):
            sp.dma_start(xn[:, 0:TILES, :], io["x_prompt"][0].rearrange("(t p) n -> p t n", p=P)).then_inc(x_in, 16)
            sp.dma_start(xn[0:NB, TILES, :], io["x_sample"][:, 0, :]).then_inc(x_in, 16)

        @block.tensor
        def _(pe):
            pe.wait_ge(x_in, 32)
            for n in range(2 * NT):
                t, hf = n // 2, n % 2
                if n >= 4:
                    pe.wait_ge(tr_out, n - 3)
                for k in range(4 * hf, 4 * hf + 4):
                    ins = nc.tensor.transpose(ps[:, n % 4, (k % 4) * P:(k % 4) * P + ROWS[t]],
                                              xn[0:ROWS[t], t, k * P:(k + 1) * P],
                                              cst["ident"][0:ROWS[t], 0:ROWS[t]])
                ins.then_inc(tr_done, 1)

        @block.vector
        def _(dve):
            for n in range(2 * NT):
                t, hf = n // 2, n % 2
                dve.wait_ge(tr_done, n + 1)
                nc.vector.tensor_copy(xT[:, 4 * hf:4 * hf + 4, t * P:t * P + ROWS[t]],
                                      ps[:, n % 4].rearrange("p (k t) -> p k t", k=4)[:, :, 0:ROWS[t]])\
                    .then_inc(tr_out, 1)


def phase_linear(nc, ps, cst, name, W, kt, mt, src, dst, residual):
    assert mt % 2 == 0
    with ExitStack() as ctx:
        def sem(n):
            return cst["sems"].new(n + "_" + name)

        w = ctx.enter_context(nc.sbuf_tensor("w_" + name, [P, 2, kt, P], F32))
        w_in = [sem("w_in0"), sem("w_in1")]
        mm_done, out_done = [sem("mm_done0"), sem("mm_done1")], [sem("out_done0"), sem("out_done1")]
        Wv = W.rearrange("(k p) n -> p k n", p=P)
        block = ctx.enter_context(nc.Block())

        @block.sync
        def _(sp):
            with sp.Fori(0, mt // 2) as i:
                for s in range(2):
                    sp.wait_ge(mm_done[s], i + 1)
                    sp.dma_start(w[:, s], Wv[:, :, bass.ds((2 * i + s) * P, P)]).then_inc(w_in[s], 16)

        @block.tensor
        def _(pe):
            for s in range(2):
                pe.sem_inc(mm_done[s], 1)
            with pe.Fori(0, mt // 2) as i:
                for s in range(2):
                    pe.wait_ge(w_in[s], 16 * i + 16)
                    pe.wait_ge(out_done[s], i + 1)
                    for hf in range(2):
                        for k in range(kt):
                            ins = nc.tensor.matmul(ps[:, 2 * s + hf, 0:HALF], w[:, s, k, :],
                                                   src[:, k, hf * HALF:(hf + 1) * HALF],
                                                   start=(k == 0), stop=(k == kt - 1))
                    ins.then_inc(mm_done[s], 1)

        @block.vector
        def _(dve):
            for s in range(2):
                dve.sem_inc(out_done[s], 1)
            with dve.Fori(0, mt // 2) as i:
                for s in range(2):
                    dve.wait_ge(mm_done[s], i + 2)
                    y = ps[:, 2 * s:2 * s + 2, 0:HALF]
                    d = dst[:, bass.ds(2 * i + s, 1), :].rearrange("p a (f n) -> p (a f) n", f=2)
                    if residual:
                        ins = nc.vector.scalar_tensor_tensor(out=d, in0=d, scalar=ALPHA, in1=y, op0=ALU.mult,
                                                             op1=ALU.add)
                    else:
                        ins = nc.vector.tensor_copy(d, y)
                    ins.then_inc(out_done[s], 1)


def phase_gate_up(nc, ps, cst, name, W, src, dst):
    with ExitStack() as ctx:
        def sem(n):
            return cst["sems"].new(n + "_" + name)

        w = ctx.enter_context(nc.sbuf_tensor("w_" + name, [P, 2, 2, KT, P], F32))
        sg = ctx.enter_context(nc.sbuf_tensor("silu_" + name, [P, 2, 2, HALF], F32))
        w_in = [sem("w_in0"), sem("w_in1")]
        mm_done, out_done = [sem("mm_done0"), sem("mm_done1")], [sem("out_done0"), sem("out_done1")]
        silu_done = [sem("silu0"), sem("silu1")]
        Wv = W.rearrange("(k p) n -> p k n", p=P)
        block = ctx.enter_context(nc.Block())

        @block.sync
        def _(sp):
            with sp.Fori(0, FT // 2) as i:
                for s in range(2):
                    sp.wait_ge(mm_done[s], i + 1)
                    for u in range(2):
                        sp.dma_start(w[:, s, u], Wv[:, :, bass.ds((2 * i + s + u * FT) * P, P)]).then_inc(w_in[s], 16)

        @block.tensor
        def _(pe):
            for s in range(2):
                pe.sem_inc(mm_done[s], 1)
            with pe.Fori(0, FT // 2) as i:
                for s in range(2):
                    pe.wait_ge(w_in[s], 32 * i + 32)
                    pe.wait_ge(out_done[s], i + 1)
                    for u in range(2):
                        for hf in range(2):
                            for k in range(KT):
                                ins = nc.tensor.matmul(ps[:, 4 * s + 2 * u + hf, 0:HALF], w[:, s, u, k, :],
                                                       src[:, k, hf * HALF:(hf + 1) * HALF],
                                                       start=(k == 0), stop=(k == KT - 1))
                    ins.then_inc(mm_done[s], 1)

        @block.scalar
        def _(act):
            with act.Fori(0, FT // 2) as i:
                for s in range(2):
                    act.wait_ge(mm_done[s], i + 2)
                    act.wait_ge(out_done[s], i + 1)
                    nc.scalar.activation(sg[:, s], ps[:, 4 * s:4 * s + 2, 0:HALF], ACT.Silu).then_inc(silu_done[s], 1)

        @block.vector
        def _(dve):
            for s in range(2):
                dve.sem_inc(out_done[s], 1)
            with dve.Fori(0, FT // 2) as i:
                for s in range(2):
                    dve.wait_ge(silu_done[s], i + 1)
                    d = dst[:, bass.ds(2 * i + s, 1), :].rearrange("p a (f n) -> p (a f) n", f=2)
                    nc.vector.tensor_tensor(d, sg[:, s], ps[:, 4 * s + 2:4 * s + 4, 0:HALF], ALU.mult)\
                        .then_inc(out_done[s], 1)


def phase_layer_norm(nc, io, ps, name, layer, which, xT, cst):
    with ExitStack() as ctx:
        def sb(n, shape):
            return ctx.enter_context(nc.sbuf_tensor(n + "_" + name, shape, F32))

        def sem(n):
            return cst["sems"].new(n + "_" + name)

        at = (layer * 2 + which) * KT
        gain, shift = cst["vec"][:, at:at + KT], cst["vec"][:, VEC_B + at:VEC_B + at + KT]
        sq = sb("ln_sq", [P, 2, KT, HALF])
        sd = sb("ln_sd", [P, 2, HALF])
        mean_done, centred, squared, var_done, std, rstd, scaled = (
            sem(n) for n in ("mean", "centred", "squared", "var", "std", "rstd", "scaled"))
        block = ctx.enter_context(nc.Block())

        def half(hf):
            return xT[:, :, hf * HALF:(hf + 1) * HALF]

        def wide(a):
            return a.unsqueeze(1).to_broadcast([P, KT, HALF])

        @block.tensor
        def _(pe):
            for hf in range(2):
                for k in range(KT):
                    ins = nc.tensor.matmul(ps[:, hf, 0:HALF], cst["mean"][:], half(hf)[:, k], start=(k == 0),
                                           stop=(k == KT - 1))
                ins.then_inc(mean_done, 1)
            for hf in range(2):
                pe.wait_ge(squared, hf + 1)
                for k in range(KT):
                    ins = nc.tensor.matmul(ps[:, 2 + hf, 0:HALF], cst["mean"][:], sq[:, hf, k], start=(k == 0),
                                           stop=(k == KT - 1))
                ins.then_inc(var_done, 1)

        @block.scalar
        def _(act):
            for hf in range(2):
                act.wait_ge(centred, hf + 1)
                nc.scalar.activation(sq[:, hf], half(hf), ACT.Square).then_inc(squared, 1)
            for hf in range(2):
                act.wait_ge(var_done, hf + 1)
                nc.scalar.activation(sd[:, hf], ps[:, 2 + hf, 0:HALF], ACT.Sqrt, bias=cst["eps"][:]).then_inc(std, 1)
            for hf in range(2):
                act.wait_ge(scaled, hf + 1)
                for k in range(0, KT, 2):
                    nc.scalar.activation(half(hf)[:, k], half(hf)[:, k], ACT.Identity, bias=shift[:, k:k + 1],
                                         scale=gain[:, k:k + 1])

        @block.vector
        def _(dve):
            for hf in range(2):
                dve.wait_ge(mean_done, hf + 1)
                nc.vector.tensor_tensor(half(hf), half(hf), wide(ps[:, hf, 0:HALF]), ALU.subtract).then_inc(centred, 1)
            for hf in range(2):
                dve.wait_ge(std, hf + 1)
                nc.vector.reciprocal(sd[:, hf], sd[:, hf]).then_inc(rstd, 1)
                dve.wait_ge(rstd, hf + 1)
                dve.wait_ge(centred, hf + 1)
                nc.vector.tensor_tensor(half(hf), half(hf), wide(sd[:, hf]), ALU.mult).then_inc(scaled, 1)
                dve.wait_ge(scaled, hf + 1)
                for k in range(1, KT, 2):
                    nc.vector.tensor_scalar(half(hf)[:, k], half(hf)[:, k], gain[:, k:k + 1], shift[:, k:k + 1],
                                            ALU.mult, ALU.add)


def phase_store_y(nc, io, ps, xT, cst):
    NT = len(ROWS)
    with ExitStack() as ctx:
        def sem(name):
            return cst["sems"].new(name)

        yn = ctx.enter_context(nc.sbuf_tensor("yn", [P, NT, D_MODEL], F32))
        tr_done, tr_out, y_out = sem("ytr_done"), sem("ytr_out"), sem("y_out")
        block = ctx.enter_context(nc.Block())

        @block.tensor
        def _(pe):
            for n in range(2 * NT):
                t, hf = n // 2, n % 2
                if n >= 4:
                    pe.wait_ge(tr_out, n - 3)
                for k in range(4 * hf, 4 * hf + 4):
                    ins = nc.tensor.transpose(ps[0:ROWS[t], n % 4, (k % 4) * P:(k % 4 + 1) * P],
                                              xT[:, k, t * P:t * P + ROWS[t]], cst["ident"][:])
                ins.then_inc(tr_done, 1)

        @block.vector
        def _(dve):
            for n in range(2 * NT):
                t, hf = n // 2, n % 2
                dve.wait_ge(tr_done, n + 1)
                nc.vector.tensor_copy(yn[0:ROWS[t], t, hf * 512:(hf + 1) * 512], ps[0:ROWS[t], n % 4, :])\
                    .then_inc(tr_out, 1)

        @block.sync
        def _(sp):
            for t in range(NT):
                sp.wait_ge(tr_out, 2 * (t + 1))
                o = io["y_p"][0, t * P:(t + 1) * P, :] if t < TILES else io["y_s"][:, 0, :]
                sp.dma_start(o, yn[0:ROWS[t], t, :]).then_inc(y_out, 16)
            sp.wait_ge(y_out, 16 * NT)


def phase_gla_v_gate(nc, io, ps, xT, T, cst):
    NT = len(ROWS)
    V0, LOW0 = 1024, 3072
    with ExitStack() as ctx:
        def sb(name, shape):
            return ctx.enter_context(nc.sbuf_tensor(name, shape, F32))

        def sem(name):
            return cst["sems"].new(name)

        w = sb("w_v", [P, 2, KT, 512])
        wl, wg, low = sb("w_low", [P, KT, 16]), sb("w_gate2", [16, 512]), sb("lowT", [16, NTOK])
        w_in, wl_in, low_done, low_out, z_done, z_out, v_done, v_out = (
            sem(n) for n in ("wv_in", "wlow_in", "low_done", "low_out", "z_done", "z_out", "v_done", "v_out"))
        wv1_in = sem("wv1_in")
        W = io["gla_w_in"][0].rearrange("(k p) n -> p k n", p=P)
        block = ctx.enter_context(nc.Block())

        @block.sync
        def _(sp):
            sp.dma_start(wl[:], W[:, :, LOW0:LOW0 + 16]).then_inc(wl_in, 16)
            sp.dma_start(wg[:], io["gla_w_gate2"][0]).then_inc(wl_in, 16)
            for c, s in ((0, w_in), (1, wv1_in)):
                sp.dma_start(w[:, c], W[:, :, V0 + c * 512:V0 + (c + 1) * 512]).then_inc(s, 16)

        @block.tensor
        def _(pe):
            pe.wait_ge(wl_in, 32)
            for hf in range(2):
                for k in range(KT):
                    ins = nc.tensor.matmul(ps[0:16, hf, 0:HALF], wl[:, k, :], xT[:, k, hf * HALF:(hf + 1) * HALF],
                                           start=(k == 0), stop=(k == KT - 1))
            ins.then_inc(low_done, 1)
            for u in range(2 * NT):
                c, t = u // NT, u % NT
                if t == 0:
                    pe.wait_ge((w_in, wv1_in)[c], 16)
                if u >= 2:
                    pe.wait_ge(v_out, u - 1)
                for k in range(KT):
                    ins = nc.tensor.matmul(ps[0:ROWS[t], 2 + u % 2, :], xT[:, k, t * P:t * P + ROWS[t]], w[:, c, k, :],
                                           start=(k == 0), stop=(k == KT - 1))
                ins.then_inc(v_done, 1)
                if u == 1:
                    pe.wait_ge(low_out, 1)
                if 1 <= u <= 4:
                    m = u - 1
                    if m >= 2:
                        pe.wait_ge(z_out, m - 1)
                    for hf in range(2):
                        ins = nc.tensor.matmul(ps[:, 4 + 2 * (m % 2) + hf, 0:HALF], wg[:, m * P:(m + 1) * P],
                                               low[:, hf * HALF:(hf + 1) * HALF], start=True, stop=True)
                    ins.then_inc(z_done, 1)

        @block.vector
        def _(dve):
            dve.wait_ge(low_done, 1)
            nc.vector.tensor_copy(low[:].rearrange("p (f n) -> p f n", f=2), ps[0:16, 0:2, 0:HALF]).then_inc(low_out, 1)
            for m in range(4):
                dve.wait_ge(z_done, m + 1)
                z = T["z"][:, m, :].rearrange("p (f n) -> p f n", f=2)
                nc.vector.tensor_scalar(z, ps[:, 4 + 2 * (m % 2):6 + 2 * (m % 2), 0:HALF],
                                        cst["vec"][:, VEC_Z + m:VEC_Z + m + 1], None, ALU.add).then_inc(z_out, 1)

        @block.scalar
        def _(act):
            for u in range(2 * NT):
                c, t = u // NT, u % NT
                act.wait_ge(v_done, u + 1)
                nc.scalar.copy(T["v"][0:ROWS[t], t, c * 512:(c + 1) * 512], ps[0:ROWS[t], 2 + u % 2, :]).then_inc(v_out, 1)


def phase_gla_core(nc, io, ps, T, cst):
    NCH = SEQ // CH
    CPT = P // CH
    with ExitStack() as ctx:
        def sb(name, shape, dt=F32):
            return ctx.enter_context(nc.sbuf_tensor(name, shape, dt))

        def sem(name):
            return cst["sems"].new(name)

        a = sb("g_a", [P, GH, NTOK])
        lb = sb("g_lb", [P, GH, SEQ])
        ep = sb("g_ep", [P, GH, SEQ])
        ki = sb("g_ki", [P, GH, SEQ])
        ks = a[:].rearrange("p h n -> p (h n)")[:, 0:GH * SEQ].rearrange("p (h n) -> p h n", h=GH)
        ksn = T["z"][:].rearrange("p h n -> p (h n)")[:, 0:GH * SEQ].rearrange("p (t h n) -> p t h n", t=TILES, h=GH)
        att = sb("g_att", [P, TILES, GH, P])
        mask = sb("g_mask", [P, P], I32)
        reset = sb("g_reset", [P, SEQ])
        st = sb("g_state", [P, NCH, GH, 256])
        tab, ach, vch = sem("g_tab"), sem("g_achain"), sem("g_vchain")
        soft, lb_ready, ep_done, en_done, d_ready, ed_done, qk_ready, ks_ready, att_zero = (
            sem(n) for n in ("g_soft", "g_lb", "g_ep", "g_en", "g_d", "g_ed", "g_qk", "g_ks", "g_attz"))
        tr_done, tr_out, att_done, att_out, kv_done, st_done, o_done, o_out, st_out = (
            sem(n) for n in ("g_tr", "g_tr_out", "g_att_done", "g_att_out", "g_kv", "g_st", "g_o", "g_o_out",
                             "g_st_out"))
        block = ctx.enter_context(nc.Block())
        q, k = T["qk"][:, 0:GH, 0:SEQ], T["qk"][:, GH:2 * GH, 0:SEQ]
        KV = [(t, hp) for t in range(TILES) for hp in range(2)]

        @block.sync
        def _(sp):
            sp.dma_start(mask[:], io["gla_mask_tab"]).then_inc(tab, 16)
            sp.dma_start(reset[:], io["gla_reset_tab"]).then_inc(tab, 16)
            sp.wait_ge(st_done, 2 * GH * NCH // 2)
            sp.dma_start(io["new_gla_p"][0, 0].rearrange("h k v -> k h v"), st[:, NCH - 1]).then_inc(st_out, 16)
            sp.wait_ge(st_out, 16)

        @block.gpsimd
        def _(pool):
            nc.gpsimd.memset(att[:], 0.0).then_inc(att_zero, 1)

        @block.scalar
        def _(act):
            ch = Chain(act, ach)
            ch.step(nc.scalar.activation(a[:], T["z"][:], ACT.Abs))
            ch.step(nc.scalar.activation(a[:], a[:], ACT.Exp, scale=-1.0))
            nc.scalar.activation(a[:], a[:], ACT.Ln, bias=cst["one"][:]).then_inc(soft, 1)
            act.wait_ge(lb_ready, 1)
            nc.scalar.activation(ep[:], lb[:], ACT.Exp, scale=1.0 / GLA_TAU).then_inc(ep_done, 1)
            nc.scalar.activation(ki[:], lb[:], ACT.Exp, scale=-1.0 / GLA_TAU).then_inc(en_done, 1)
            ch.step(nc.scalar.activation(T["as"][:], T["z"][:, :, SEQ:NTOK], ACT.Exp, scale=1.0 / GLA_TAU))
            act.wait_ge(d_ready, 1)
            nc.scalar.activation(ks, ks, ACT.Exp, scale=1.0 / GLA_TAU).then_inc(ed_done, 1)
            for t in range(TILES):
                act.wait_ge(tr_done, t + 1)
                nc.scalar.copy(ksn[:, t], ps[:, t % 2, :].rearrange("p (h n) -> p h n", h=GH)).then_inc(tr_out, 1)
            for u in range(8):
                act.wait_ge(o_done, u + 1)
                nc.scalar.copy(T["o"][:, u, 0:SEQ], ps[:, u % 4, :]).then_inc(o_out, 1)

        @block.vector
        def _(dve):
            ch = Chain(dve, vch)
            dve.wait_ge(tab, 32)
            dve.wait_ge(soft, 1)
            ch.step(nc.vector.scalar_tensor_tensor(out=T["z"][:], in0=T["z"][:], scalar=0.0, in1=a[:], op0=ALU.min,
                                                   op1=ALU.subtract))
            for h in range(GH):
                ins = nc.vector.tensor_tensor_scan(lb[:, h, :], reset[:], T["z"][:, h, 0:SEQ], 0.0, ALU.mult, ALU.add)
                if h < GH - 1:
                    ch.step(ins)
            ins.then_inc(lb_ready, 1)
            dve.wait_ge(lb_ready, 1)
            l4 = lb[:].rearrange("p h (c n) -> p h c n", n=CH)
            d4 = ks.rearrange("p h (c n) -> p h c n", n=CH)
            nc.vector.tensor_tensor(d4, l4[:, :, :, CH - 1:CH].to_broadcast([P, GH, NCH, CH]), l4,
                                    ALU.subtract).then_inc(d_ready, 1)
            dve.wait_ge(ep_done, 1)
            ch.step(nc.vector.scalar_tensor_tensor(out=q, in0=q, scalar=GSCALE, in1=ep[:], op0=ALU.mult, op1=ALU.mult))
            dve.wait_ge(en_done, 1)
            nc.vector.tensor_tensor(ki[:], ki[:], k, ALU.mult).then_inc(qk_ready, 1)
            dve.wait_ge(ed_done, 1)
            nc.vector.tensor_tensor(ks, ks, k, ALU.mult).then_inc(ks_ready, 1)
            dve.wait_ge(att_zero, 1)
            for t in range(TILES):
                dve.wait_ge(att_done, t + 1)
                nc.vector.copy_predicated(att[:, t], mask[:].unsqueeze(1).to_broadcast([P, GH, P]),
                                          ps[:, 2 + t % 2, :].rearrange("p (h n) -> p h n", h=GH)).then_inc(att_out, 1)
            done = 0
            for u, (t, hp) in enumerate(KV):
                dve.wait_ge(kv_done, CPT * (u + 1))
                for c in range(CPT):
                    j = t * CPT + c
                    for s in range(2):
                        h = 2 * hp + s
                        kv = ps[:, 4 * (u % 2) + c, s * 256:(s + 1) * 256]
                        if j == 0:
                            ins = nc.vector.tensor_copy(st[:, 0, h], kv)
                        else:
                            ins = nc.vector.scalar_tensor_tensor(out=st[:, j, h], in0=st[:, j - 1, h],
                                                                 scalar=ep[:, h, (j + 1) * CH - 1:(j + 1) * CH],
                                                                 in1=kv, op0=ALU.mult, op1=ALU.add)
                        ins.then_inc(st_done, 1)
                        done += 1
                    dve.wait_ge(st_done, done)

        @block.tensor
        def _(pe):
            pe.wait_ge(ks_ready, 1)
            pe.wait_ge(qk_ready, 1)
            for t in range(TILES):
                sl = slice(t * P, (t + 1) * P)
                if t >= 2:
                    pe.wait_ge(tr_out, t - 1)
                for h in range(GH):
                    ins = nc.tensor.transpose(ps[:, t % 2, h * P:(h + 1) * P], ks[:, h, sl], cst["ident"][:])
                ins.then_inc(tr_done, 1)
                if t >= 2:
                    pe.wait_ge(att_out, t - 1)
                for h in range(GH):
                    ins = nc.tensor.matmul(ps[:, 2 + t % 2, h * P:(h + 1) * P], ki[:, h, sl], q[:, h, sl],
                                           start=True, stop=True)
                ins.then_inc(att_done, 1)
            pe.wait_ge(tr_out, TILES)
            pe.wait_ge(att_out, TILES)
            for u, (t, hp) in enumerate(KV):
                if u >= 2:
                    pe.wait_ge(st_done, 8 * (u - 1))
                for c in range(CPT):
                    r = slice(c * CH, (c + 1) * CH)
                    for s in range(2):
                        h = 2 * hp + s
                        ins = nc.tensor.matmul(ps[:, 4 * (u % 2) + c, s * 256:(s + 1) * 256], ksn[r, t, h, :],
                                               T["v"][r, t, h * 256:(h + 1) * 256], start=True, stop=True,
                                               tile_position=(c * CH, 0))
                    ins.then_inc(kv_done, 1)
            pe.wait_ge(st_done, 2 * GH * NCH // 2)
            for u in range(8):
                h, dv = u // 2, (u % 2) * P
                if u >= 4:
                    pe.wait_ge(o_out, u - 3)
                for t in range(TILES):
                    nc.tensor.matmul(ps[:, u % 4, t * P:(t + 1) * P], T["v"][:, t, h * 256 + dv:h * 256 + dv + P],
                                     att[:, t, h, :], start=True, stop=False, skip_group_check=True)
                    for c in range(CPT):
                        j = t * CPT + c
                        if j:
                            ins = nc.tensor.matmul(ps[:, u % 4, j * CH:(j + 1) * CH], st[:, j - 1, h, dv:dv + P],
                                                   q[:, h, j * CH:(j + 1) * CH], start=False, stop=True,
                                                   skip_group_check=True)
                ins.then_inc(o_done, 1)


def phase_gla_sample(nc, io, ps, T, cst):
    with ExitStack() as ctx:
        def sb(name, shape, dt=F32):
            return ctx.enter_context(nc.sbuf_tensor(name, shape, dt))

        def sem(name):
            return cst["sems"].new(name)

        st = sb("s_state", [P, NB, GH, 256])
        hot = sb("s_onehot", [NB, NB, P])
        qs = sb("s_q", [P, GH, NB])
        st_in, hot_in = [sem("s_state_in%d" % b) for b in range(NB)], sem("s_onehot_in")
        q_ready, vb_done, decayed, st_done, o_done, o_out, st_out = (
            sem(n) for n in ("s_q_ready", "s_vb", "s_decayed", "s_state_done", "s_o", "s_o_out", "s_state_out"))
        block = ctx.enter_context(nc.Block())

        @block.sync
        def _(sp):
            sp.dma_start(hot[:], io["onehot_tab"]).then_inc(hot_in, 16)
            for b in range(NB):
                sp.dma_start(st[:, b], io["state_gla"][0, b].rearrange("h k v -> k h v")).then_inc(st_in[b], 16)
            for b in range(NB):
                sp.wait_ge(st_done, GH * (b + 1))
                sp.dma_start(io["new_gla_s"][0, b].rearrange("h k v -> k h v"), st[:, b]).then_inc(st_out, 16)
            sp.wait_ge(st_out, 16 * NB)

        @block.tensor
        def _(pe):
            pe.wait_ge(hot_in, 16)
            pe.wait_ge(q_ready, 1)

            def spread(b):
                if b >= 3:
                    pe.wait_ge(st_done, GH * (b - 2))
                for c in range(2):
                    ins = nc.tensor.matmul(ps[:, 2 + 2 * (b % 3) + c, :], hot[:, b, :],
                                           T["v"][0:NB, TILES, c * 512:(c + 1) * 512], start=True, stop=True)
                ins.then_inc(vb_done, 1)

            spread(0)
            for b in range(NB):
                if b + 1 < NB:
                    spread(b + 1)
                pe.wait_ge(st_done, GH * (b + 1))
                for h in range(GH):
                    for dv in range(2):
                        c = (2 * h + dv) * NB + b
                        ins = nc.tensor.matmul(ps[:, 0, c:c + 1], st[:, b, h, dv * P:(dv + 1) * P],
                                               qs[:, h, b:b + 1], start=True, stop=True)
            ins.then_inc(o_done, 1)

        @block.scalar
        def _(act):
            for b in range(NB):
                act.wait_ge(st_in[b], 16)
                for h in range(GH):
                    nc.scalar.activation(st[:, b, h], st[:, b, h], ACT.Copy, scale=T["as"][:, h, b:b + 1])\
                        .then_inc(decayed, 1)

        @block.vector
        def _(dve):
            nc.vector.tensor_scalar(qs[:], T["qk"][:, 0:GH, SEQ:NTOK], GSCALE, None, ALU.mult).then_inc(q_ready, 1)
            for b in range(NB):
                dve.wait_ge(vb_done, b + 1)
                for h in range(GH):
                    dve.wait_ge(decayed, GH * b + h + 1)
                    nc.vector.scalar_tensor_tensor(out=st[:, b, h], in0=ps[:, 2 + 2 * (b % 3) + h // 2,
                                                                           (h % 2) * 256:(h % 2) * 256 + 256],
                                                   scalar=T["qk"][:, GH + h, SEQ + b:SEQ + b + 1], in1=st[:, b, h],
                                                   op0=ALU.mult, op1=ALU.add).then_inc(st_done, 1)
            dve.wait_ge(o_done, 1)
            nc.vector.tensor_copy(T["o"][:, :, SEQ:NTOK], ps[:, 0, 0:8 * NB].rearrange("p (k b) -> p k b", k=8))


def phase_gla_gate_out(nc, ps, T, cst):
    with ExitStack() as ctx:
        def sb(name, shape, dt=F32):
            return ctx.enter_context(nc.sbuf_tensor(name, shape, dt))

        def sem(name):
            return cst["sems"].new(name)

        sq = sb("n_sq", [P, 8, NTOK])
        sd = sb("n_sd", [P, GH, NTOK])
        squared, ms_done, std, rstd, scaled, silu = (sem(n) for n in ("n_sq_done", "n_ms", "n_std", "n_rstd",
                                                                      "n_scaled", "n_silu"))
        block = ctx.enter_context(nc.Block())

        @block.scalar
        def _(act):
            for h in range(GH):
                nc.scalar.activation(sq[:, 2 * h:2 * h + 2], T["o"][:, 2 * h:2 * h + 2], ACT.Square).then_inc(squared, 1)
            nc.scalar.activation(T["r"][:], T["r"][:], ACT.Silu).then_inc(silu, 1)
            for h in range(GH):
                act.wait_ge(ms_done, h + 1)
                nc.scalar.activation(sd[:, h].rearrange("p (f n) -> p f n", f=2), ps[:, 2 * h:2 * h + 2, 0:HALF],
                                     ACT.Sqrt, bias=cst["eps"][:], scale=4.0).then_inc(std, 1)

        @block.tensor
        def _(pe):
            for h in range(GH):
                pe.wait_ge(squared, h + 1)
                for hf in range(2):
                    for c in range(2):
                        ins = nc.tensor.matmul(ps[:, 2 * h + hf, 0:HALF], cst["mean"][:],
                                               sq[:, 2 * h + c, hf * HALF:(hf + 1) * HALF],
                                               start=(c == 0), stop=(c == 1))
                ins.then_inc(ms_done, 1)

        @block.vector
        def _(dve):
            for h in range(GH):
                dve.wait_ge(std, h + 1)
                nc.vector.reciprocal(sd[:, h], sd[:, h]).then_inc(rstd, 1)
                dve.wait_ge(rstd, h + 1)
                nc.vector.tensor_tensor(T["o"][:, 2 * h:2 * h + 2], T["o"][:, 2 * h:2 * h + 2],
                                        sd[:, h].unsqueeze(1).to_broadcast([P, 2, NTOK]), ALU.mult).then_inc(scaled, 1)
            dve.wait_ge(silu, 1)
            dve.wait_ge(scaled, GH)
            for k in range(8):
                nc.vector.scalar_tensor_tensor(out=T["o"][:, k], in0=T["o"][:, k],
                                               scalar=cst["vec"][:, VEC_N + k:VEC_N + k + 1], in1=T["r"][:, k],
                                               op0=ALU.mult, op1=ALU.mult)


def shape_tables():
    half = D // 2
    inv = (10000.0 ** (-np.arange(half) / half)).astype(np.float32)
    pos = np.zeros((P, len(ROWS)), np.float32)
    pos[:, :TILES] = np.arange(SEQ, dtype=np.float32).reshape(TILES, P).T
    pos[:, TILES] = PAST
    ang = (pos[:, :, None] * inv).astype(np.float32)
    rope = np.zeros((P, len(ROWS), 2, D), np.float32)
    rope[:, :, 0, :half] = rope[:, :, 0, half:] = np.cos(ang)
    rope[:, :, 1, :half] = -np.sin(ang)
    rope[:, :, 1, half:] = np.sin(ang)
    n = np.arange(SEQ // BLK)
    ok = ((n + 1) * BLK - 1)[None, None, :] <= (np.arange(TILES)[None, :, None] * P + np.arange(P)[:, None, None])
    q, k = np.arange(P)[:, None], np.arange(NB * PAGES * G)[None, :]
    own = (q // HEADS == k // (PAGES * G)) & ((q % HEADS) // R == k % G)
    bg = np.arange(NB * G)[None, :]
    gsum = (q // HEADS == bg // G) & ((q % HEADS) // R == bg % G)
    expand = gsum.T.reshape(NB * G, NB, HEADS)
    tri = np.broadcast_to(np.arange(NBLK)[None, :] < np.arange(NBLK)[:, None], (NB * G, NBLK, NBLK))
    f = np.float32
    return {"rope_tab": rope, "ident_tab": np.eye(P, dtype=f), "pm_01_tab": ok.astype(f),
            "pm_add_tab": np.where(ok, f(0), f(NEG)), "mask_s_tab": np.where(own, f(0), f(NEG)),
            "gsum_tab": gsum.astype(f), "expand_tab": np.ascontiguousarray(expand.astype(f)),
            "tri_tab": tri.astype(f),
            "gla_mask_tab": ((q // CH == q.T // CH) & (q <= q.T)).astype(np.int32),
            "gla_reset_tab": np.broadcast_to(f(1) * (np.arange(SEQ) % CH != 0), (P, SEQ)).astype(f),
            "onehot_tab": np.broadcast_to(np.eye(NB, dtype=f)[:, :, None], (NB, NB, P)).copy(),
            "causal_tab": np.where(np.arange(P)[None, :] <= np.arange(P)[:, None], f(0), f(NEG)),
            "gmask_tab": (np.arange(HEADS)[:, None] // R == np.arange(G)[None, :]).astype(f)}


def feed_forward(nc, io, ps, layer, xT, cst):
    with nc.sbuf_tensor("hT%d" % layer, [P, FT, NTOK], F32) as hT:
        phase_gate_up(nc, ps, cst, "gu%d" % layer, io["ffn_w_gu"][layer], xT, hT)
        phase_linear(nc, ps, cst, "down%d" % layer, io["ffn_w_down"][layer], FT, KT, hT, xT, True)
    phase_layer_norm(nc, io, ps, "ln%d1" % layer, layer, 1, xT, cst)


def build(nc, io):
    with ExitStack() as top:
        def sb(name, shape, dt=F32):
            return top.enter_context(nc.sbuf_tensor(name, shape, dt))

        ps = top.enter_context(nc.psum_tensor("ps", [P, 8, 512], F32))
        cst = {"ident": sb("ident", [P, P]), "in": top.enter_context(nc.semaphore("consts_in")), "n": 16}
        cst["sems"] = sems = Semaphores(nc)
        with nc.Block() as block:
            @block.sync
            def _(sp):
                sp.dma_start(cst["ident"][:], io["ident_tab"]).then_inc(cst["in"], 16)
        S = {"actA": sb("actA", [P, KT, NTOK])}
        S["qT"] = S["actA"][:, :, 0:SEQ]
        cst["mean"] = sb("mean_mat", [P, P])
        cst["eps"] = sb("eps", [P, 1])
        cst["one"] = sb("one", [P, 1])
        cst["vec"] = sb("vec", [P, VECS])
        with nc.Block() as block, nc.sbuf_tensor("vec_rows", [VECS, P], F32) as rows, \
                nc.semaphore("vec_in") as vec_in, nc.semaphore("vec_tr") as vec_tr:
            @block.sync
            def _(sp):
                for at, v in ((0, io["ln_g"].rearrange("l w (k p) -> (l w k) p", p=P)),
                              (VEC_B, io["ln_b"].rearrange("l w (k p) -> (l w k) p", p=P)),
                              (VEC_N, io["gla_norm_g"].rearrange("l (k p) -> (l k) p", p=P)),
                              (VEC_Z, io["gla_b_gate2"].rearrange("l (k p) -> (l k) p", p=P))):
                    sp.dma_start(rows[at:at + v.shape[0], :], v).then_inc(vec_in, 16)

            @block.tensor
            def _(pe):
                pe.wait_ge(cst["in"], cst["n"])
                pe.wait_ge(vec_in, 16 * 4)
                nc.tensor.transpose(ps[:, 0, 0:VECS], rows[:], cst["ident"][0:VECS, 0:VECS]).then_inc(vec_tr, 1)

            @block.vector
            def _(dve):
                dve.wait_ge(vec_tr, 1)
                nc.vector.tensor_copy(cst["vec"][:], ps[:, 0, 0:VECS])
                nc.vector.memset(cst["mean"][:], 1.0 / D_MODEL)
                nc.vector.memset(cst["eps"][:], EPS)
                nc.vector.memset(cst["one"][:], 1.0)
        with ExitStack() as nsa:
            def keep(name, shape):
                S[name] = nsa.enter_context(nc.sbuf_tensor(name, shape, F32))

            keep("qrT", [P, KT, SEQ])
            keep("kT", [P, 2, G, SEQ])
            keep("cmpn", [P, len(ROWS), 512])
            keep("slcn", [P, len(ROWS), 512])
            keep("winn", [P, len(ROWS), 512])
            keep("gates", [P, len(ROWS), 48])
            keep("qs", [P, NB, HEADS])
            keep("qz", [P, 2, NB, HEADS])
            keep("knew", [P, 2, 2, NB])
            phase_project(nc, io, ps, S, cst)
            keep("ckT", [P, 2, NB * PAGES * G + TILES * G])
            phase_compress(nc, io, ps, S, cst)
            keep("oacc", [P, TILES, D_MODEL])
            keep("osn", [NB, 3, D_MODEL])
            keep("selneg", [HEADS, NB, NBLK])
            phase_cmp_attention(nc, io, ps, S, cst)
            sems.recycle()
            phase_sample_attention(nc, io, ps, S, cst)
            phase_prompt_attention(nc, io, ps, S, cst)
            phase_attention_out(nc, io, ps, S, cst)
        sems.recycle()
        xT = sb("xT", [P, KT, NTOK])
        phase_residual_in(nc, io, ps, xT, cst)
        phase_linear(nc, ps, cst, "nsa_out", io["nsa_w_out"][0], KT, KT, S["actA"], xT, True)
        phase_layer_norm(nc, io, ps, "ln00", 0, 0, xT, cst)
        feed_forward(nc, io, ps, 0, xT, cst)
        with ExitStack() as gla:
            T = {"o": S["actA"]}

            def hold(name, shape):
                T[name] = gla.enter_context(nc.sbuf_tensor("gla_" + name, shape, F32))

            hold("qk", [P, 2 * GH, NTOK])
            hold("r", [P, KT, NTOK])
            hold("v", [P, len(ROWS), D_MODEL])
            hold("z", [P, GH, NTOK])
            hold("as", [P, GH, NB])
            sems.recycle()
            Wg = io["gla_w_in"][0]
            phase_linear(nc, ps, cst, "gla_qk", Wg[:, 0:1024], KT, KT, xT, T["qk"], False)
            phase_linear(nc, ps, cst, "gla_r", Wg[:, 2048:3072], KT, KT, xT, T["r"], False)
            phase_gla_v_gate(nc, io, ps, xT, T, cst)
            phase_gla_core(nc, io, ps, T, cst)
            phase_gla_sample(nc, io, ps, T, cst)
            phase_gla_gate_out(nc, ps, T, cst)
            phase_linear(nc, ps, cst, "gla_out", io["gla_w_out"][0], KT, KT, T["o"], xT, True)
        sems.recycle()
        phase_layer_norm(nc, io, ps, "ln10", 1, 0, xT, cst)
        feed_forward(nc, io, ps, 1, xT, cst)
        phase_store_y(nc, io, ps, xT, cst)


_OUTS = [("y_p", (1, SEQ, D_MODEL)), ("y_s", (NB, 1, D_MODEL)),
         ("new_cmp_p", (1, 1, SEQ, 2, G, D)), ("new_slc_p", (1, 1, SEQ, 2, G, D)), ("new_win_p", (1, 1, WIN, 2, G, D)),
         ("new_gla_p", (1, 1, GH, 128, 256)),
         ("new_cmp_s", (1, NB, 1, 2, G, D)), ("new_slc_s", (1, NB, 1, 2, G, D)), ("new_win_s", (1, NB, WIN, 2, G, D)),
         ("new_gla_s", (1, NB, GH, 128, 256))]
_RENAME = {"cache_cmp_kv": "cache_cmp", "cache_slc_kv": "cache_slc", "cache_win_kv": "cache_win"}


def kernel(**inputs):
    import concourse.bacc as _bacc
    from concourse.bass_utils import run_bass_kernel_spmd as _run

    nc = _bacc.Bacc("TRN2", target_bir_lowering=False, num_devices=1)
    arrays, io = {}, {}
    data = {_RENAME.get(k, k): np.ascontiguousarray(v) for k, v in inputs.items()}
    data.update(shape_tables())
    for name, a in data.items():
        arrays["in_" + name] = a
        io[name] = nc.dram_tensor("in_" + name, a.shape, mybir.dt.from_np(a.dtype), kind="ExternalInput").ap()
    for name, shape in _OUTS:
        io[name] = nc.dram_tensor("out_" + name, shape, F32, kind="ExternalOutput").ap()
    build(nc, io)
    r = _run(nc, [arrays], core_ids=[0])
    return tuple(r.results[0]["out_" + name] for name, _ in _OUTS)
```

```python
from contextlib import ExitStack

import numpy as np

import concourse.bass as bass
from concourse import mybir

ALU = mybir.AluOpType
ACT = mybir.ActivationFunctionType
AX = mybir.AxisListType
F32 = mybir.dt.float32
F32R = mybir.dt.float32r
I32 = mybir.dt.int32
U32 = mybir.dt.uint32

P = 128
D_MODEL = 1024
KT = D_MODEL // P
SEQ = 512
TILES = SEQ // P
NB = 8
NTOK = SEQ + NB
HALF = NTOK // 2
ROWS = [P] * TILES + [NB]
PAST = 2048
PAGE = 128
PAGES = PAST // PAGE
N_POOL = 160
HEADS = 16
G = 4
R = 4
D = 64
BLK = 64
WIN = 512
NBLK = PAST // BLK + 1
N_SEL = 16
SCALE = D ** -0.5
NEG = -1e30
FORCE = 1e4
NSA_PROJ = 2608
DFF = 2816
FT = DFF // P
ALPHA = 4.0 ** 0.25
EPS = 1e-5
GH = 4
CH = 32
LOADS = 8
GLA_TAU = 16.0
VEC_B, VEC_N, VEC_Z = 32, 64, 72
VECS = VEC_Z + 4
GSCALE = 128 ** -0.5


class Chain:

    def __init__(self, eng, sem):
        self.eng, self.sem, self.n = eng, sem, 0

    def step(self, ins):
        self.n += 1
        ins.then_inc(self.sem, 1)
        self.eng.wait_ge(self.sem, self.n)


class Semaphores:

    def __init__(self, nc):
        self.nc, self.all = nc, []

    def new(self, name):
        self.all.append(self.nc.alloc_semaphore(name))
        return self.all[-1]

    def recycle(self):
        self.nc.clear_and_free_semaphores(self.all)
        self.nc.all_engine_barrier()
        self.all = []


def phase_project(nc, io, ps, S, cst):
    CW = 512
    CHUNKS = [512] * 5 + [NSA_PROJ - 5 * 512]
    NT = len(ROWS)
    UNITS = [(c, t) for c in range(len(CHUNKS)) for t in range(NT)]
    ROPE_UNITS = [i for i, (c, t) in enumerate(UNITS) if c not in (2, 5)]

    TR = [("q", t, hf) for t in range(TILES) for hf in range(2)] + \
         [("r", t, hf) for t in range(TILES) for hf in range(2)] + \
         [("k", t, br) for t in range(TILES) for br in range(2)]

    with ExitStack() as ctx:
        def sb(name, shape, dt=F32):
            return ctx.enter_context(nc.sbuf_tensor(name, shape, dt))

        def sem(name):
            return cst["sems"].new(name)

        xn = sb("xn", [P, NT, D_MODEL])
        xT = sb("xT0", [P, KT, NTOK])
        w = sb("w_in", [P, 2, KT, CW])
        qn = sb("qn", [P, NT, D_MODEL])
        qrn = sb("qrn", [P, NT, D_MODEL])
        t1 = sb("rope_t1", [P, CW])
        t2 = sb("rope_t2", [P, CW])
        rope = sb("rope_tab", [P, NT, 2, D])
        bg = sb("b_gate", [P, 48])
        gpre = sb("gpre", [P, NT, 48])

        kdup = xn[:, 0:TILES, :].rearrange("p t (a g u d) -> p t a g u d", a=2, g=G, u=2)
        qdup = w[0:NB, 0, 0:4, :].rearrange("b k n -> b (k n)").rearrange("b (h u d) -> b h u d", h=HEADS, u=2)
        qgrp = w[0:NB, 0, 4:6, :].rearrange("b k n -> b (k n)").rearrange("b (j r g d) -> b j r g d", j=2, r=R, g=2)
        kdup_done = sem("kdup_done")
        x_in, w_in = sem("x_in"), [sem("w_in0"), sem("w_in1")]
        tab_in = sem("tab_in")
        xtr_done, xT_ready = sem("xtr_done"), sem("xT_ready")
        proj_done, raw_done, rope_done = sem("proj_done"), sem("raw_done"), sem("rope_done")
        tr_done, trA, trV = sem("tr_done"), sem("tr_evac_act"), sem("tr_evac_dve")
        gate_pre, gate_done = sem("gate_pre"), sem("gate_done")
        vch, vmul, vmul2 = sem("p0_vchain"), sem("p0_vmul"), sem("p0_vmul2")
        smp_tr, smp_ev = sem("smp_tr"), sem("smp_ev")
        kv_out = sem("kv_out")

        W = io["nsa_w_in"][0].rearrange("(k p) n -> p k n", p=P)
        col = [c * CW for c in range(len(CHUNKS))]
        block = ctx.enter_context(nc.Block())

        @block.sync
        def _(sp):
            for t in range(TILES):
                sp.dma_start(xn[:, t, :], io["x_prompt"][0, t * P:(t + 1) * P, :]).then_inc(x_in, 16)
            sp.dma_start(xn[0:NB, TILES, :], io["x_sample"][:, 0, :]).then_inc(x_in, 16)
            for c, n in enumerate(CHUNKS):
                if c >= 2:
                    sp.wait_ge(proj_done, NT * (c - 1))
                sp.dma_start(w[:, c % 2, :, 0:n], W[:, :, col[c]:col[c] + n]).then_inc(w_in[c % 2], 16)
            sp.wait_ge(rope_done, len(ROPE_UNITS))
            sp.wait_ge(raw_done, len(UNITS))
            for src, name in ((S["cmpn"], "cmp"), (S["slcn"], "slc"), (S["winn"], "win")):
                o = io["new_%s_p" % name][0, 0].rearrange("(t p) a g d -> p t (a g d)", p=P)
                sp.dma_start(o, src[:, 0:TILES, :]).then_inc(kv_out, 16)
            for src, name in ((S["cmpn"], "cmp"), (S["slcn"], "slc")):
                o = io["new_%s_s" % name][0].rearrange("b t a g d -> b (t a g d)")
                sp.dma_start(o, src[0:NB, TILES, :]).then_inc(kv_out, 16)
            ow = io["new_win_s"][0].rearrange("b t a g d -> b t (a g d)")
            sp.dma_start(ow[:, WIN - 1, :], S["winn"][0:NB, TILES, :]).then_inc(kv_out, 16)
            cw = io["cache_win"][0].rearrange("b t a g d -> b (t a g d)")
            ROW = 2 * G * D
            sp.dma_start(ow.rearrange("b t n -> b (t n)")[:, 0:(WIN - 1) * ROW],
                         cw[:, ROW:WIN * ROW]).then_inc(kv_out, 16)
            sp.wait_ge(kv_out, 16 * 7)

        @block.gpsimd
        def _(pool):
            pool.dma_start(rope[:], io["rope_tab"]).then_inc(tab_in, 16)
            pool.dma_start(bg[:], io["nsa_b_gate"][0:1, :].to_broadcast([P, 48])).then_inc(tab_in, 16)
            pool.wait_ge(rope_done, len(ROPE_UNITS))
            pool.wait_ge(raw_done, len(UNITS))
            pool.wait_ge(proj_done, len(UNITS))
            for t in range(TILES):
                for br in range(2):
                    k = (S["slcn"], S["winn"])[br][:, t, 0:G * D].rearrange("p (g d) -> p g d", g=G)
                    for u in range(2):
                        ins = nc.gpsimd.tensor_copy(kdup[:, t, br, :, u, :], k)
                ins.then_inc(kdup_done, 1)
            for u in range(2):
                nc.gpsimd.tensor_copy(qdup[:, :, u, :], qn[0:NB, TILES, :].rearrange("b (h d) -> b h d", h=HEADS))
            for j in range(2):
                for gi in range(2):
                    g = 2 * j + gi
                    ins = nc.gpsimd.tensor_copy(qgrp[:, j, :, gi, :],
                                                qrn[0:NB, TILES, g * R * D:(g + 1) * R * D]
                                                .rearrange("b (r d) -> b r d", r=R))
            ins.then_inc(kdup_done, 1)

        @block.tensor
        def _(pe):
            pe.wait_ge(cst["in"], cst["n"])
            pe.wait_ge(x_in, 16 * NT)
            n = 0
            for t in range(NT):
                for hf in range(2):
                    if n >= 2:
                        pe.wait_ge(xT_ready, n - 1)
                    for k in range(4):
                        ins = nc.tensor.transpose(ps[:, n % 2, k * P:k * P + ROWS[t]],
                                                  xn[0:ROWS[t], t, (hf * 4 + k) * P:(hf * 4 + k + 1) * P],
                                                  cst["ident"][0:ROWS[t], 0:ROWS[t]])
                    ins.then_inc(xtr_done, 1)
                    n += 1
            pe.wait_ge(xT_ready, n)
            for u, (c, t) in enumerate(UNITS):
                if t == 0:
                    pe.wait_ge(w_in[c % 2], 16 * (c // 2 + 1))
                if u >= 4:
                    pe.wait_ge(raw_done, u - 3)
                m = CHUNKS[c]
                for k in range(KT):
                    ins = nc.tensor.matmul(ps[0:ROWS[t], 2 + u % 4, 0:m], xT[:, k, t * P:t * P + ROWS[t]],
                                           w[:, c % 2, k, 0:m], start=(k == 0), stop=(k == KT - 1))
                ins.then_inc(proj_done, 1)
            pe.wait_ge(rope_done, len(ROPE_UNITS))
            pe.wait_ge(raw_done, len(UNITS))
            for n, (kind, t, a) in enumerate(TR):
                if n >= 2:
                    pe.wait_ge(trA if n % 2 == 0 else trV, n // 2)
                if kind == "k" and a == 0:
                    pe.wait_ge(kdup_done, t + 1)
                for k in range(4):
                    if kind == "k":
                        src = kdup[:, t, a, k].rearrange("p u d -> p (u d)")
                    else:
                        src = (qn if kind == "q" else qrn)[:, t, (a * 4 + k) * P:(a * 4 + k + 1) * P]
                    ins = nc.tensor.transpose(ps[:, n % 2, k * P:(k + 1) * P], src, cst["ident"][:])
                ins.then_inc(tr_done, 1)
            id8 = cst["ident"][0:NB, 0:NB]
            pe.wait_ge(kdup_done, TILES + 1)
            for h in range(HEADS):
                nc.tensor.transpose(ps[:, 6, h * NB:(h + 1) * NB], qdup[:, h].rearrange("b u d -> b (u d)"), id8)
            for j in range(2):
                for r in range(R):
                    nc.tensor.transpose(ps[:, 7, (j * R + r) * NB:(j * R + r + 1) * NB],
                                        qgrp[:, j, r].rearrange("b g d -> b (g d)"), id8)
            for br in range(2):
                for j in range(2):
                    src = (S["slcn"], S["winn"])[br]
                    c = 64 + (br * 2 + j) * NB
                    ins = nc.tensor.transpose(ps[:, 7, c:c + NB], src[0:NB, TILES, j * P:(j + 1) * P], id8)
            ins.then_inc(smp_tr, 1)

        def tr_dst(n):
            kind, t, a = TR[n]
            if kind == "k":
                return S["kT"][:, a, :, t * P:(t + 1) * P]
            return (S["qT"] if kind == "q" else S["qrT"])[:, a * 4:a * 4 + 4, t * P:(t + 1) * P]

        @block.scalar
        def _(act):
            for u, (c, t) in enumerate(UNITS):
                m = ROWS[t]
                b = ps[0:m, 2 + u % 4, :]
                act.wait_ge(proj_done, u + 1)
                if c < 2:
                    ins = nc.scalar.copy(qn[0:m, t, c * CW:(c + 1) * CW], b)
                elif c == 2:
                    ins = nc.scalar.copy(S["cmpn"][0:m, t, :], b)
                elif c < 5:
                    ins = nc.scalar.copy((S["slcn"], S["winn"])[c - 3][0:m, t, :], b)
                else:
                    ins = nc.scalar.copy(gpre[0:m, t, :], b[:, 0:48])
                ins.then_inc(raw_done, 1)
            for t in range(NT):
                m = ROWS[t]
                act.wait_ge(gate_pre, t + 1)
                nc.scalar.activation(S["gates"][0:m, t, :], gpre[0:m, t, :], ACT.Sigmoid).then_inc(gate_done, 1)
            for n in range(0, len(TR), 2):
                act.wait_ge(tr_done, n + 1)
                nc.scalar.copy(tr_dst(n), ps[:, 0, :].rearrange("p (k t) -> p k t", k=4)).then_inc(trA, 1)

        @block.vector
        def _(dve):
            ch = Chain(dve, vch)
            for n in range(2 * NT):
                t, hf = n // 2, n % 2
                dve.wait_ge(xtr_done, n + 1)
                src = ps[:, n % 2, :].rearrange("p (k t) -> p k t", k=4)[:, :, 0:ROWS[t]]
                nc.vector.tensor_copy(xT[:, hf * 4:hf * 4 + 4, t * P:t * P + ROWS[t]], src).then_inc(xT_ready, 1)
            dve.wait_ge(tab_in, 32)
            roped = 0
            for u in ROPE_UNITS + [i for i, (c, t) in enumerate(UNITS) if c == 5]:
                c, t = UNITS[u]
                m = ROWS[t]
                dve.wait_ge(raw_done, u + 1)
                if c == 5:
                    nc.vector.tensor_tensor(gpre[0:m, t, :], gpre[0:m, t, :], bg[0:m, :],
                                            ALU.add).then_inc(gate_pre, 1)
                    continue
                nh = 8 if c < 2 else 4
                if c < 2:
                    v, out = (q[0:m, t, c * CW:(c + 1) * CW] for q in (qn, qrn))
                else:
                    v = out = (S["slcn"], S["winn"])[c - 3][0:m, t, 0:256]
                v = v.rearrange("p (h d) -> p h d", d=D)
                a = t1[0:m, 0:nh * D].rearrange("p (h d) -> p h d", d=D)
                b = t2[0:m, 0:nh * D].rearrange("p (h d) -> p h d", d=D)
                cos = rope[0:m, t, 0, :].unsqueeze(1).to_broadcast([m, nh, D])
                sin = rope[0:m, t, 1, :].unsqueeze(1).to_broadcast([m, nh, D])
                if roped:
                    dve.wait_ge(rope_done, roped)
                roped += 1
                nc.vector.tensor_tensor(a, v, cos, ALU.mult).then_inc(vmul, 1)
                nc.vector.tensor_tensor(b[:, :, 0:32], v[:, :, 32:64], sin[:, :, 0:32], ALU.mult).then_inc(vmul2, 1)
                dve.wait_ge(vmul2, roped)
                ch.step(nc.vector.tensor_tensor(b[:, :, 32:64], v[:, :, 0:32], sin[:, :, 32:64], ALU.mult))
                dve.wait_ge(vmul, roped)
                nc.vector.tensor_tensor(out.rearrange("p (h d) -> p h d", d=D), a, b, ALU.add).then_inc(rope_done, 1)
            for n in range(1, len(TR), 2):
                dve.wait_ge(tr_done, n + 1)
                nc.vector.tensor_copy(tr_dst(n), ps[:, 1, :].rearrange("p (k t) -> p k t", k=4)).then_inc(trV, 1)
            dve.wait_ge(smp_tr, 1)
            nc.vector.memset(S["qz"][:], 0.0).then_inc(smp_ev, 1)
            nc.vector.tensor_copy(S["qs"][:].rearrange("p b h -> p h b"),
                                  ps[:, 6, 0:P].rearrange("p (h b) -> p h b", h=HEADS))
            nc.vector.tensor_copy(S["knew"][:].rearrange("p a j b -> p (a j b)"), ps[:, 7, 64:96])
            dve.wait_ge(smp_ev, 1)
            for j in range(2):
                for gi in range(2):
                    h0 = 8 * j + 4 * gi
                    dst = S["qz"][64 * gi:64 * gi + 64, j, :, h0:h0 + 4].rearrange("p b r -> p r b")
                    nc.vector.tensor_copy(dst, ps[64 * gi:64 * gi + 64, 7, j * 32:(j + 1) * 32]
                                          .rearrange("p (r b) -> p r b", r=R))


def phase_compress(nc, io, ps, S, cst):
    QP = 32
    BY_SP, BY_ACT = 12, 10
    BY_POOL = QP - BY_SP - BY_ACT
    PARTS = NB * PAGES // QP
    EXTRA = TILES
    SLOTS = QP + EXTRA + 1
    COLS = QP * G
    XC = EXTRA * G
    NALL = NB * PAGES * G + XC
    UN = [(c, u) for c in range(2) for u in range(PARTS)]

    def cols(u):
        return COLS + (XC + 1 if u == 0 else 0)

    with ExitStack() as ctx:
        def sb(name, shape, dt=F32):
            return ctx.enter_context(nc.sbuf_tensor(name, shape, dt))

        def sem(name):
            return cst["sems"].new(name)

        rows = sb("rows", [P, 2, SLOTS, G, D])
        w1 = sb("w1", [P, D, P])
        w2 = sb("w2", [P, 2, P])
        hid = sb("hid", [P, 2, NALL])
        pe_bias = sb("pe_bias", [P, 2])
        pt = sb("pt", [1, NB * PAGES], I32)
        sig = sb("c_sig", [P, 2, cols(0)])
        pre = sb("c_pre", [P, 2, cols(0)])

        pt_in = sem("pt_in")
        rows_in = [sem("rows_in0"), sem("rows_in1")]
        rows_in_sw = [sem("rows_in_sw0"), sem("rows_in_sw1")]
        rows_in_act = [sem("rows_in_act0"), sem("rows_in_act1")]
        ex_in = sem("pe_in")
        w1_in, w1v_in, w1_zero, w2_in = sem("w1_in"), sem("w1v_in"), sem("w1_zero"), sem("w2_in")
        ex_ready, conv_done, pre_done, sig_done, hid_done = (sem(n) for n in
                                                             ("ex_ready", "conv_done", "pre_done", "sig_done", "hid_done"))
        bias_done, out_done, ck_done = sem("bias_done"), sem("cmp_out_done"), sem("ck_done")
        block = ctx.enter_context(nc.Block())
        cache = io["cache_cmp"][0].rearrange("n t a g d -> n t a (g d)")

        def rows_parts(n, count):
            return 16 * count * (n // 2 + 1)

        def load_part(eng, n, at, count, arrived):
            c, u = UN[n]
            pages = [eng.value_load(pt[0:1, u * QP + at + m:u * QP + at + m + 1], min_val=0, max_val=N_POOL - 1)
                     for m in range(count)]
            if n >= 2:
                eng.wait_ge(conv_done, n - 1)
            for m, page in enumerate(pages):
                eng.dma_start(rows[:, n % 2, at + m].rearrange("p g d -> p (g d)"),
                              cache[bass.ds(page, 1), :, c, :].rearrange("n t x -> (n t) x")).then_inc(arrived, 16)

        @block.sync
        def _(sp):
            sp.dma_start(pt[:], io["page_table"].rearrange("b p -> (b p)").unsqueeze(0)).then_inc(pt_in, 16)
            sp.wait_ge(pt_in, 16)
            for n in range(len(UN)):
                load_part(sp, n, 0, BY_SP, rows_in[n % 2])

        @block.gpsimd
        def _(pool):
            pool.wait_ge(pt_in, 16)
            for n, (c, u) in enumerate(UN):
                load_part(pool, n, BY_SP + BY_ACT, BY_POOL, rows_in_sw[n % 2])
                if u:
                    continue
                sl = rows[:, n % 2]
                for hf in range(2):
                    pool.dma_start(sl[64 * hf:64 * hf + 64, QP + EXTRA, 0, :],
                                   io["nsa_pe_cmp"][0, :, c, :]).then_inc(ex_in, 16)
                if c:
                    pool.wait_ge(conv_done, PARTS)
                    for hf in range(2):
                        o = 64 * hf
                        pool.dma_start(w1[o:o + 64, :, o:o + 64], io["nsa_w_cmp1"][0, :, 1]).then_inc(w1v_in, 16)

        @block.scalar
        def _(act):
            for hf in range(2):
                o = 64 * hf
                act.dma_start(w1[o:o + 64, :, o:o + 64], io["nsa_w_cmp1"][0, :, 0]).then_inc(w1_in, 16)
                for c in range(2):
                    act.dma_start(w2[o:o + 64, c, o:o + 64], io["nsa_w_cmp2"][0, c]).then_inc(w2_in, 16)
            act.wait_ge(pt_in, 16)
            for n in range(2):
                load_part(act, n, BY_SP, BY_ACT, rows_in_act[n % 2])
            for n in range(len(UN)):
                act.wait_ge(pre_done, n + 1)
                k = cols(UN[n][1])
                if n >= 2:
                    act.wait_ge(hid_done, n - 1)
                nc.scalar.activation(sig[:, n % 2, 0:k], pre[:, n % 2, 0:k], ACT.Sigmoid).then_inc(sig_done, 1)
                if n + 2 < len(UN):
                    load_part(act, n + 2, BY_SP, BY_ACT, rows_in_act[n % 2])

        @block.vector
        def _(dve):
            def prompt_rows(c):
                for t in range(TILES):
                    nc.vector.tensor_copy(rows[:, c * PARTS % 2, QP + t].rearrange("p g d -> p (g d)"),
                                          S["cmpn"][:, t, c * 256:(c + 1) * 256]).then_inc(ex_ready, 1)

            prompt_rows(0)
            for w in (w1, w2):
                for hf in range(2):
                    o = 64 * hf
                    nc.vector.memset(w[o:o + 64, :, 64 - o:128 - o], 0.0).then_inc(w1_zero, 1)
            for n, (c, u) in enumerate(UN):
                k = cols(u)
                dve.wait_ge(conv_done, n + 1)
                if n == PARTS - 2:
                    prompt_rows(1)
                if u == 0:
                    nc.vector.tensor_copy(pe_bias[:, c:c + 1], ps[:, n % 2, k - 1:k]).then_inc(bias_done, 1)
                    dve.wait_ge(bias_done, c + 1)
                if n >= 2:
                    dve.wait_ge(hid_done, n - 1)
                nc.vector.tensor_scalar(pre[:, n % 2, 0:k], ps[:, n % 2, 0:k], pe_bias[:, c:c + 1], None,
                                        ALU.add).then_inc(pre_done, 1)
                dve.wait_ge(sig_done, n + 1)
                dve.wait_ge(pre_done, n + 1)
                if u == 0:
                    nc.vector.tensor_tensor(hid[:, c, NALL - XC:NALL], pre[:, n % 2, COLS:COLS + XC],
                                            sig[:, n % 2, COLS:COLS + XC], ALU.mult).then_inc(out_done, 1)
                nc.vector.tensor_tensor(hid[:, c, u * COLS:(u + 1) * COLS], pre[:, n % 2, 0:COLS],
                                        sig[:, n % 2, 0:COLS], ALU.mult).then_inc(hid_done, 1)
            for c in range(2):
                dve.wait_ge(ck_done, c + 1)
                nc.vector.tensor_copy(S["ckT"][:, c, 0:NALL - XC], ps[:, 2 + c, 0:NALL - XC])
                nc.vector.tensor_copy(S["ckT"][:, c, NALL - XC:NALL], ps[:, 4 + c, 0:XC])

        @block.tensor
        def _(pe):
            for n, (c, u) in enumerate(UN):
                k = cols(u)
                if n == 0:
                    pe.wait_ge(w1_zero, 4)
                if u == 0:
                    pe.wait_ge(w1v_in if c else w1_in, 32)
                    pe.wait_ge(ex_ready, TILES * (c + 1))
                    pe.wait_ge(ex_in, 32 * (c + 1))
                pe.wait_ge(rows_in[n % 2], rows_parts(n, BY_SP))
                pe.wait_ge(rows_in_act[n % 2], rows_parts(n, BY_ACT))
                pe.wait_ge(rows_in_sw[n % 2], rows_parts(n, BY_POOL))
                if n >= 2:
                    pe.wait_ge(pre_done, n - 1)
                flat = rows[:, n % 2].rearrange("p s g d -> p d (s g)")
                for d in range(D):
                    ins = nc.tensor.matmul(ps[:, n % 2, 0:k], w1[:, d, :], flat[:, d, 0:k],
                                           start=(d == 0), stop=(d == D - 1))
                ins.then_inc(conv_done, 1)
            pe.wait_ge(w2_in, 64)
            pe.wait_ge(hid_done, len(UN))
            pe.wait_ge(out_done, 2)
            for c in range(2):
                nc.tensor.matmul(ps[:, 2 + c, 0:NALL - XC], w2[:, c, :], hid[:, c, 0:NALL - XC], start=True, stop=True)
                nc.tensor.matmul(ps[:, 4 + c, 0:XC], w2[:, c, :], hid[:, c, NALL - XC:NALL], start=True,
                                 stop=True).then_inc(ck_done, 1)


def phase_cmp_attention(nc, io, ps, S, cst):
    NP4 = TILES * HEADS
    NPB = SEQ // BLK
    COLS = NB * PAGES * G
    BY_SP = 10
    with ExitStack() as ctx:
        def sb(name, shape, dt=F32):
            return ctx.enter_context(nc.sbuf_tensor(name, shape, dt))

        def sem(name):
            return cst["sems"].new(name)

        kp = sb("kp", [P, G, NPB])
        vp = sb("vp", [TILES * G, P])
        vb = sb("vb", [P, HEADS, D])
        sp_ = sb("sp_", [P, NP4, NPB])
        mx = sb("mx_p", [P, NP4])
        sm = sb("sm_p", [P, NP4])
        pT = sb("pT_p", [P, TILES, P])
        pm = sb("pm_add", [P, TILES, NPB])
        pm01 = sb("pm_01", [P, TILES, NPB])
        ss = sb("ss", [P, 2, COLS])
        ms = sb("mask_s", [P, COLS])
        mxs, nmx, sms = sb("mxs", [P, 1]), sb("nmx", [P, 1]), sb("sms", [P, 1])
        psT = sb("psT", [P, 8, P])
        vn = sb("vn", [P, 4, P])
        os_ = sb("os_", [P, D])
        gsum = sb("gsum", [P, NB * G])
        expand = sb("expand", [NB * G, NB, HEADS])
        imp = sb("imp", [NB * G, NBLK])
        tri = sb("tri", [NB * G, NBLK, NBLK])
        gt = sb("gt", [NB * G, NBLK, NBLK])
        eq = sb("eq", [NB * G, NBLK, NBLK])
        rank = sb("rank", [NB * G, NBLK])
        sel = sb("sel", [NB * G, NBLK])

        tab, vch, vb_zero = sem("p2_tab"), sem("p2_vchain"), sem("vb_zero")
        kp_ready, s_done, e_ready, e_done, p_ready, pT_done, pT_ready, o_done, o_out = (
            sem(n) for n in ("kp_ready", "s_prompt", "shifted_prompt", "exp_prompt", "p_prompt", "pT_prompt",
                             "pT_in_sbuf", "o_prompt", "o_in_sbuf"))
        vp_done, vp_ready, vb_in = sem("vp_done"), sem("vp_ready"), sem("vb_in")
        vb_in_sw = sem("vb_in_sw")
        s2_done, s2_ready, e2_done, p2_ready, imp_done, sel_ready, selx_done = (
            sem(n) for n in ("s_sample", "max_sample", "exp_sample", "p_sample", "imp_done", "sel_ready", "selx_done"))
        pT2_done, pT2_ready, o2_done, o2_ready, osn_in = (
            sem(n) for n in ("pT_sample", "pT_sample_sbuf", "o_sample", "o_sample_sbuf", "osn_cmp_in"))
        block = ctx.enter_context(nc.Block())

        def diagonal_v(eng, heads, arrived):
            for h in heads:
                for t in range(TILES):
                    r = t * G + h // R
                    eng.dma_start(vb[h * NPB + 2 * t:h * NPB + 2 * t + 2, h, :],
                                  vp[r:r + 1, :].rearrange("r (u f) -> r u f", u=2)).then_inc(arrived, 16)

        @block.sync
        def _(sp):
            for dst, name in ((pm, "pm_add"), (pm01, "pm_01"), (ms, "mask_s"), (gsum, "gsum"), (expand, "expand"),
                              (tri, "tri")):
                sp.dma_start(dst[:], io[name + "_tab"]).then_inc(tab, 16)
            sp.wait_ge(vp_ready, 1)
            sp.wait_ge(vb_zero, 1)
            diagonal_v(sp, range(BY_SP), vb_in)
            sp.wait_ge(o2_ready, 1)
            sp.dma_start(S["osn"][:, 0, :].rearrange("b (h d) -> b h d", d=D), os_[:]).then_inc(osn_in, 16)
            sp.wait_ge(osn_in, 16)

        @block.gpsimd
        def _(pool):
            nc.gpsimd.memset(vb[:], 0.0).then_inc(vb_zero, 1)
            pool.wait_ge(vp_ready, 1)
            pool.wait_ge(vb_zero, 1)
            diagonal_v(pool, range(BY_SP, HEADS), vb_in_sw)

        @block.tensor
        def _(pe):
            for hf in range(2):
                a = slice(64 * hf, 64 * hf + 64)
                ins = nc.tensor.matmul(ps[:, 1 + hf, :], S["qs"][a].rearrange("p b h -> p (b h)"),
                                       S["ckT"][a, 0, 0:COLS], start=True, stop=True)
            ins.then_inc(s2_done, 1)
            nc.tensor.transpose(ps[0:TILES * G, 7, 0:P], S["ckT"][:, 1, COLS:COLS + TILES * G],
                                cst["ident"][:]).then_inc(vp_done, 1)
            pe.wait_ge(kp_ready, 1)
            for t in range(TILES):
                for h in range(HEADS):
                    a = slice(64 * (h % 2), 64 * (h % 2) + 64)
                    c = (t * HEADS + h) * NPB
                    ins = nc.tensor.matmul(ps[:, 3 * (h % 2), c:c + NPB], S["qT"][a, h // 2, t * P:(t + 1) * P],
                                           kp[a, h // R, :], start=True, stop=True)
            ins.then_inc(s_done, 1)
            pe.wait_ge(p2_ready, 1)
            pe.wait_ge(tab, 16 * 6)
            for hf in range(2):
                ins = nc.tensor.matmul(ps[0:NB * G, 1 + hf, :], gsum[:], ss[:, hf, :], start=True, stop=True)
            ins.then_inc(imp_done, 1)
            for hf in range(2):
                for c in range(4):
                    ins = nc.tensor.transpose(ps[:, 5 + hf, c * P:(c + 1) * P], ss[:, hf, c * P:(c + 1) * P],
                                              cst["ident"][:])
            pe.wait_ge(vp_ready, 1)
            for c in range(4):
                ins = nc.tensor.transpose(ps[:, 7, c * P:(c + 1) * P], S["ckT"][:, 1, c * P:(c + 1) * P],
                                          cst["ident"][:])
            ins.then_inc(pT2_done, 1)
            pe.wait_ge(pT2_ready, 1)
            for n in range(8):
                hf, c = n // 4, n % 4
                ins = nc.tensor.matmul(ps[:, 4, 0:D], psT[:, n, :], vn[:, c, 64 * hf:64 * hf + 64],
                                       start=(n == 0), stop=(n == 7))
            ins.then_inc(o2_done, 1)
            pe.wait_ge(p_ready, 1)
            for t in range(TILES):
                ins = nc.tensor.transpose(ps[:, 5, t * P:(t + 1) * P],
                                          sp_[:, t * HEADS:(t + 1) * HEADS, :].rearrange("p h n -> p (h n)"),
                                          cst["ident"][:])
            ins.then_inc(pT_done, 1)
            pe.wait_ge(sel_ready, 1)
            for b in range(NB):
                ins = nc.tensor.matmul(ps[0:HEADS, 2, b * NBLK:(b + 1) * NBLK], expand[:, b, :], sel[:],
                                       start=True, stop=True)
            ins.then_inc(selx_done, 1)
            pe.wait_ge(pT_ready, 1)
            pe.wait_ge(vb_in, 16 * BY_SP * TILES)
            pe.wait_ge(vb_in_sw, 16 * (HEADS - BY_SP) * TILES)
            for n in range(2 * TILES):
                t, hf = n // 2, n % 2
                bank = 6 + n % 2
                if n >= 2:
                    pe.wait_ge(o_out, n - 1)
                nc.tensor.matmul(ps[:, bank, :], pT[:, t, :],
                                 vb[:, 8 * hf:8 * hf + 8, :].rearrange("p h d -> p (h d)"),
                                 start=True, stop=True).then_inc(o_done, 1)

        @block.scalar
        def _(act):
            act.wait_ge(s2_ready, 1)
            nc.scalar.activation(ss[:], ss[:], ACT.Exp, bias=nmx[:], scale=SCALE, accum_out=sms[:]).then_inc(e2_done, 1)
            act.wait_ge(e_ready, 1)
            nc.scalar.activation(sp_[:], sp_[:], ACT.Exp, scale=SCALE).then_inc(e_done, 1)
            act.wait_ge(pT2_done, 1)
            nc.scalar.copy(psT[:, 0:4, :], ps[:, 5, :].rearrange("p (c q) -> p c q", c=4))
            nc.scalar.copy(psT[:, 4:8, :], ps[:, 6, :].rearrange("p (c q) -> p c q", c=4))
            nc.scalar.copy(vn[:], ps[:, 7, :].rearrange("p (c q) -> p c q", c=4)).then_inc(pT2_ready, 1)
            act.wait_ge(o2_done, 1)
            nc.scalar.copy(os_[:], ps[:, 4, 0:D]).then_inc(o2_ready, 1)
            act.wait_ge(pT_done, 1)
            nc.scalar.copy(pT[:], ps[:, 5, :].rearrange("p (t q) -> p t q", t=TILES)).then_inc(pT_ready, 1)
            for n in range(2 * TILES):
                act.wait_ge(o_done, n + 1)
                nc.scalar.copy(S["oacc"][:, n // 2, 512 * (n % 2):512 * (n % 2) + 512], ps[:, 6 + n % 2, :])\
                    .then_inc(o_out, 1)

        @block.vector
        def _(dve):
            ch = Chain(dve, vch)
            for dup in range(2):
                for hf in range(2):
                    src = S["ckT"][64 * hf:64 * hf + 64, 0, COLS:].rearrange("p (t g) -> p g t", g=G)
                    dst = kp[64 * dup:64 * dup + 64].rearrange("p g (t u) -> p g t u", u=2)[:, :, :, hf]
                    ins = nc.vector.tensor_copy(dst, src)
                    if dup == 0 or hf == 0:
                        ch.step(ins)
            ins.then_inc(kp_ready, 1)
            dve.wait_ge(vp_done, 1)
            nc.vector.tensor_copy(vp[:], ps[0:TILES * G, 7, 0:P]).then_inc(vp_ready, 1)
            dve.wait_ge(tab, 16 * 6)
            dve.wait_ge(s2_done, 1)
            for hf in range(2):
                ch.step(nc.vector.tensor_tensor(ss[:, hf, :], ps[:, 1 + hf, :], ms[:], ALU.add))
            ch.step(nc.vector.tensor_reduce(mxs[:], ss[:].rearrange("p a c -> p (a c)"), AX.X, ALU.max))
            nc.vector.tensor_scalar(nmx[:], mxs[:], -SCALE, None, ALU.mult).then_inc(s2_ready, 1)
            dve.wait_ge(e2_done, 1)
            ch.step(nc.vector.reciprocal(sms[:], sms[:]))
            nc.vector.tensor_scalar(ss[:], ss[:], sms[:], None, ALU.mult).then_inc(p2_ready, 1)
            dve.wait_ge(s_done, 1)
            s4 = sp_[:].rearrange("p (t h) n -> p t h n", t=TILES)
            for t in range(TILES):
                for par in range(2):
                    src = ps[:, 3 * par, t * P:(t + 1) * P].rearrange("p (h u n) -> p h u n", u=2, n=NPB)[:, :, par]
                    ch.step(nc.vector.tensor_tensor(s4[:, t].rearrange("p (h u) n -> p h u n", u=2)[:, :, par], src,
                                                    pm[:, t, :].unsqueeze(1).to_broadcast([P, HEADS // 2, NPB]),
                                                    ALU.add))
            ch.step(nc.vector.tensor_reduce(mx[:], sp_[:], AX.X, ALU.max))
            nc.vector.tensor_tensor(sp_[:], sp_[:], mx[:].unsqueeze(2).to_broadcast([P, NP4, NPB]),
                                    ALU.subtract).then_inc(e_ready, 1)
            dve.wait_ge(e_done, 1)
            for t in range(TILES):
                ch.step(nc.vector.tensor_tensor(s4[:, t], s4[:, t],
                                                pm01[:, t, :].unsqueeze(1).to_broadcast([P, HEADS, NPB]), ALU.mult))
            ch.step(nc.vector.tensor_reduce(sm[:], sp_[:], AX.X, ALU.add))
            ch.step(nc.vector.tensor_scalar(sm[:], sm[:], 1e-30, None, ALU.max))
            ch.step(nc.vector.reciprocal(sm[:], sm[:]))
            ch.step(nc.vector.tensor_tensor(sm[:].rearrange("p (t h) -> p t h", t=TILES),
                                            sm[:].rearrange("p (t h) -> p t h", t=TILES),
                                            S["gates"][:, 0:TILES, 0:HEADS], ALU.mult))
            nc.vector.tensor_tensor(sp_[:], sp_[:], sm[:].unsqueeze(2).to_broadcast([P, NP4, NPB]),
                                    ALU.mult).then_inc(p_ready, 1)
            dve.wait_ge(imp_done, 1)
            iv = imp[:, 0:NBLK - 1].rearrange("q (p u) -> q p u", u=2)
            for hf in range(2):
                ch.step(nc.vector.tensor_reduce(iv[:, :, hf], ps[0:NB * G, 1 + hf, :]
                                                .rearrange("q (b p g) -> q p b g", b=NB, g=G), AX.XY, ALU.add))
            ch.step(nc.vector.memset(imp[:, NBLK - 2:NBLK], FORCE))
            ch.step(nc.vector.memset(imp[:, 0:1], FORCE))
            a = imp[:].unsqueeze(1).to_broadcast([NB * G, NBLK, NBLK])
            b = imp[:].unsqueeze(2).to_broadcast([NB * G, NBLK, NBLK])
            ch.step(nc.vector.tensor_tensor(gt[:], a, b, ALU.is_gt))
            ch.step(nc.vector.tensor_tensor(eq[:], a, b, ALU.is_equal))
            ch.step(nc.vector.tensor_tensor(eq[:], eq[:], tri[:], ALU.mult))
            ch.step(nc.vector.tensor_tensor(gt[:], gt[:], eq[:], ALU.add))
            ch.step(nc.vector.tensor_reduce(rank[:], gt[:], AX.X, ALU.add))
            nc.vector.tensor_scalar(sel[:], rank[:], N_SEL - 0.5, None, ALU.is_lt).then_inc(sel_ready, 1)
            dve.wait_ge(selx_done, 1)
            nc.vector.tensor_scalar(S["selneg"][:].rearrange("h b n -> h (b n)"), ps[0:HEADS, 2, 0:NB * NBLK],
                                    -1.0, -NEG, ALU.add, ALU.mult)


def phase_sample_attention(nc, io, ps, S, cst):
    WP = WIN // PAGE
    NPG = PAGES + WP
    GRP = NPG // 4
    NS, NW = PAST + 1, WIN + 1
    KEYS = NS + NW
    with ExitStack() as ctx:
        def sb(name, shape, dt=F32):
            return ctx.enter_context(nc.sbuf_tensor(name, shape, dt))

        def sem(name):
            return cst["sems"].new(name)

        kv = sb("kv", [P, 2, NPG, 2 * G * D])
        dead = S["cmpn"][:].rearrange("p t n -> p (t n)")
        kTs = dead[:, 0:2048].rearrange("p (s j n) -> p s j n", s=2, j=2)
        pt = sb("pt3", [1, NB * PAGES], I32)
        sc = S["actA"][0:HEADS].rearrange("h k n -> h (k n)")[:, 0:KEYS]
        pTs = dead[:, 2048:2048 + (NPG + 2) * HEADS].rearrange("p (n h) -> p n h", h=HEADS)
        vnew = sb("vnew", [1, 2, 2, G * D])
        gm = sb("gmask", [HEADS, G])
        mx, nmx, sm = sb("mx3", [HEADS, 2]), sb("nmx3", [HEADS, 2]), sb("sm3", [HEADS, NB, 2])
        og = sb("og", [HEADS, 2, G, D])
        ob = S["ckT"][0:HEADS].rearrange("h a n -> h (a n)")[:, 0:2 * NB * D].rearrange("h (a b d) -> h a b d", a=2,
                                                                                       b=NB)

        pt_in, vn_in, gm_in = sem("pt3_in"), [sem("vnew_in0"), sem("vnew_in1")], sem("gmask_in")
        kv_in_sw = [sem("kv_in_sw0"), sem("kv_in_sw1")]
        kv_in, wkv_in = [sem("kv_in0"), sem("kv_in1")], [sem("wkv_in0"), sem("wkv_in1")]
        ktr_done, kT_a, kT_v = sem("ktr_done"), sem("kT_evac_act"), sem("kT_evac_dve")
        sc_done, sc_out, new_done = sem("sc_done"), sem("sc_out"), sem("sc_new_done")
        mx_ready, exp_done, pT_done, pT_out, pv_done, og_done = (
            sem(n) for n in ("mx_ready3", "exp_done3", "pT_done3", "pT_out3", "pv_done3", "og_done3"))
        vch, ob_ready, osn_in = sem("p3_vchain"), sem("ob_ready"), sem("osn_in")
        block = ctx.enter_context(nc.Block())
        cache = io["cache_slc"][0].rearrange("n t a g d -> n t (a g d)")
        wcache = io["cache_win"][0].rearrange("b (w p) a g d -> b p w (a g d)", p=P)

        def key0(i):
            return i * PAGE if i < PAGES else NS + (i - PAGES) * PAGE

        def load_pages(eng, b, at, arrived):
            pages = [eng.value_load(pt[0:1, b * PAGES + at + m:b * PAGES + at + m + 1], min_val=0,
                                    max_val=N_POOL - 1) for m in range(PAGES // 2)]
            if b >= 2:
                eng.wait_ge(pv_done, b - 1)
            for m, page in enumerate(pages):
                eng.dma_start(kv[:, b % 2, at + m, :], cache[bass.ds(page, 1)].rearrange("n t x -> (n t) x"))\
                    .then_inc(arrived, 16)

        @block.gpsimd
        def _(pool):
            pool.wait_ge(pt_in, 16)
            for b in range(NB):
                load_pages(pool, b, PAGES // 2, kv_in_sw[b % 2])

        @block.sync
        def _(sp):
            sp.dma_start(pt[:], io["page_table"].rearrange("b p -> (b p)").unsqueeze(0)).then_inc(pt_in, 16)
            sp.dma_start(gm[:], io["gmask_tab"]).then_inc(gm_in, 16)
            sp.wait_ge(pt_in, 16)
            for b in range(NB):
                load_pages(sp, b, 0, kv_in[b % 2])
                for br, src in enumerate((S["slcn"], S["winn"])):
                    sp.dma_start(vnew[:, b % 2, br, :], src[b:b + 1, TILES, G * D:]).then_inc(vn_in[b % 2], 16)
                sp.dma_start(kv[:, b % 2, PAGES:NPG, :], wcache[b]).then_inc(wkv_in[b % 2], 16)
            sp.wait_ge(ob_ready, 2 * NB)
            for br in range(2):
                for b in range(NB):
                    sp.dma_start(S["osn"][b:b + 1, 1 + br, :].rearrange("b (h d) -> b h d", d=D),
                                 ob[:, br, b, :]).then_inc(osn_in, 16)
            sp.wait_ge(osn_in, 16 * 2 * NB)

        def scores(pe, n):
            b, g = n // GRP, n % GRP
            pe.wait_ge(kT_a, n + 1)
            pe.wait_ge(kT_v, n + 1)
            if n >= 2:
                pe.wait_ge(sc_out, n - 1)
            for j in range(2):
                ins = nc.tensor.matmul(ps[0:HEADS, 4 + n % 2, :], S["qz"][:, j, b, :], kTs[:, n % 2, j, :],
                                       start=(j == 0), stop=(j == 1))
            ins.then_inc(sc_done, 1)
            if g == GRP - 1:
                if b >= 1:
                    pe.wait_ge(og_done, 2 * b)
                for br in range(2):
                    for j in range(2):
                        ins = nc.tensor.matmul(ps[0:HEADS, 7, br:br + 1], S["qz"][:, j, b, :],
                                               S["knew"][:, br, j, b:b + 1], start=(j == 0), stop=(j == 1))
                ins.then_inc(new_done, 1)

        def finish(pe, b):
            pe.wait_ge(exp_done, 2 * (b + 1))
            if b >= 1:
                pe.wait_ge(pT_out, b)
            idh = cst["ident"][0:HEADS, 0:HEADS]
            for i in range(NPG):
                nc.tensor.transpose(ps[:, 6, i * HEADS:(i + 1) * HEADS], sc[:, key0(i):key0(i) + PAGE], idh)
            for br in range(2):
                last = (NS if br == 0 else KEYS) - 1
                c = (NPG + br) * HEADS
                ins = nc.tensor.transpose(ps[0:1, 6, c:c + HEADS], sc[:, last:last + 1], idh)
            ins.then_inc(pT_done, 1)
            pe.wait_ge(pT_out, b + 1)
            pe.wait_ge(mx_ready, 2 * (b + 1))
            pe.wait_ge(vn_in[b % 2], 32 * (b // 2 + 1))
            for br in range(2):
                pages = range(PAGES) if br == 0 else range(PAGES, NPG)
                for i in pages:
                    nc.tensor.matmul(ps[0:HEADS, 7, br * 256:br * 256 + 256], pTs[:, i, :],
                                     kv[:, b % 2, i, 256:512], start=(i == pages[0]), stop=False)
                ins = nc.tensor.matmul(ps[0:HEADS, 7, br * 256:br * 256 + 256], pTs[0:1, NPG + br, :],
                                       vnew[0:1, b % 2, br, :], start=False, stop=True)
            ins.then_inc(pv_done, 1)

        @block.tensor
        def _(pe):
            for b in range(NB):
                for g in range(GRP):
                    n = b * GRP + g
                    if g == 0:
                        pe.wait_ge(kv_in[b % 2], 16 * (PAGES // 2) * (b // 2 + 1))
                    if g == GRP - 1:
                        pe.wait_ge(wkv_in[b % 2], 16 * (b // 2 + 1))
                    if g == 2:
                        pe.wait_ge(kv_in_sw[b % 2], 16 * (PAGES // 2) * (b // 2 + 1))
                    if n >= 2:
                        pe.wait_ge(kT_a, n - 1)
                        pe.wait_ge(kT_v, n - 1)
                    for j in range(2):
                        for i in range(4):
                            ins = nc.tensor.transpose(ps[:, 2 * (n % 2) + j, i * P:(i + 1) * P],
                                                      kv[:, b % 2, 4 * g + i, j * P:(j + 1) * P], cst["ident"][:])
                    ins.then_inc(ktr_done, 1)
                    if n >= 1:
                        scores(pe, n - 1)
                    if g == 1 and b >= 1:
                        finish(pe, b - 1)
            scores(pe, NB * GRP - 1)
            finish(pe, NB - 1)

        @block.scalar
        def _(act):
            for n in range(NB * GRP + 1):
                if n < NB * GRP:
                    act.wait_ge(ktr_done, n + 1)
                    if n >= 2:
                        act.wait_ge(sc_done, n - 1)
                    nc.scalar.copy(kTs[:, n % 2, 0, :], ps[:, 2 * (n % 2), :]).then_inc(kT_a, 1)
                if n >= GRP and n % GRP == 0:
                    b = n // GRP - 1
                    for br, a, z in ((0, 0, NS), (1, NS, KEYS)):
                        act.wait_ge(mx_ready, 2 * b + br + 1)
                        nc.scalar.activation(sc[:, a:z], sc[:, a:z], ACT.Exp, bias=nmx[:, br:br + 1], scale=SCALE,
                                             accum_out=sm[:, b, br:br + 1]).then_inc(exp_done, 1)

        @block.vector
        def _(dve):
            ch = Chain(dve, vch)

            def evac(n):
                dve.wait_ge(ktr_done, n + 1)
                if n >= 2:
                    dve.wait_ge(sc_done, n - 1)
                nc.vector.tensor_copy(kTs[:, n % 2, 1, :], ps[:, 2 * (n % 2) + 1, :]).then_inc(kT_v, 1)

            def take(n):
                b, g = n // GRP, n % GRP
                dve.wait_ge(sc_done, n + 1)
                if g == 0 and b >= 1:
                    dve.wait_ge(pT_done, b)
                src = ps[0:HEADS, 4 + n % 2, :]
                if g < GRP - 1:
                    m = S["selneg"][:, b, 8 * g:8 * g + 8].unsqueeze(2).to_broadcast([HEADS, 8, BLK])
                    nc.vector.tensor_tensor(sc[:, g * 512:(g + 1) * 512].rearrange("h (n l) -> h n l", l=BLK),
                                            src.rearrange("h (n l) -> h n l", l=BLK), m, ALU.add).then_inc(sc_out, 1)
                else:
                    nc.vector.tensor_copy(sc[:, NS:NS + WIN], src).then_inc(sc_out, 1)
                    dve.wait_ge(new_done, b + 1)
                    ch.step(nc.vector.tensor_copy(sc[:, NS - 1:NS], ps[0:HEADS, 7, 0:1]))
                    ch.step(nc.vector.tensor_copy(sc[:, KEYS - 1:KEYS], ps[0:HEADS, 7, 1:2]))
                    dve.wait_ge(sc_out, n + 1)
                    for br, a, z in ((0, 0, NS), (1, NS, KEYS)):
                        ch.step(nc.vector.tensor_reduce(mx[:, br:br + 1], sc[:, a:z], AX.X, ALU.max))
                        if b >= 1:
                            dve.wait_ge(exp_done, 2 * b)
                        nc.vector.tensor_scalar(nmx[:, br:br + 1], mx[:, br:br + 1], -SCALE, None,
                                                ALU.mult).then_inc(mx_ready, 1)

            def take_pT(b):
                dve.wait_ge(pT_done, b + 1)
                if b >= 1:
                    dve.wait_ge(pv_done, b)
                nc.vector.tensor_copy(pTs[:, 0:NPG, :].rearrange("p n h -> p (n h)"), ps[:, 6, 0:NPG * HEADS])
                nc.vector.tensor_copy(pTs[0:1, NPG:NPG + 2, :].rearrange("p n h -> p (n h)"),
                                      ps[0:1, 6, NPG * HEADS:(NPG + 2) * HEADS]).then_inc(pT_out, 1)

            def take_o(b):
                dve.wait_ge(pv_done, b + 1)
                ch.step(nc.vector.reciprocal(sm[:, b, :], sm[:, b, :]))
                for br in range(2):
                    nc.vector.tensor_tensor(og[:, br], ps[0:HEADS, 7, br * 256:br * 256 + 256]
                                            .rearrange("h (g d) -> h g d", g=G),
                                            gm[:].unsqueeze(2).to_broadcast([HEADS, G, D]), ALU.mult)\
                        .then_inc(og_done, 1)
                    dve.wait_ge(og_done, 2 * b + br + 1)
                    ch.step(nc.vector.tensor_reduce(ob[:, br, b, :], og[:, br].rearrange("h g d -> h d g"), AX.X,
                                                    ALU.add))
                    nc.vector.tensor_scalar(ob[:, br, b, :], ob[:, br, b, :], sm[:, b, br:br + 1], None,
                                            ALU.mult).then_inc(ob_ready, 1)

            dve.wait_ge(gm_in, 16)
            for n in range(NB * GRP + 1):
                if n < NB * GRP:
                    evac(n)
                if n % GRP == 1 and n > GRP:
                    take_pT(n // GRP - 1)
                if n >= 1:
                    take(n - 1)
                if n % GRP == 3 and n > GRP:
                    take_o(n // GRP - 1)
            take_pT(NB - 1)
            take_o(NB - 1)


def phase_prompt_attention(nc, io, ps, S, cst):
    assert SEQ // BLK <= N_SEL and SEQ <= WIN
    UN = [(br, t, p) for br in range(2) for p in range(HEADS // 2) for t in (3, 0, 2, 1)]
    U = len(UN)
    with ExitStack() as ctx:
        def sb(name, shape, dt=F32):
            return ctx.enter_context(nc.sbuf_tensor(name, shape, dt))

        def sem(name):
            return cst["sems"].new(name)

        e = sb("e4", [P, 4, 2, 512])
        pT = sb("pT4", [P, 2, 2, 512])
        causal = sb("causal", [P, P])
        qh = sb("qh4", [P, 4, 2, P])
        mx, nmx, sm, rg = (sb(n, [P, 4, 2]) for n in ("mx4", "nmx4", "sm4", "rg4"))
        tab, qh_zero, qh_ready = sem("causal_in"), sem("qh_zero"), sem("qh_ready")
        qk_done, masked, maxed, nmx_ready, exp_done, tp_done, pT_a, pT_v, pv_done, recip, rg_ready, o_done = (
            sem(n) for n in ("qk_done4", "masked4", "maxed4", "nmx_ready4", "exp_done4", "tp_done4", "pT_act4",
                             "pT_dve4", "pv_done4", "recip4", "rg_ready4", "o_done4"))
        block = ctx.enter_context(nc.Block())

        @block.sync
        def _(sp):
            sp.dma_start(causal[:], io["causal_tab"]).then_inc(tab, 16)

        @block.gpsimd
        def _(pool):
            nc.gpsimd.memset(qh[:], 0.0).then_inc(qh_zero, 1)
            pool.wait_ge(qh_zero, 1)
            for n in range(U):
                br, t, p = UN[n]
                if n >= 4:
                    pool.wait_ge(qk_done, 2 * (n - 3))
                for s in range(2):
                    a = slice(64 * s, 64 * s + 64)
                    nc.gpsimd.tensor_copy(qh[a, n % 4, s, :], S["qrT"][a, p, t * P:(t + 1) * P]).then_inc(qh_ready, 1)

        @block.tensor
        def _(pe):
            def qk(n):
                br, t, p = UN[n]
                w = (t + 1) * P
                if n >= 2:
                    pe.wait_ge(exp_done, 2 * (n - 1))
                pe.wait_ge(qh_ready, 2 * (n + 1))
                for s in range(2):
                    nc.tensor.matmul(ps[:, 2 * (n % 2) + s, 0:w], qh[:, n % 4, s, :], S["kT"][:, br, p // 2, 0:w],
                                     start=True, stop=True).then_inc(qk_done, 1)

            def turn(n):
                t = UN[n][1]
                pe.wait_ge(exp_done, 2 * (n + 1))
                if n >= 1:
                    pe.wait_ge(pT_a, n)
                    pe.wait_ge(pT_v, n)
                for s in range(2):
                    for k in range(t + 1):
                        ins = nc.tensor.transpose(ps[:, 4 + s, k * P:(k + 1) * P], e[:, n % 4, s, k * P:(k + 1) * P],
                                                  cst["ident"][:])
                ins.then_inc(tp_done, 1)

            def pv(n):
                br, t, p = UN[n]
                pe.wait_ge(pT_a, n + 1)
                pe.wait_ge(pT_v, n + 1)
                if n >= 2:
                    pe.wait_ge(o_done, 2 * (n - 1))
                v = (S["slcn"], S["winn"])[br]
                c = G * D + (p // 2) * D
                for s in range(2):
                    for k in range(t + 1):
                        ins = nc.tensor.matmul(ps[:, 6 + n % 2, s * D:(s + 1) * D], pT[:, n % 2, s, k * P:(k + 1) * P],
                                               v[:, k, c:c + D], start=(k == 0), stop=(k == t))
                ins.then_inc(pv_done, 1)

            for n in range(U + 3):
                if n < U:
                    qk(n)
                if 2 <= n < U + 2:
                    turn(n - 2)
                if n >= 3:
                    pv(n - 3)

        @block.scalar
        def _(act):
            for n in range(U + 2):
                if n >= 2:
                    m = n - 2
                    w = (UN[m][1] + 1) * P
                    act.wait_ge(tp_done, m + 1)
                    if m >= 2:
                        act.wait_ge(pv_done, m - 1)
                    nc.scalar.copy(pT[:, m % 2, 0, 0:w], ps[:, 4, 0:w]).then_inc(pT_a, 1)
                if n < U:
                    w = (UN[n][1] + 1) * P
                    act.wait_ge(nmx_ready, n + 1)
                    if n >= 4:
                        act.wait_ge(tp_done, n - 3)
                        act.wait_ge(rg_ready, n - 3)
                    for s in range(2):
                        nc.scalar.activation(e[:, n % 4, s, 0:w], ps[:, 2 * (n % 2) + s, 0:w], ACT.Exp,
                                             bias=nmx[:, n % 4, s:s + 1], scale=SCALE,
                                             accum_out=sm[:, n % 4, s:s + 1]).then_inc(exp_done, 1)

        @block.vector
        def _(dve):
            def stats(n):
                t = UN[n][1]
                w = (t + 1) * P
                dve.wait_ge(qk_done, 2 * (n + 1))
                sc = ps[:, 2 * (n % 2):2 * (n % 2) + 2, 0:w]
                m = causal[:].unsqueeze(1).to_broadcast([P, 2, P])
                nc.vector.tensor_tensor(sc[:, :, t * P:w], sc[:, :, t * P:w], m, ALU.add).then_inc(masked, 1)
                dve.wait_ge(masked, n + 1)
                nc.vector.tensor_reduce(mx[:, n % 4], sc, AX.X, ALU.max).then_inc(maxed, 1)
                dve.wait_ge(maxed, n + 1)
                if n >= 4:
                    dve.wait_ge(exp_done, 2 * (n - 3))
                nc.vector.tensor_scalar(nmx[:, n % 4], mx[:, n % 4], -SCALE, None, ALU.mult).then_inc(nmx_ready, 1)

            def copy(n):
                w = (UN[n][1] + 1) * P
                dve.wait_ge(tp_done, n + 1)
                if n >= 2:
                    dve.wait_ge(pv_done, n - 1)
                nc.vector.tensor_copy(pT[:, n % 2, 1, 0:w], ps[:, 5, 0:w]).then_inc(pT_v, 1)

            def gate(n):
                br, t, p = UN[n]
                dve.wait_ge(exp_done, 2 * (n + 1))
                if n >= 4:
                    dve.wait_ge(o_done, 2 * (n - 3))
                nc.vector.reciprocal(rg[:, n % 4], sm[:, n % 4]).then_inc(recip, 1)
                dve.wait_ge(recip, n + 1)
                c = (1 + br) * HEADS + 2 * p
                nc.vector.tensor_tensor(rg[:, n % 4], rg[:, n % 4], S["gates"][:, t, c:c + 2],
                                        ALU.mult).then_inc(rg_ready, 1)

            def add(n):
                br, t, p = UN[n]
                dve.wait_ge(pv_done, n + 1)
                dve.wait_ge(rg_ready, n + 1)
                for s in range(2):
                    o = S["oacc"][:, t, (2 * p + s) * D:(2 * p + s + 1) * D]
                    nc.vector.scalar_tensor_tensor(out=o, in0=ps[:, 6 + n % 2, s * D:(s + 1) * D],
                                                   scalar=rg[:, n % 4, s:s + 1], in1=o, op0=ALU.mult,
                                                   op1=ALU.add).then_inc(o_done, 1)

            dve.wait_ge(tab, 16)
            for n in range(U + 4):
                if n < U:
                    stats(n)
                if 2 <= n < U + 2:
                    copy(n - 2)
                    gate(n - 2)
                if n >= 4:
                    if n == 4 + U // 2:
                        dve.wait_ge(o_done, U)
                    add(n - 4)


def phase_attention_out(nc, io, ps, S, cst):
    NT = len(ROWS)
    with ExitStack() as ctx:
        def sem(name):
            return cst["sems"].new(name)

        og = ctx.enter_context(nc.sbuf_tensor("os_gated", [NB, 3, D_MODEL], F32))
        os_ = ctx.enter_context(nc.sbuf_tensor("os_sum", [NB, D_MODEL], F32))
        vch, os_ready, tr_done, tr_out = sem("p5_vchain"), sem("os_ready"), sem("otr_done"), sem("otr_out")
        block = ctx.enter_context(nc.Block())

        @block.tensor
        def _(pe):
            pe.wait_ge(os_ready, 1)
            for n in range(2 * NT):
                t, hf = n // 2, n % 2
                if n >= 4:
                    pe.wait_ge(tr_out, n - 3)
                for k in range(4 * hf, 4 * hf + 4):
                    src = S["oacc"][:, t] if t < TILES else os_[:]
                    ins = nc.tensor.transpose(ps[:, n % 4, (k % 4) * P:(k % 4) * P + ROWS[t]],
                                              src[:, k * P:(k + 1) * P], cst["ident"][0:ROWS[t], 0:ROWS[t]])
                ins.then_inc(tr_done, 1)

        @block.vector
        def _(dve):
            ch = Chain(dve, vch)
            for br in range(3):
                g = S["gates"][0:NB, TILES, br * HEADS:(br + 1) * HEADS].unsqueeze(2).to_broadcast([NB, HEADS, D])
                ch.step(nc.vector.tensor_tensor(og[:, br].rearrange("b (h d) -> b h d", d=D),
                                                S["osn"][:, br].rearrange("b (h d) -> b h d", d=D), g, ALU.mult))
            ch.step(nc.vector.tensor_tensor(os_[:], og[:, 0], og[:, 1], ALU.add))
            nc.vector.tensor_tensor(os_[:], os_[:], og[:, 2], ALU.add).then_inc(os_ready, 1)
            for n in range(2 * NT):
                t, hf = n // 2, n % 2
                dve.wait_ge(tr_done, n + 1)
                nc.vector.tensor_copy(S["actA"][:, 4 * hf:4 * hf + 4, t * P:t * P + ROWS[t]],
                                      ps[:, n % 4].rearrange("p (k t) -> p k t", k=4)[:, :, 0:ROWS[t]])\
                    .then_inc(tr_out, 1)


def phase_residual_in(nc, io, ps, xT, attn, X, cst):
    NT = len(ROWS)
    with ExitStack() as ctx:
        def sem(name):
            return cst["sems"].new(name)

        xn = ctx.enter_context(nc.sbuf_tensor("xn5", [P, NT, D_MODEL], F32))
        x_in, tr_done, tr_out = sem("x_in5"), sem("xtr_done5"), sem("xtr_out5")
        high_done = sem("attn_high")
        block = ctx.enter_context(nc.Block())

        @block.sync
        def _(sp):
            sp.dma_start(xn[:, 0:TILES, :], io["x_prompt"][0].rearrange("(t p) n -> p t n", p=P)).then_inc(x_in, 16)
            sp.dma_start(xn[0:NB, TILES, :], io["x_sample"][:, 0, :]).then_inc(x_in, 16)

        @block.tensor
        def _(pe):
            pe.wait_ge(x_in, 32)
            for n in range(2 * NT):
                t, hf = n // 2, n % 2
                if n >= 4:
                    pe.wait_ge(tr_out, n - 3)
                for k in range(4 * hf, 4 * hf + 4):
                    ins = nc.tensor.transpose(ps[:, n % 4, (k % 4) * P:(k % 4) * P + ROWS[t]],
                                              xn[0:ROWS[t], t, k * P:(k + 1) * P],
                                              cst["ident"][0:ROWS[t], 0:ROWS[t]])
                ins.then_inc(tr_done, 1)

        @block.scalar
        def _(act):
            nc.scalar.copy(X[0][:], attn[:]).then_inc(high_done, 1)

        @block.vector
        def _(dve):
            dve.wait_ge(high_done, 1)
            nc.vector.tensor_tensor(X[1][:], attn[:], X[0][:].bitcast(F32), ALU.subtract)
            for n in range(2 * NT):
                t, hf = n // 2, n % 2
                dve.wait_ge(tr_done, n + 1)
                nc.vector.tensor_copy(xT[:, 4 * hf:4 * hf + 4, t * P:t * P + ROWS[t]],
                                      ps[:, n % 4].rearrange("p (k t) -> p k t", k=4)[:, :, 0:ROWS[t]])\
                    .then_inc(tr_out, 1)


def split_pipeline(nc, cst, ctx, name, W, mt, parts, kc, src, units):
    per = 2 * parts
    use = per // 2

    def sb(n, dt):
        return ctx.enter_context(nc.sbuf_tensor(n + "_" + name, [P, 2, kc, P], dt))

    raw, high, low = sb("w", F32), sb("w_high", F32R), sb("w_low", F32R)
    w_in, split, mm_done = ([cst["sems"].new("%s%d_%s" % (n, s, name)) for s in range(2)]
                            for n in ("w_in", "w_split", "mm_done"))
    high_done = [cst["sems"].new("w_high%d_%s" % (s, name)) for s in range(2)]
    Wv = W.rearrange("(k p) n -> p k n", p=P)

    def load(sp, i):
        for q in range(per):
            s, n = q % 2, i * use + q // 2
            col, k0 = units(i, q)
            sp.wait_ge(split[s], n + 1)
            sp.dma_start(raw[:, s], Wv[:, k0:k0 + kc, bass.ds(col, P)]).then_inc(w_in[s], 16)

    def round_high(act, s, n):
        act.wait_ge(mm_done[s], n + 1)
        act.wait_ge(w_in[s], 16 * n + 16)
        nc.scalar.copy(high[:, s], raw[:, s]).then_inc(high_done[s], 1)

    def take_low(pool, i):
        for q in range(per):
            s, n = q % 2, i * use + q // 2
            pool.wait_ge(high_done[s], n + 1)
            nc.gpsimd.tensor_tensor(low[:, s], raw[:, s], high[:, s].bitcast(F32), ALU.subtract).then_inc(split[s], 1)

    def multiply(pe, i, q, bank, first, last):
        s, n = q % 2, i * use + q // 2
        k0 = units(0, q)[1]
        pe.wait_ge(split[s], n + 2)
        for hf in range(2):
            cols = slice(hf * HALF, (hf + 1) * HALF)
            for k in range(kc):
                terms = ((high, src[0]), (high, src[1]), (low, src[0]))
                for j, (a, x) in enumerate(terms):
                    ins = nc.tensor.matmul(cst["ps"][:, bank + hf, 0:HALF], a[:, s, k, :], x[:, k0 + k, cols],
                                           start=first and k == 0 and j == 0, stop=last and k == kc - 1 and j == 2)
        ins.then_inc(mm_done[s], 1)

    return load, round_high, take_low, multiply, split, mm_done


def phase_linear(nc, ps, cst, name, W, kt, mt, src, dst, residual):
    parts = 1 if kt == KT else 2
    kc = kt // parts
    with ExitStack() as ctx:
        load, round_high, take_low, multiply, split, mm_done = split_pipeline(
            nc, cst, ctx, name, W, mt, parts, kc, src, lambda i, q: ((2 * i + q // parts) * P, (q % parts) * kc))
        out_done = [cst["sems"].new("out_done%d_%s" % (s, name)) for s in range(2)]
        block = ctx.enter_context(nc.Block())

        @block.sync
        def _(sp):
            with sp.Fori(0, mt // 2) as i:
                load(sp, i)

        @block.gpsimd
        def _(pool):
            for s in range(2):
                pool.sem_inc(split[s], 1)
            with pool.Fori(0, mt // 2) as i:
                take_low(pool, i)

        @block.scalar
        def _(act):
            with act.Fori(0, mt // 2) as i:
                for q in range(2 * parts):
                    round_high(act, q % 2, i * parts + q // 2)

        @block.tensor
        def _(pe):
            for s in range(2):
                pe.sem_inc(mm_done[s], 1)
            with pe.Fori(0, mt // 2) as i:
                for q in range(2 * parts):
                    m = q // parts
                    if q % parts == 0:
                        pe.wait_ge(out_done[m], i + 1)
                    multiply(pe, i, q, 2 * m, q % parts == 0, q % parts == parts - 1)

        @block.vector
        def _(dve):
            for m in range(2):
                dve.sem_inc(out_done[m], 1)
            with dve.Fori(0, mt // 2) as i:
                for m in range(2):
                    if parts == 1:
                        dve.wait_ge(mm_done[m], i + 2)
                    else:
                        dve.wait_ge(mm_done[1], 2 * i + m + 2)
                    y = ps[:, 2 * m:2 * m + 2, 0:HALF]
                    d = dst[:, bass.ds(2 * i + m, 1), :].rearrange("p a (f n) -> p (a f) n", f=2)
                    if residual:
                        ins = nc.vector.scalar_tensor_tensor(out=d, in0=d, scalar=ALPHA, in1=y, op0=ALU.mult,
                                                             op1=ALU.add)
                    else:
                        ins = nc.vector.tensor_copy(d, y)
                    ins.then_inc(out_done[m], 1)


def phase_gate_up(nc, ps, cst, name, W, src, dst):
    with ExitStack() as ctx:
        def sb(n):
            return ctx.enter_context(nc.sbuf_tensor(n + "_" + name, [P, 2, 2, HALF], F32))

        sg, h = sb("silu"), sb("h")
        load, round_high, take_low, multiply, split, mm_done = split_pipeline(
            nc, cst, ctx, name, W, FT, 2, KT, src, lambda i, q: ((2 * i + q // 2 + (q % 2) * FT) * P, 0))
        silu_done, out_done, h_done, high_out = ([cst["sems"].new("%s%d_%s" % (n, s, name)) for s in range(2)]
                                                 for n in ("silu", "out_done", "h", "h_high"))
        block = ctx.enter_context(nc.Block())

        @block.sync
        def _(sp):
            with sp.Fori(0, FT // 2) as i:
                load(sp, i)

        @block.gpsimd
        def _(pool):
            for s in range(2):
                pool.sem_inc(split[s], 1)
            with pool.Fori(0, FT // 2) as i:
                take_low(pool, i)

        @block.tensor
        def _(pe):
            for s in range(2):
                pe.sem_inc(mm_done[s], 1)
            with pe.Fori(0, FT // 2) as i:
                for q in range(4):
                    if q % 2 == 0:
                        pe.wait_ge(h_done[q // 2], i + 1)
                    multiply(pe, i, q, 4 * (q // 2) + 2 * (q % 2), True, True)

        @block.scalar
        def _(act):
            def finish(i, m):
                act.wait_ge(mm_done[1], 2 * i + m + 2)
                act.wait_ge(h_done[m], i + 1)
                nc.scalar.activation(sg[:, m], ps[:, 4 * m:4 * m + 2, 0:HALF], ACT.Silu).then_inc(silu_done[m], 1)
                act.wait_ge(h_done[m], i + 2)
                d = dst[0][:, bass.ds(2 * i + m, 1), :].rearrange("p a (f n) -> p (a f) n", f=2)
                nc.scalar.copy(d, h[:, m]).then_inc(high_out[m], 1)

            def ahead(n):
                for s in range(2):
                    round_high(act, s, n)

            ahead(0)
            with act.Fori(0, FT // 2 - 1) as i:
                for m in range(2):
                    ahead(2 * i + m + 1)
                    finish(i, m)
            ahead(FT - 1)
            finish(FT // 2 - 1, 0)
            finish(FT // 2 - 1, 1)

        @block.vector
        def _(dve):
            for m in range(2):
                dve.sem_inc(h_done[m], 1)
                dve.sem_inc(out_done[m], 1)
            with dve.Fori(0, FT // 2) as i:
                for m in range(2):
                    dve.wait_ge(silu_done[m], i + 1)
                    dve.wait_ge(out_done[m], i + 1)
                    nc.vector.tensor_tensor(h[:, m], sg[:, m], ps[:, 4 * m + 2:4 * m + 4, 0:HALF], ALU.mult)\
                        .then_inc(h_done[m], 1)
                    dve.wait_ge(high_out[m], i + 1)
                    high, low = (x[:, bass.ds(2 * i + m, 1), :].rearrange("p a (f n) -> p (a f) n", f=2) for x in dst)
                    nc.vector.tensor_tensor(low, h[:, m], high.bitcast(F32), ALU.subtract).then_inc(out_done[m], 1)


def phase_layer_norm(nc, io, ps, name, layer, which, xT, X, cst):
    with ExitStack() as ctx:
        def sb(n, shape):
            return ctx.enter_context(nc.sbuf_tensor(n + "_" + name, shape, F32))

        def sem(n):
            return cst["sems"].new(n + "_" + name)

        at = (layer * 2 + which) * KT
        gain, shift = cst["vec"][:, at:at + KT], cst["vec"][:, VEC_B + at:VEC_B + at + KT]
        sq = sb("ln_sq", [P, 2, KT, HALF])
        sd = sb("ln_sd", [P, 2, HALF])
        mean_done, centred, squared, var_done, std, rstd, scaled = (
            sem(n) for n in ("mean", "centred", "squared", "var", "std", "rstd", "scaled"))
        block = ctx.enter_context(nc.Block())

        normed_a, normed_v, high_done = sem("normed_act"), sem("normed_dve"), sem("x_high")

        def half(hf):
            return xT[:, :, hf * HALF:(hf + 1) * HALF]

        def wide(a):
            return a.unsqueeze(1).to_broadcast([P, KT, HALF])

        @block.tensor
        def _(pe):
            for hf in range(2):
                for k in range(KT):
                    ins = nc.tensor.matmul(ps[:, hf, 0:HALF], cst["mean"][:], half(hf)[:, k], start=(k == 0),
                                           stop=(k == KT - 1))
                ins.then_inc(mean_done, 1)
            for hf in range(2):
                pe.wait_ge(squared, hf + 1)
                for k in range(KT):
                    ins = nc.tensor.matmul(ps[:, 2 + hf, 0:HALF], cst["mean"][:], sq[:, hf, k], start=(k == 0),
                                           stop=(k == KT - 1))
                ins.then_inc(var_done, 1)

        @block.scalar
        def _(act):
            for hf in range(2):
                act.wait_ge(centred, hf + 1)
                nc.scalar.activation(sq[:, hf], half(hf), ACT.Square).then_inc(squared, 1)
            for hf in range(2):
                act.wait_ge(var_done, hf + 1)
                nc.scalar.activation(sd[:, hf], ps[:, 2 + hf, 0:HALF], ACT.Sqrt, bias=cst["eps"][:]).then_inc(std, 1)
            for hf in range(2):
                act.wait_ge(scaled, hf + 1)
                for k in range(0, KT, 2):
                    nc.scalar.activation(half(hf)[:, k], half(hf)[:, k], ACT.Identity, bias=shift[:, k:k + 1],
                                         scale=gain[:, k:k + 1]).then_inc(normed_a, 1)
                act.wait_ge(normed_a, KT // 2 * (hf + 1))
                act.wait_ge(normed_v, KT // 2 * (hf + 1))
                cols = slice(hf * HALF, (hf + 1) * HALF)
                nc.scalar.copy(X[0][:, :, cols], half(hf)).then_inc(high_done, 1)

        @block.vector
        def _(dve):
            for hf in range(2):
                dve.wait_ge(mean_done, hf + 1)
                nc.vector.tensor_tensor(half(hf), half(hf), wide(ps[:, hf, 0:HALF]), ALU.subtract).then_inc(centred, 1)
            for hf in range(2):
                dve.wait_ge(std, hf + 1)
                nc.vector.reciprocal(sd[:, hf], sd[:, hf]).then_inc(rstd, 1)
                dve.wait_ge(rstd, hf + 1)
                dve.wait_ge(centred, hf + 1)
                nc.vector.tensor_tensor(half(hf), half(hf), wide(sd[:, hf]), ALU.mult).then_inc(scaled, 1)
                dve.wait_ge(scaled, hf + 1)
                for k in range(1, KT, 2):
                    nc.vector.tensor_scalar(half(hf)[:, k], half(hf)[:, k], gain[:, k:k + 1], shift[:, k:k + 1],
                                            ALU.mult, ALU.add).then_inc(normed_v, 1)
            for hf in range(2):
                dve.wait_ge(high_done, hf + 1)
                cols = slice(hf * HALF, (hf + 1) * HALF)
                nc.vector.tensor_tensor(X[1][:, :, cols], half(hf), X[0][:, :, cols].bitcast(F32), ALU.subtract)


def phase_store_y(nc, io, ps, xT, cst):
    NT = len(ROWS)
    with ExitStack() as ctx:
        def sem(name):
            return cst["sems"].new(name)

        yn = ctx.enter_context(nc.sbuf_tensor("yn", [P, NT, D_MODEL], F32))
        tr_done, tr_out, y_out = sem("ytr_done"), sem("ytr_out"), sem("y_out")
        block = ctx.enter_context(nc.Block())

        @block.tensor
        def _(pe):
            for n in range(2 * NT):
                t, hf = n // 2, n % 2
                if n >= 4:
                    pe.wait_ge(tr_out, n - 3)
                for k in range(4 * hf, 4 * hf + 4):
                    ins = nc.tensor.transpose(ps[0:ROWS[t], n % 4, (k % 4) * P:(k % 4 + 1) * P],
                                              xT[:, k, t * P:t * P + ROWS[t]], cst["ident"][:])
                ins.then_inc(tr_done, 1)

        @block.vector
        def _(dve):
            for n in range(2 * NT):
                t, hf = n // 2, n % 2
                dve.wait_ge(tr_done, n + 1)
                nc.vector.tensor_copy(yn[0:ROWS[t], t, hf * 512:(hf + 1) * 512], ps[0:ROWS[t], n % 4, :])\
                    .then_inc(tr_out, 1)

        @block.sync
        def _(sp):
            for t in range(NT):
                sp.wait_ge(tr_out, 2 * (t + 1))
                o = io["y_p"][0, t * P:(t + 1) * P, :] if t < TILES else io["y_s"][:, 0, :]
                sp.dma_start(o, yn[0:ROWS[t], t, :]).then_inc(y_out, 16)
            sp.wait_ge(y_out, 16 * NT)


def phase_gla_v_gate(nc, io, ps, xT, X, T, cst):
    NT = len(ROWS)
    V0, LOW0 = 1024, 3072
    with ExitStack() as ctx:
        def sb(name, shape):
            return ctx.enter_context(nc.sbuf_tensor(name, shape, F32))

        def sem(name):
            return cst["sems"].new(name)

        w = sb("w_v", [P, 2, KT, 512])
        wl, wg, low = sb("w_low", [P, KT, 16]), sb("w_gate2", [16, 512]), sb("lowT", [16, NTOK])
        w_in, wl_in, low_done, low_out, z_done, z_out, v_done, v_out = (
            sem(n) for n in ("wv_in", "wlow_in", "low_done", "low_out", "z_done", "z_out", "v_done", "v_out"))
        wv1_in = sem("wv1_in")
        W = io["gla_w_in"][0].rearrange("(k p) n -> p k n", p=P)
        block = ctx.enter_context(nc.Block())

        @block.sync
        def _(sp):
            sp.dma_start(wl[:], W[:, :, LOW0:LOW0 + 16]).then_inc(wl_in, 16)
            sp.dma_start(wg[:], io["gla_w_gate2"][0]).then_inc(wl_in, 16)
            for c, s in ((0, w_in), (1, wv1_in)):
                sp.dma_start(w[:, c], W[:, :, V0 + c * 512:V0 + (c + 1) * 512]).then_inc(s, 16)

        @block.tensor
        def _(pe):
            pe.wait_ge(wl_in, 32)
            for hf in range(2):
                for k in range(KT):
                    ins = nc.tensor.matmul(ps[0:16, hf, 0:HALF], wl[:, k, :], xT[:, k, hf * HALF:(hf + 1) * HALF],
                                           start=(k == 0), stop=(k == KT - 1))
            ins.then_inc(low_done, 1)
            for u in range(2 * NT):
                c, t = u // NT, u % NT
                if t == 0:
                    pe.wait_ge((w_in, wv1_in)[c], 16)
                if u >= 2:
                    pe.wait_ge(v_out, u - 1)
                for k in range(KT):
                    ins = nc.tensor.matmul(ps[0:ROWS[t], 2 + u % 2, :], xT[:, k, t * P:t * P + ROWS[t]], w[:, c, k, :],
                                           start=(k == 0), stop=(k == KT - 1))
                ins.then_inc(v_done, 1)
                if u == 1:
                    pe.wait_ge(low_out, 1)
                if 1 <= u <= 4:
                    m = u - 1
                    if m >= 2:
                        pe.wait_ge(z_out, m - 1)
                    for hf in range(2):
                        ins = nc.tensor.matmul(ps[:, 4 + 2 * (m % 2) + hf, 0:HALF], wg[:, m * P:(m + 1) * P],
                                               low[:, hf * HALF:(hf + 1) * HALF], start=True, stop=True)
                    ins.then_inc(z_done, 1)

        @block.vector
        def _(dve):
            dve.wait_ge(low_done, 1)
            nc.vector.tensor_copy(low[:].rearrange("p (f n) -> p f n", f=2), ps[0:16, 0:2, 0:HALF]).then_inc(low_out, 1)
            for m in range(4):
                dve.wait_ge(z_done, m + 1)
                z = T["z"][:, m, :].rearrange("p (f n) -> p f n", f=2)
                nc.vector.tensor_scalar(z, ps[:, 4 + 2 * (m % 2):6 + 2 * (m % 2), 0:HALF],
                                        cst["vec"][:, VEC_Z + m:VEC_Z + m + 1], None, ALU.add).then_inc(z_out, 1)

        @block.scalar
        def _(act):
            for u in range(2 * NT):
                c, t = u // NT, u % NT
                act.wait_ge(v_done, u + 1)
                nc.scalar.copy(T["v"][0:ROWS[t], t, c * 512:(c + 1) * 512], ps[0:ROWS[t], 2 + u % 2, :]).then_inc(v_out, 1)


def phase_gla_core(nc, io, ps, T, cst):
    NCH = SEQ // CH
    CPT = P // CH
    with ExitStack() as ctx:
        def sb(name, shape, dt=F32):
            return ctx.enter_context(nc.sbuf_tensor(name, shape, dt))

        def sem(name):
            return cst["sems"].new(name)

        a = sb("g_a", [P, GH, NTOK])
        lb = sb("g_lb", [P, GH, SEQ])
        ep = sb("g_ep", [P, GH, SEQ])
        ki = lb
        ks = a[:].rearrange("p h n -> p (h n)")[:, 0:GH * SEQ].rearrange("p (h n) -> p h n", h=GH)
        ksn = T["z"][:].rearrange("p h n -> p (h n)")[:, 0:GH * SEQ].rearrange("p (t h n) -> p t h n", t=TILES, h=GH)
        att = sb("g_att", [P, TILES, GH, P])
        mask = sb("g_mask", [P, P], I32)
        reset = sb("g_reset", [P, SEQ])
        st = sb("g_state", [P, 2 * CPT, GH, 256])
        tab, ach, vch = sem("g_tab"), sem("g_achain"), sem("g_vchain")
        soft, lb_ready, ep_done, en_done, d_ready, ed_done, qk_ready, ks_ready, att_zero = (
            sem(n) for n in ("g_soft", "g_lb", "g_ep", "g_en", "g_d", "g_ed", "g_qk", "g_ks", "g_attz"))
        tr_done, tr_out, att_done, att_out, kv_done, st_done, o_done, o_out, st_out = (
            sem(n) for n in ("g_tr", "g_tr_out", "g_att_done", "g_att_out", "g_kv", "g_st", "g_o", "g_o_out",
                             "g_st_out"))
        block = ctx.enter_context(nc.Block())
        q, k = T["qk"][:, 0:GH, 0:SEQ], T["qk"][:, GH:2 * GH, 0:SEQ]
        KV = [(t, hp) for t in range(TILES) for hp in range(2)]

        @block.sync
        def _(sp):
            sp.dma_start(mask[:], io["gla_mask_tab"]).then_inc(tab, 16)
            sp.dma_start(reset[:], io["gla_reset_tab"]).then_inc(tab, 16)
            sp.wait_ge(st_done, 2 * GH * NCH // 2)
            sp.dma_start(io["new_gla_p"][0, 0].rearrange("h k v -> k h v"), st[:, (NCH - 1) % (2 * CPT)]).then_inc(st_out, 16)
            sp.wait_ge(st_out, 16)

        @block.gpsimd
        def _(pool):
            nc.gpsimd.memset(att[:], 0.0).then_inc(att_zero, 1)

        @block.scalar
        def _(act):
            ch = Chain(act, ach)
            ch.step(nc.scalar.activation(a[:], T["z"][:], ACT.Abs))
            ch.step(nc.scalar.activation(a[:], a[:], ACT.Exp, scale=-1.0))
            nc.scalar.activation(a[:], a[:], ACT.Ln, bias=cst["one"][:]).then_inc(soft, 1)
            act.wait_ge(lb_ready, 1)
            nc.scalar.activation(ep[:], lb[:], ACT.Exp, scale=1.0 / GLA_TAU).then_inc(ep_done, 1)
            act.wait_ge(ep_done, 1)
            act.wait_ge(d_ready, 1)
            nc.scalar.activation(ki[:], lb[:], ACT.Exp, scale=-1.0 / GLA_TAU).then_inc(en_done, 1)
            ch.step(nc.scalar.activation(T["as"][:], T["z"][:, :, SEQ:NTOK], ACT.Exp, scale=1.0 / GLA_TAU))
            nc.scalar.activation(ks, ks, ACT.Exp, scale=1.0 / GLA_TAU).then_inc(ed_done, 1)
            for t in range(TILES):
                act.wait_ge(tr_done, t + 1)
                nc.scalar.copy(ksn[:, t], ps[:, 4 + t % 2, :].rearrange("p (h n) -> p h n", h=GH)).then_inc(tr_out, 1)
            for t in range(TILES):
                for hp in range(2):
                    act.wait_ge(o_done, 2 * t + hp + 1)
                    nc.scalar.copy(T["o"][:, 4 * hp:4 * hp + 4, t * P:(t + 1) * P],
                                   ps[:, 4 + 2 * (t % 2) + hp, :].rearrange("p (u n) -> p u n", u=4)).then_inc(o_out, 1)

        @block.vector
        def _(dve):
            ch = Chain(dve, vch)
            dve.wait_ge(tab, 32)
            dve.wait_ge(soft, 1)
            ch.step(nc.vector.scalar_tensor_tensor(out=T["z"][:], in0=T["z"][:], scalar=0.0, in1=a[:], op0=ALU.min,
                                                   op1=ALU.subtract))
            for h in range(GH):
                ins = nc.vector.tensor_tensor_scan(lb[:, h, :], reset[:], T["z"][:, h, 0:SEQ], 0.0, ALU.mult, ALU.add)
                if h < GH - 1:
                    ch.step(ins)
            ins.then_inc(lb_ready, 1)
            dve.wait_ge(lb_ready, 1)
            l4 = lb[:].rearrange("p h (c n) -> p h c n", n=CH)
            d4 = ks.rearrange("p h (c n) -> p h c n", n=CH)
            nc.vector.tensor_tensor(d4, l4[:, :, :, CH - 1:CH].to_broadcast([P, GH, NCH, CH]), l4,
                                    ALU.subtract).then_inc(d_ready, 1)
            dve.wait_ge(ep_done, 1)
            ch.step(nc.vector.scalar_tensor_tensor(out=q, in0=q, scalar=GSCALE, in1=ep[:], op0=ALU.mult, op1=ALU.mult))
            dve.wait_ge(en_done, 1)
            nc.vector.tensor_tensor(ki[:], ki[:], k, ALU.mult).then_inc(qk_ready, 1)
            dve.wait_ge(ed_done, 1)
            nc.vector.tensor_tensor(ks, ks, k, ALU.mult).then_inc(ks_ready, 1)
            dve.wait_ge(att_zero, 1)
            for t in range(TILES):
                dve.wait_ge(att_done, t + 1)
                nc.vector.copy_predicated(att[:, t], mask[:].unsqueeze(1).to_broadcast([P, GH, P]),
                                          ps[:, 6 + t % 2, :].rearrange("p (h n) -> p h n", h=GH)).then_inc(att_out, 1)
            done = 0
            for u, (t, hp) in enumerate(KV):
                dve.wait_ge(kv_done, CPT * (u + 1))
                for c in range(CPT):
                    j = t * CPT + c
                    if c == CPT - 1 and t >= 1:
                        dve.wait_ge(o_done, 2 * t)
                    for s in range(2):
                        h = 2 * hp + s
                        kv = ps[:, c, s * 256:(s + 1) * 256]
                        if j == 0:
                            ins = nc.vector.tensor_copy(st[:, 0, h], kv)
                        else:
                            ins = nc.vector.scalar_tensor_tensor(out=st[:, j % (2 * CPT), h],
                                                                 in0=st[:, (j - 1) % (2 * CPT), h],
                                                                 scalar=ep[:, h, (j + 1) * CH - 1:(j + 1) * CH],
                                                                 in1=kv, op0=ALU.mult, op1=ALU.add)
                        ins.then_inc(st_done, 1)
                        done += 1
                    dve.wait_ge(st_done, done)

        @block.tensor
        def _(pe):
            pe.wait_ge(ks_ready, 1)
            pe.wait_ge(qk_ready, 1)
            for t in range(TILES):
                sl = slice(t * P, (t + 1) * P)
                if t >= 2:
                    pe.wait_ge(tr_out, t - 1)
                for h in range(GH):
                    ins = nc.tensor.transpose(ps[:, 4 + t % 2, h * P:(h + 1) * P], ks[:, h, sl], cst["ident"][:])
                ins.then_inc(tr_done, 1)
                if t >= 2:
                    pe.wait_ge(att_out, t - 1)
                for h in range(GH):
                    ins = nc.tensor.matmul(ps[:, 6 + t % 2, h * P:(h + 1) * P], ki[:, h, sl], q[:, h, sl],
                                           start=True, stop=True)
                ins.then_inc(att_done, 1)
            pe.wait_ge(tr_out, TILES)
            pe.wait_ge(att_out, TILES)

            def update(u):
                t, hp = KV[u]
                if u >= 1:
                    pe.wait_ge(st_done, 8 * u)
                for c in range(CPT):
                    r = slice(c * CH, (c + 1) * CH)
                    for s in range(2):
                        h = 2 * hp + s
                        ins = nc.tensor.matmul(ps[:, c, s * 256:(s + 1) * 256], ksn[r, t, h, :],
                                               T["v"][r, t, h * 256:(h + 1) * 256], start=True, stop=True,
                                               tile_position=(c * CH, 0))
                    ins.then_inc(kv_done, 1)

            def output(t):
                pe.wait_ge(st_done, 8 * (2 * t + 2))
                if t >= 2:
                    pe.wait_ge(o_out, 2 * (t - 1))
                for hp in range(2):
                    bank = 4 + 2 * (t % 2) + hp
                    for u in range(4):
                        h, dv = 2 * hp + u // 2, (u % 2) * P
                        ins = nc.tensor.matmul(ps[:, bank, u * P:(u + 1) * P],
                                               T["v"][:, t, h * 256 + dv:h * 256 + dv + P], att[:, t, h, :],
                                               start=True, stop=False, skip_group_check=True)
                        for c in range(CPT):
                            j = t * CPT + c
                            if j:
                                ins = nc.tensor.matmul(ps[:, bank, u * P + c * CH:u * P + (c + 1) * CH],
                                                       st[:, (j - 1) % (2 * CPT), h, dv:dv + P],
                                                       q[:, h, j * CH:(j + 1) * CH], start=False, stop=True,
                                                       skip_group_check=True)
                    ins.then_inc(o_done, 1)

            for t in range(TILES):
                update(2 * t)
                if t:
                    output(t - 1)
                update(2 * t + 1)
            output(TILES - 1)


def phase_gla_sample(nc, io, ps, T, cst):
    with ExitStack() as ctx:
        def sb(name, shape, dt=F32):
            return ctx.enter_context(nc.sbuf_tensor(name, shape, dt))

        def sem(name):
            return cst["sems"].new(name)

        st = sb("s_state", [P, NB, GH, 256])
        hot = sb("s_onehot", [NB, NB, P])
        qs = sb("s_q", [P, GH, NB])
        st_in, hot_in = [sem("s_state_in%d" % b) for b in range(NB)], sem("s_onehot_in")
        q_ready, vb_done, decayed, st_done, o_done, o_out, st_out = (
            sem(n) for n in ("s_q_ready", "s_vb", "s_decayed", "s_state_done", "s_o", "s_o_out", "s_state_out"))
        block = ctx.enter_context(nc.Block())

        @block.sync
        def _(sp):
            sp.dma_start(hot[:], io["onehot_tab"]).then_inc(hot_in, 16)
            for b in range(NB):
                sp.dma_start(st[:, b], io["state_gla"][0, b].rearrange("h k v -> k h v")).then_inc(st_in[b], 16)
            for b in range(NB):
                sp.wait_ge(st_done, GH * (b + 1))
                sp.dma_start(io["new_gla_s"][0, b].rearrange("h k v -> k h v"), st[:, b]).then_inc(st_out, 16)
            sp.wait_ge(st_out, 16 * NB)

        @block.tensor
        def _(pe):
            pe.wait_ge(hot_in, 16)
            pe.wait_ge(q_ready, 1)

            def spread(b):
                if b >= 3:
                    pe.wait_ge(st_done, GH * (b - 2))
                for c in range(2):
                    ins = nc.tensor.matmul(ps[:, 2 + 2 * (b % 3) + c, :], hot[:, b, :],
                                           T["v"][0:NB, TILES, c * 512:(c + 1) * 512], start=True, stop=True)
                ins.then_inc(vb_done, 1)

            spread(0)
            for b in range(NB):
                if b + 1 < NB:
                    spread(b + 1)
                pe.wait_ge(st_done, GH * (b + 1))
                for h in range(GH):
                    for dv in range(2):
                        c = (2 * h + dv) * NB + b
                        ins = nc.tensor.matmul(ps[:, 0, c:c + 1], st[:, b, h, dv * P:(dv + 1) * P],
                                               qs[:, h, b:b + 1], start=True, stop=True)
            ins.then_inc(o_done, 1)

        @block.scalar
        def _(act):
            for b in range(NB):
                act.wait_ge(st_in[b], 16)
                for h in range(GH):
                    nc.scalar.activation(st[:, b, h], st[:, b, h], ACT.Copy, scale=T["as"][:, h, b:b + 1])\
                        .then_inc(decayed, 1)

        @block.vector
        def _(dve):
            nc.vector.tensor_scalar(qs[:], T["qk"][:, 0:GH, SEQ:NTOK], GSCALE, None, ALU.mult).then_inc(q_ready, 1)
            for b in range(NB):
                dve.wait_ge(vb_done, b + 1)
                for h in range(GH):
                    dve.wait_ge(decayed, GH * b + h + 1)
                    nc.vector.scalar_tensor_tensor(out=st[:, b, h], in0=ps[:, 2 + 2 * (b % 3) + h // 2,
                                                                           (h % 2) * 256:(h % 2) * 256 + 256],
                                                   scalar=T["qk"][:, GH + h, SEQ + b:SEQ + b + 1], in1=st[:, b, h],
                                                   op0=ALU.mult, op1=ALU.add).then_inc(st_done, 1)
            dve.wait_ge(o_done, 1)
            nc.vector.tensor_copy(T["o"][:, :, SEQ:NTOK], ps[:, 0, 0:8 * NB].rearrange("p (k b) -> p k b", k=8))


def phase_gla_gate_out(nc, ps, T, X, cst):
    with ExitStack() as ctx:
        def sb(name, shape, dt=F32):
            return ctx.enter_context(nc.sbuf_tensor(name, shape, dt))

        def sem(name):
            return cst["sems"].new(name)

        sq = sb("n_sq", [P, 8, NTOK])
        sd = sb("n_sd", [P, GH, NTOK])
        gated, high_done = sem("n_gated"), sem("n_high")
        squared, ms_done, std, rstd, scaled, silu = (sem(n) for n in ("n_sq_done", "n_ms", "n_std", "n_rstd",
                                                                      "n_scaled", "n_silu"))
        block = ctx.enter_context(nc.Block())

        @block.scalar
        def _(act):
            for h in range(GH):
                nc.scalar.activation(sq[:, 2 * h:2 * h + 2], T["o"][:, 2 * h:2 * h + 2], ACT.Square).then_inc(squared, 1)
            nc.scalar.activation(T["r"][:], T["r"][:], ACT.Silu).then_inc(silu, 1)
            for h in range(GH):
                act.wait_ge(ms_done, h + 1)
                nc.scalar.activation(sd[:, h].rearrange("p (f n) -> p f n", f=2), ps[:, 2 * h:2 * h + 2, 0:HALF],
                                     ACT.Sqrt, bias=cst["eps"][:], scale=4.0).then_inc(std, 1)
            for k in range(8):
                act.wait_ge(gated, k + 1)
                nc.scalar.copy(X[0][:, k], T["o"][:, k]).then_inc(high_done, 1)

        @block.tensor
        def _(pe):
            for h in range(GH):
                pe.wait_ge(squared, h + 1)
                for hf in range(2):
                    for c in range(2):
                        ins = nc.tensor.matmul(ps[:, 2 * h + hf, 0:HALF], cst["mean"][:],
                                               sq[:, 2 * h + c, hf * HALF:(hf + 1) * HALF],
                                               start=(c == 0), stop=(c == 1))
                ins.then_inc(ms_done, 1)

        @block.vector
        def _(dve):
            for h in range(GH):
                dve.wait_ge(std, h + 1)
                nc.vector.reciprocal(sd[:, h], sd[:, h]).then_inc(rstd, 1)
                dve.wait_ge(rstd, h + 1)
                nc.vector.tensor_tensor(T["o"][:, 2 * h:2 * h + 2], T["o"][:, 2 * h:2 * h + 2],
                                        sd[:, h].unsqueeze(1).to_broadcast([P, 2, NTOK]), ALU.mult).then_inc(scaled, 1)
            dve.wait_ge(silu, 1)
            dve.wait_ge(scaled, GH)
            for k in range(8):
                nc.vector.scalar_tensor_tensor(out=T["o"][:, k], in0=T["o"][:, k],
                                               scalar=cst["vec"][:, VEC_N + k:VEC_N + k + 1], in1=T["r"][:, k],
                                               op0=ALU.mult, op1=ALU.mult).then_inc(gated, 1)
            for k in range(8):
                dve.wait_ge(high_done, k + 1)
                nc.vector.tensor_tensor(X[1][:, k], T["o"][:, k], X[0][:, k].bitcast(F32), ALU.subtract)


def shape_tables():
    half = D // 2
    inv = (10000.0 ** (-np.arange(half) / half)).astype(np.float32)
    pos = np.zeros((P, len(ROWS)), np.float32)
    pos[:, :TILES] = np.arange(SEQ, dtype=np.float32).reshape(TILES, P).T
    pos[:, TILES] = PAST
    ang = (pos[:, :, None] * inv).astype(np.float32)
    rope = np.zeros((P, len(ROWS), 2, D), np.float32)
    rope[:, :, 0, :half] = rope[:, :, 0, half:] = np.cos(ang)
    rope[:, :, 1, :half] = -np.sin(ang)
    rope[:, :, 1, half:] = np.sin(ang)
    n = np.arange(SEQ // BLK)
    ok = ((n + 1) * BLK - 1)[None, None, :] <= (np.arange(TILES)[None, :, None] * P + np.arange(P)[:, None, None])
    q, k = np.arange(P)[:, None], np.arange(NB * PAGES * G)[None, :]
    own = (q // HEADS == k // (PAGES * G)) & ((q % HEADS) // R == k % G)
    bg = np.arange(NB * G)[None, :]
    gsum = (q // HEADS == bg // G) & ((q % HEADS) // R == bg % G)
    expand = gsum.T.reshape(NB * G, NB, HEADS)
    tri = np.broadcast_to(np.arange(NBLK)[None, :] < np.arange(NBLK)[:, None], (NB * G, NBLK, NBLK))
    f = np.float32
    return {"rope_tab": rope, "ident_tab": np.eye(P, dtype=f), "pm_01_tab": ok.astype(f),
            "pm_add_tab": np.where(ok, f(0), f(NEG)), "mask_s_tab": np.where(own, f(0), f(NEG)),
            "gsum_tab": gsum.astype(f), "expand_tab": np.ascontiguousarray(expand.astype(f)),
            "tri_tab": tri.astype(f),
            "gla_mask_tab": ((q // CH == q.T // CH) & (q <= q.T)).astype(np.int32),
            "gla_reset_tab": np.broadcast_to(f(1) * (np.arange(SEQ) % CH != 0), (P, SEQ)).astype(f),
            "onehot_tab": np.broadcast_to(np.eye(NB, dtype=f)[:, :, None], (NB, NB, P)).copy(),
            "causal_tab": np.where(np.arange(P)[None, :] <= np.arange(P)[:, None], f(0), f(NEG)),
            "gmask_tab": (np.arange(HEADS)[:, None] // R == np.arange(G)[None, :]).astype(f)}


def feed_forward(nc, io, ps, layer, xT, X, cst):
    with ExitStack() as ctx:
        H = [ctx.enter_context(nc.sbuf_tensor("h_%s%d" % (n, layer), [P, FT, NTOK], F32R)) for n in ("high", "low")]
        phase_gate_up(nc, ps, cst, "gu%d" % layer, io["ffn_w_gu"][layer], X, H)
        phase_linear(nc, ps, cst, "down%d" % layer, io["ffn_w_down"][layer], FT, KT, H, xT, True)
    phase_layer_norm(nc, io, ps, "ln%d1" % layer, layer, 1, xT, X, cst)


def build(nc, io):
    with ExitStack() as top:
        def sb(name, shape, dt=F32):
            return top.enter_context(nc.sbuf_tensor(name, shape, dt))

        ps = top.enter_context(nc.psum_tensor("ps", [P, 8, 512], F32))
        cst = {"ident": sb("ident", [P, P]), "in": top.enter_context(nc.semaphore("consts_in")), "n": 16}
        cst["ps"] = ps
        cst["sems"] = sems = Semaphores(nc)
        with nc.Block() as block:
            @block.sync
            def _(sp):
                sp.dma_start(cst["ident"][:], io["ident_tab"]).then_inc(cst["in"], 16)
        S = {"actA": sb("actA", [P, KT, NTOK])}
        S["qT"] = S["actA"][:, :, 0:SEQ]
        cst["mean"] = sb("mean_mat", [P, P])
        cst["eps"] = sb("eps", [P, 1])
        cst["one"] = sb("one", [P, 1])
        cst["vec"] = sb("vec", [P, VECS])
        with nc.Block() as block, nc.sbuf_tensor("vec_rows", [VECS, P], F32) as rows, \
                nc.semaphore("vec_in") as vec_in, nc.semaphore("vec_tr") as vec_tr:
            @block.sync
            def _(sp):
                for at, v in ((0, io["ln_g"].rearrange("l w (k p) -> (l w k) p", p=P)),
                              (VEC_B, io["ln_b"].rearrange("l w (k p) -> (l w k) p", p=P)),
                              (VEC_N, io["gla_norm_g"].rearrange("l (k p) -> (l k) p", p=P)),
                              (VEC_Z, io["gla_b_gate2"].rearrange("l (k p) -> (l k) p", p=P))):
                    sp.dma_start(rows[at:at + v.shape[0], :], v).then_inc(vec_in, 16)

            @block.tensor
            def _(pe):
                pe.wait_ge(cst["in"], cst["n"])
                pe.wait_ge(vec_in, 16 * 4)
                nc.tensor.transpose(ps[:, 0, 0:VECS], rows[:], cst["ident"][0:VECS, 0:VECS]).then_inc(vec_tr, 1)

            @block.vector
            def _(dve):
                dve.wait_ge(vec_tr, 1)
                nc.vector.tensor_copy(cst["vec"][:], ps[:, 0, 0:VECS])
                nc.vector.memset(cst["mean"][:], 1.0 / D_MODEL)
                nc.vector.memset(cst["eps"][:], EPS)
                nc.vector.memset(cst["one"][:], 1.0)
        with ExitStack() as nsa:
            def keep(name, shape):
                S[name] = nsa.enter_context(nc.sbuf_tensor(name, shape, F32))

            keep("qrT", [P, KT, SEQ])
            keep("kT", [P, 2, G, SEQ])
            keep("cmpn", [P, len(ROWS), 512])
            keep("slcn", [P, len(ROWS), 512])
            keep("winn", [P, len(ROWS), 512])
            keep("gates", [P, len(ROWS), 48])
            keep("qs", [P, NB, HEADS])
            keep("qz", [P, 2, NB, HEADS])
            keep("knew", [P, 2, 2, NB])
            phase_project(nc, io, ps, S, cst)
            keep("ckT", [P, 2, NB * PAGES * G + TILES * G])
            phase_compress(nc, io, ps, S, cst)
            keep("oacc", [P, TILES, D_MODEL])
            keep("osn", [NB, 3, D_MODEL])
            keep("selneg", [HEADS, NB, NBLK])
            phase_cmp_attention(nc, io, ps, S, cst)
            sems.recycle()
            phase_sample_attention(nc, io, ps, S, cst)
            phase_prompt_attention(nc, io, ps, S, cst)
            phase_attention_out(nc, io, ps, S, cst)
        sems.recycle()
        xT = sb("xT", [P, KT, NTOK])
        X = [top.enter_context(nc.sbuf_tensor("x_" + n, [P, KT, NTOK], F32R)) for n in ("high", "low")]
        phase_residual_in(nc, io, ps, xT, S["actA"], X, cst)
        phase_linear(nc, ps, cst, "nsa_out", io["nsa_w_out"][0], KT, KT, X, xT, True)
        phase_layer_norm(nc, io, ps, "ln00", 0, 0, xT, X, cst)
        feed_forward(nc, io, ps, 0, xT, X, cst)
        with ExitStack() as gla:
            T = {"o": S["actA"]}

            def hold(name, shape):
                T[name] = gla.enter_context(nc.sbuf_tensor("gla_" + name, shape, F32))

            hold("qk", [P, 2 * GH, NTOK])
            hold("r", [P, KT, NTOK])
            hold("v", [P, len(ROWS), D_MODEL])
            hold("z", [P, GH, NTOK])
            hold("as", [P, GH, NB])
            sems.recycle()
            Wg = io["gla_w_in"][0]
            phase_linear(nc, ps, cst, "gla_qk", Wg[:, 0:1024], KT, KT, X, T["qk"], False)
            phase_linear(nc, ps, cst, "gla_r", Wg[:, 2048:3072], KT, KT, X, T["r"], False)
            phase_gla_v_gate(nc, io, ps, xT, X, T, cst)
            phase_gla_core(nc, io, ps, T, cst)
            phase_gla_sample(nc, io, ps, T, cst)
            phase_gla_gate_out(nc, ps, T, X, cst)
            phase_linear(nc, ps, cst, "gla_out", io["gla_w_out"][0], KT, KT, X, xT, True)
        sems.recycle()
        phase_layer_norm(nc, io, ps, "ln10", 1, 0, xT, X, cst)
        feed_forward(nc, io, ps, 1, xT, X, cst)
        phase_store_y(nc, io, ps, xT, cst)


_OUTS = [("y_p", (1, SEQ, D_MODEL)), ("y_s", (NB, 1, D_MODEL)),
         ("new_cmp_p", (1, 1, SEQ, 2, G, D)), ("new_slc_p", (1, 1, SEQ, 2, G, D)), ("new_win_p", (1, 1, WIN, 2, G, D)),
         ("new_gla_p", (1, 1, GH, 128, 256)),
         ("new_cmp_s", (1, NB, 1, 2, G, D)), ("new_slc_s", (1, NB, 1, 2, G, D)), ("new_win_s", (1, NB, WIN, 2, G, D)),
         ("new_gla_s", (1, NB, GH, 128, 256))]
_RENAME = {"cache_cmp_kv": "cache_cmp", "cache_slc_kv": "cache_slc", "cache_win_kv": "cache_win"}


def kernel(**inputs):
    import concourse.bacc as _bacc
    from concourse.bass_utils import run_bass_kernel_spmd as _run

    nc = _bacc.Bacc("TRN2", target_bir_lowering=False, num_devices=1)
    arrays, io = {}, {}
    data = {_RENAME.get(k, k): np.ascontiguousarray(v) for k, v in inputs.items()}
    data.update(shape_tables())
    for name, a in data.items():
        arrays["in_" + name] = a
        io[name] = nc.dram_tensor("in_" + name, a.shape, mybir.dt.from_np(a.dtype), kind="ExternalInput").ap()
    for name, shape in _OUTS:
        io[name] = nc.dram_tensor("out_" + name, shape, F32, kind="ExternalOutput").ap()
    build(nc, io)
    r = _run(nc, [arrays], core_ids=[0])
    return tuple(r.results[0]["out_" + name] for name, _ in _OUTS)
```
